# Optimizing a Trainium2 kernel written in Bass

```python
import math
import jax
import jax.numpy as jnp
from jax import lax
import numpy as np

D_MODEL = 1024
BATCH = 1
SEQ = 256
DEPTH = 2

GRID_W = 64
CTX_LEN = 256
N_MIXERS = 2
NORM_EPS = 1e-6
N_MOD = 6

SSD_D_INNER = 2 * D_MODEL
SSD_HEAD_DIM = 64
SSD_N_HEADS = SSD_D_INNER // SSD_HEAD_DIM
SSD_N_GROUPS = 4
SSD_D_STATE = 128
SSD_CONV = 5
SSD_CHUNK = 128
SSD_CONV_DIM = SSD_D_INNER + 2 * SSD_N_GROUPS * SSD_D_STATE
SSD_IN_DIM = SSD_D_INNER + SSD_CONV_DIM + 2 * SSD_N_HEADS

ATT_HEAD_DIM = 64
ATT_Q_HEADS = D_MODEL // ATT_HEAD_DIM
ATT_KV_HEADS = 4
ATT_GROUP = ATT_Q_HEADS // ATT_KV_HEADS
ATT_Q_BLOCK = 128
ATT_SCALE = ATT_HEAD_DIM ** -0.5
ROPE_THETA = 10000.0
ATT_QKV_DIM = (ATT_Q_HEADS + 2 * ATT_KV_HEADS) * ATT_HEAD_DIM

MOE_GROUPS = 4
MOE_EXPERTS_PER_GROUP = 8
MOE_EXPERTS = MOE_GROUPS * MOE_EXPERTS_PER_GROUP
MOE_TOP_K = 2
MOE_D_FF = D_MODEL // 2
MOE_ROW_BLOCK = 256

N_SSD_LAYERS = (DEPTH + 1) // 2
N_ATT_LAYERS = DEPTH // 2

kernel_name = "hybrid_ssd_gqa_hmoe_dit"

def rms_norm(x, g):
    xf = x.astype(jnp.float32)
    y = xf * lax.rsqrt(jnp.mean(xf * xf, axis=-1, keepdims=True) + NORM_EPS)
    return (y * g.astype(jnp.float32)).astype(x.dtype)

def modulate(x, g, shift, scale):
    return rms_norm(x, g) * (1 + scale) + shift

def axial_rope_tables(n_tokens):
    rows = n_tokens // GRID_W
    row = jnp.repeat(jnp.arange(rows), GRID_W).astype(jnp.float32)
    col = (jnp.arange(n_tokens) % GRID_W).astype(jnp.float32)
    half = ATT_HEAD_DIM // 2
    freqs = ROPE_THETA ** (-jnp.arange(0, half, 2, dtype=jnp.float32) / half)
    ang = jnp.concatenate([row[:, None] * freqs, col[:, None] * freqs], axis=-1)
    return jnp.cos(ang), jnp.sin(ang)

def apply_rope(x, cos, sin):
    xf = x.astype(jnp.float32).reshape(*x.shape[:-1], ATT_HEAD_DIM // 2, 2)
    x0, x1 = xf[..., 0], xf[..., 1]
    c = cos[None, :, None, :]
    s = sin[None, :, None, :]
    out = jnp.stack([x0 * c - x1 * s, x0 * s + x1 * c], axis=-1)
    return out.reshape(x.shape).astype(x.dtype)

def gqa_attend(q, k, v):
    b, lq = q.shape[:2]
    qg = q.reshape(b, lq, ATT_KV_HEADS, ATT_GROUP, ATT_HEAD_DIM)
    s = jnp.einsum("bqkgd,bskd->bkgqs", qg, k, preferred_element_type=jnp.float32) * ATT_SCALE
    p = jax.nn.softmax(s, axis=-1).astype(v.dtype)
    o = jnp.einsum("bkgqs,bskd->bqkgd", p, v)
    return o.reshape(b, lq, ATT_Q_HEADS, ATT_HEAD_DIM)

def gqa_mixer(h_lat, h_ctx, w_qkv, q_gain, k_gain, w_o, ctx_out):
    b, n_lat = h_lat.shape[:2]

    def project(h):
        qkv = h @ w_qkv
        q, k, v = jnp.split(qkv, [ATT_Q_HEADS * ATT_HEAD_DIM, (ATT_Q_HEADS + ATT_KV_HEADS) * ATT_HEAD_DIM], axis=-1)
        lead = h.shape[:2]
        q = rms_norm(q.reshape(*lead, ATT_Q_HEADS, ATT_HEAD_DIM), q_gain)
        k = rms_norm(k.reshape(*lead, ATT_KV_HEADS, ATT_HEAD_DIM), k_gain)
        v = v.reshape(*lead, ATT_KV_HEADS, ATT_HEAD_DIM)
        return q, k, v

    q_l, k_l, v_l = project(h_lat)
    q_c, k_c, v_c = project(h_ctx)
    cos, sin = axial_rope_tables(n_lat)
    q_l = apply_rope(q_l, cos, sin)
    k_l = apply_rope(k_l, cos, sin)
    k_all = jnp.concatenate([k_l, k_c], axis=1)
    v_all = jnp.concatenate([v_l, v_c], axis=1)
    n_blk = n_lat // ATT_Q_BLOCK
    q_blocks = jnp.moveaxis(q_l.reshape(b, n_blk, ATT_Q_BLOCK, ATT_Q_HEADS, ATT_HEAD_DIM), 1, 0)
    o_blocks = lax.map(lambda qb: gqa_attend(qb, k_all, v_all), q_blocks)
    o_l = jnp.moveaxis(o_blocks, 0, 1).reshape(b, n_lat, ATT_Q_HEADS * ATT_HEAD_DIM)
    out_l = o_l @ w_o
    out_c = None
    if ctx_out:
        o_c = gqa_attend(q_c, k_c, v_c)
        out_c = o_c.reshape(*h_ctx.shape[:2], ATT_Q_HEADS * ATT_HEAD_DIM) @ w_o
    return out_l, out_c

def depthwise_conv_centered(u, w, bias):
    ch = u.shape[-1]
    out = lax.conv_general_dilated(
        u, w[:, None, :].astype(u.dtype), window_strides=(1,),
        padding=[(SSD_CONV // 2, SSD_CONV // 2)],
        dimension_numbers=("NWC", "WIO", "NWC"), feature_group_count=ch)
    return out + bias

def ssd_chunked(x, dt, a, bm, cm, h0):
    f32 = jnp.float32
    bsz, n, nh, p = x.shape
    g, ns = bm.shape[-2:]
    r = nh // g
    q = SSD_CHUNK
    nc = n // q
    x = x.astype(f32).reshape(bsz, nc, q, g, r, p)
    dt = dt.astype(f32).reshape(bsz, nc, q, g, r)
    bm = bm.astype(f32).reshape(bsz, nc, q, g, ns)
    cm = cm.astype(f32).reshape(bsz, nc, q, g, ns)
    a_cum = jnp.cumsum(dt * a.astype(f32).reshape(g, r), axis=2)
    seg = a_cum[:, :, :, None] - a_cum[:, :, None, :]
    mask = jnp.tril(jnp.ones((q, q), dtype=bool))[:, :, None, None]
    decay = jnp.exp(jnp.where(mask, seg, -jnp.inf))
    cb = jnp.einsum("bcign,bcjgn->bcijg", cm, bm)
    mix = cb[..., None] * decay * dt[:, :, None]
    y_diag = jnp.einsum("bcijgr,bcjgrp->bcigrp", mix, x)
    w_end = jnp.exp(a_cum[:, :, -1:] - a_cum) * dt
    states = jnp.einsum("bcjgn,bcjgrp->bcgrpn", bm, x * w_end[..., None])
    chunk_decay = jnp.exp(a_cum[:, :, -1])

    def step(h, inp):
        s_c, d_c = inp
        return h * d_c[..., None, None] + s_c, h

    h_last, h_starts = lax.scan(step, h0.astype(f32).reshape(bsz, g, r, p, ns),
                                (jnp.moveaxis(states, 1, 0), jnp.moveaxis(chunk_decay, 1, 0)))
    h_starts = jnp.moveaxis(h_starts, 0, 1)
    y_off = jnp.einsum("bcign,bcgrpn->bcigrp", cm, h_starts) * jnp.exp(a_cum)[..., None]
    y = (y_diag + y_off).reshape(bsz, n, nh, p)
    return y, h_last.reshape(bsz, nh, p, ns)

def ssd_mixer(h_lat, h_ctx, w_in, conv_w, conv_b, dt_bias, a_log, d_skip, norm_g, w_out, ctx_out):
    gn = SSD_N_GROUPS * SSD_D_STATE

    def project(h):
        bb, ll = h.shape[:2]
        zxbcdt = h @ w_in
        z, xbc, dt = jnp.split(zxbcdt, [SSD_D_INNER, SSD_D_INNER + SSD_CONV_DIM], axis=-1)
        xbc = jax.nn.silu(depthwise_conv_centered(xbc, conv_w, conv_b))
        xs, bm, cm = jnp.split(xbc, [SSD_D_INNER, SSD_D_INNER + gn], axis=-1)
        xs = xs.reshape(bb, ll, SSD_N_HEADS, SSD_HEAD_DIM)
        bm = bm.reshape(bb, ll, SSD_N_GROUPS, SSD_D_STATE)
        cm = cm.reshape(bb, ll, SSD_N_GROUPS, SSD_D_STATE)
        dt = jax.nn.softplus(dt.astype(jnp.float32).reshape(bb, ll, 2, SSD_N_HEADS)
                             + dt_bias.astype(jnp.float32))
        return z, xs, bm, cm, dt

    z_l, x_l, b_l, c_l, dt_l = project(h_lat)
    z_c, x_c, b_c, c_c, dt_c = project(h_ctx)
    a = -jnp.exp(a_log.astype(jnp.float32))
    h0 = jnp.zeros((h_lat.shape[0], SSD_N_HEADS, SSD_HEAD_DIM, SSD_D_STATE), jnp.float32)
    flip = lambda t: jnp.flip(t, axis=1)
    yc_f, hc_f = ssd_chunked(x_c, dt_c[:, :, 0], a[0], b_c, c_c, h0)
    yl_f, _ = ssd_chunked(x_l, dt_l[:, :, 0], a[0], b_l, c_l, hc_f)
    yc_b, hc_b = ssd_chunked(flip(x_c), flip(dt_c[:, :, 1]), a[1], flip(b_c), flip(c_c), h0)
    yl_b, _ = ssd_chunked(flip(x_l), flip(dt_l[:, :, 1]), a[1], flip(b_l), flip(c_l), hc_b)

    def finish(yf, yb, xs, z):
        bb, ll = xs.shape[:2]
        y = (yf + flip(yb)).astype(xs.dtype) + xs * d_skip[:, None]
        y = y.reshape(bb, ll, SSD_D_INNER) * jax.nn.silu(z)
        y = rms_norm(y.reshape(bb, ll, SSD_N_GROUPS, SSD_D_INNER // SSD_N_GROUPS),
                     norm_g.reshape(SSD_N_GROUPS, SSD_D_INNER // SSD_N_GROUPS))
        return y.reshape(bb, ll, SSD_D_INNER) @ w_out

    out_l = finish(yl_f, yl_b, x_l, z_l)
    out_c = finish(yc_f, yc_b, x_c, z_c) if ctx_out else None
    return out_l, out_c

def hier_moe(h, w_group, b_group, w_router, b_router, w_gate, w_up, w_down):
    t, d = h.shape
    hf = h.astype(jnp.float32)
    g_logits = hf @ w_group.astype(jnp.float32) + b_group.astype(jnp.float32)
    g_prob = jax.nn.softmax(g_logits, axis=-1)
    g_sel = jnp.argmax(g_logits, axis=-1)
    g_w = jnp.take_along_axis(g_prob, g_sel[:, None], axis=-1)[:, 0]
    e_logits = (hf @ w_router.astype(jnp.float32) + b_router.astype(jnp.float32)).reshape(
        t, MOE_GROUPS, MOE_EXPERTS_PER_GROUP)
    e_logits = jnp.take_along_axis(e_logits, g_sel[:, None, None], axis=1)[:, 0]
    top_v, top_i = lax.top_k(e_logits, MOE_TOP_K)
    e_w = jax.nn.softmax(top_v, axis=-1) * g_w[:, None]
    expert_id = g_sel[:, None] * MOE_EXPERTS_PER_GROUP + top_i

    n_assign = t * MOE_TOP_K
    flat_e = expert_id.reshape(-1)
    flat_tok = jnp.repeat(jnp.arange(t, dtype=jnp.int32), MOE_TOP_K)
    flat_w = e_w.reshape(-1)
    order = jnp.argsort(flat_e)
    sorted_e = flat_e[order]
    counts = jnp.bincount(flat_e, length=MOE_EXPERTS)
    starts = jnp.cumsum(counts) - counts
    padded = (counts + MOE_ROW_BLOCK - 1) // MOE_ROW_BLOCK * MOE_ROW_BLOCK
    pad_ends = jnp.cumsum(padded)
    pad_starts = pad_ends - padded
    dest = pad_starts[sorted_e] + (jnp.arange(n_assign) - starts[sorted_e])
    n_blocks = -(-n_assign // MOE_ROW_BLOCK) + MOE_EXPERTS
    cap = n_blocks * MOE_ROW_BLOCK
    buf_tok = jnp.zeros((cap,), jnp.int32).at[dest].set(flat_tok[order])
    buf_w = jnp.zeros((cap,), jnp.float32).at[dest].set(flat_w[order])
    block_e = jnp.minimum(
        jnp.searchsorted(pad_ends, jnp.arange(n_blocks) * MOE_ROW_BLOCK, side="right"), MOE_EXPERTS - 1)
    xb = h[buf_tok].reshape(n_blocks, MOE_ROW_BLOCK, d)

    def run_block(args):
        xblk, e = args
        return (jax.nn.silu(xblk @ w_gate[e]) * (xblk @ w_up[e])) @ w_down[e]

    yb = lax.map(run_block, (xb, block_e)).reshape(cap, d)
    return jax.ops.segment_sum(yb * buf_w[:, None].astype(yb.dtype), buf_tok, num_segments=t)

def setup_inputs(seed: int = 0) -> dict:
    key = jax.random.key(seed)
    ks = jax.random.split(key, 32)
    f32 = jnp.float32
    nrm = lambda k, shape, s: jax.random.normal(k, shape, f32) * s
    D = D_MODEL
    H = SSD_N_HEADS
    dt0 = jnp.exp(jax.random.uniform(ks[10], (N_SSD_LAYERS, 2, H), f32,
                                     minval=math.log(1e-3), maxval=math.log(1e-1)))
    dt_bias = dt0 + jnp.log(-jnp.expm1(-dt0))
    a_log = jnp.log(jax.random.uniform(ks[11], (N_SSD_LAYERS, 2, H), f32, minval=1.0, maxval=16.0))
    return {
        "x": nrm(ks[0], (BATCH, SEQ, D), 1.0),
        "c": nrm(ks[1], (BATCH, D), 1.0),
        "ctx": nrm(ks[2], (BATCH, CTX_LEN, D), 1.0),
        "c_ctx": nrm(ks[3], (D,), 1.0),
        "mod_w": nrm(ks[4], (DEPTH, D, N_MOD * D), 0.5 * D ** -0.5),
        "mod_b": nrm(ks[5], (DEPTH, N_MOD * D), 0.01),
        "norm1_g": 1.0 + nrm(ks[6], (DEPTH, D), 0.02),
        "norm2_g": 1.0 + nrm(ks[7], (DEPTH, D), 0.02),
        "ssd_w_in": nrm(ks[8], (N_SSD_LAYERS, D, SSD_IN_DIM), D ** -0.5),
        "ssd_conv_w": nrm(ks[9], (N_SSD_LAYERS, SSD_CONV, SSD_CONV_DIM), SSD_CONV ** -0.5),
        "ssd_conv_b": nrm(ks[12], (N_SSD_LAYERS, SSD_CONV_DIM), 0.01),
        "ssd_dt_bias": dt_bias,
        "ssd_a_log": a_log,
        "ssd_d": 1.0 + nrm(ks[13], (N_SSD_LAYERS, H), 0.02),
        "ssd_norm_g": 1.0 + nrm(ks[14], (N_SSD_LAYERS, SSD_D_INNER), 0.02),
        "ssd_w_out": nrm(ks[15], (N_SSD_LAYERS, SSD_D_INNER, D), SSD_D_INNER ** -0.5),
        "att_w_qkv": nrm(ks[16], (N_ATT_LAYERS, D, ATT_QKV_DIM), D ** -0.5),
        "att_q_gain": 1.0 + nrm(ks[17], (N_ATT_LAYERS, ATT_HEAD_DIM), 0.02),
        "att_k_gain": 1.0 + nrm(ks[18], (N_ATT_LAYERS, ATT_HEAD_DIM), 0.02),
        "att_w_o": nrm(ks[19], (N_ATT_LAYERS, D, D), D ** -0.5),
        "moe_w_group": nrm(ks[20], (DEPTH, D, MOE_GROUPS), D ** -0.5),
        "moe_b_group": nrm(ks[21], (DEPTH, MOE_GROUPS), 0.01),
        "moe_w_router": nrm(ks[22], (DEPTH, D, MOE_EXPERTS), D ** -0.5),
        "moe_b_router": nrm(ks[23], (DEPTH, MOE_EXPERTS), 0.01),
        "moe_w_gate": nrm(ks[24], (DEPTH, MOE_EXPERTS, D, MOE_D_FF), D ** -0.5),
        "moe_w_up": nrm(ks[25], (DEPTH, MOE_EXPERTS, D, MOE_D_FF), D ** -0.5),
        "moe_w_down": nrm(ks[26], (DEPTH, MOE_EXPERTS, MOE_D_FF, D), MOE_D_FF ** -0.5),
    }

def reference(x, c, ctx, c_ctx, mod_w, mod_b, norm1_g, norm2_g,
              ssd_w_in, ssd_conv_w, ssd_conv_b, ssd_dt_bias, ssd_a_log, ssd_d, ssd_norm_g, ssd_w_out,
              att_w_qkv, att_q_gain, att_k_gain, att_w_o,
              moe_w_group, moe_b_group, moe_w_router, moe_b_router, moe_w_gate, moe_w_up, moe_w_down):
    b, n_lat, d = x.shape
    n_ctx = ctx.shape[1]
    silu_c = jax.nn.silu(c)
    silu_cc = jax.nn.silu(c_ctx)[None]
    x_lat, x_ctx = x, ctx
    for layer in range(DEPTH):
        last = layer == DEPTH - 1
        mod_l = jnp.split((silu_c @ mod_w[layer] + mod_b[layer])[:, None, :], N_MOD, axis=-1)
        mod_c = jnp.split((silu_cc @ mod_w[layer] + mod_b[layer])[:, None, :], N_MOD, axis=-1)
        sh1, sc1, g1, sh2, sc2, g2 = mod_l
        csh1, csc1, cg1, csh2, csc2, cg2 = mod_c
        a_l = modulate(x_lat, norm1_g[layer], sh1, sc1)
        a_c = modulate(x_ctx, norm1_g[layer], csh1, csc1)
        j = layer // N_MIXERS
        if layer % N_MIXERS == 0:
            m_l, m_c = ssd_mixer(a_l, a_c, ssd_w_in[j], ssd_conv_w[j], ssd_conv_b[j], ssd_dt_bias[j],
                                 ssd_a_log[j], ssd_d[j], ssd_norm_g[j], ssd_w_out[j], not last)
        else:
            m_l, m_c = gqa_mixer(a_l, a_c, att_w_qkv[j], att_q_gain[j], att_k_gain[j], att_w_o[j], not last)
        x_lat = x_lat + g1 * m_l
        f_l = modulate(x_lat, norm2_g[layer], sh2, sc2).reshape(b * n_lat, d)
        moe_args = (moe_w_group[layer], moe_b_group[layer], moe_w_router[layer], moe_b_router[layer],
                    moe_w_gate[layer], moe_w_up[layer], moe_w_down[layer])
        if last:
            y = hier_moe(f_l, *moe_args)
            x_lat = x_lat + g2 * y.reshape(b, n_lat, d)
        else:
            x_ctx = x_ctx + cg1 * m_c
            f_c = modulate(x_ctx, norm2_g[layer], csh2, csc2).reshape(b * n_ctx, d)
            y = hier_moe(jnp.concatenate([f_l, f_c], axis=0), *moe_args)
            x_lat = x_lat + g2 * y[: b * n_lat].reshape(b, n_lat, d)
            x_ctx = x_ctx + cg2 * y[b * n_lat:].reshape(b, n_ctx, d)
    return x_lat


_drawn_inputs = setup_inputs


def setup_inputs(seed=0):
    import zlib

    import numpy as np

    out = dict(_drawn_inputs(seed))
    spreads = {}
    factors = {'mod_b': 2.966,
     'norm1_g': 4.753,
     'norm2_g': 3.369,
     'ssd_conv_b': 6.542,
     'ssd_d': 64.0,
     'ssd_norm_g': 7.109,
     'att_q_gain': 8.0,
     'att_k_gain': 8.0,
     'moe_b_group': 8.0,
     'moe_b_router': 8.0}
    for name, (base, spread) in spreads.items():
        noise = np.random.default_rng([zlib.crc32(name.encode()), seed]).standard_normal(out[name].shape)
        drawn = base * np.exp(spread * noise) if base else spread * noise
        out[name] = jnp.asarray(drawn.astype(out[name].dtype))
    for name, factor in factors.items():
        out[name] = (out[name] * factor).astype(out[name].dtype)
    return out
```

```python
from contextlib import ExitStack

import numpy as np
import concourse.bass as bass
from concourse import mybir

ALU = mybir.AluOpType
ACT = mybir.ActivationFunctionType
AX = mybir.AxisListType.X
F32 = mybir.dt.float32
I32 = mybir.dt.int32
U32 = mybir.dt.uint32

P = 128
D = 1024
KD = D // P
SEQ = 256
NT = 2 * SEQ // P
NTL = SEQ // P
EPS = 1e-6
NMOD = 6
SLOT = 4096
COLS = 512
MODU = NMOD * D // COLS

DI = 2048
HEADS, HD, GROUPS, NS = 32, 64, 4, 128
HG = HEADS // GROUPS
TAPS = 5
XBC = DI + 2 * GROUPS * NS
NCH = XBC // P
GW = DI // GROUPS

QH, KVH = 16, 4
E, EG, EPG, F = 32, 4, 8, 512

C_ID, C_LE, C_GT, C_GE, C_LT, C_ONE, C_IOTA = (i * P for i in range(7))
C_TOK = 7 * P
C_SEL = C_TOK + NT
C_E = C_SEL + 2
C_B0 = C_E + E
C_ZERO = C_B0 + E
C_N = C_ZERO + P


def overflow_blocks(tokens):
    return 2 * tokens // (P + 1)


def consts_array():
    k, i = np.meshgrid(np.arange(P), np.arange(P), indexing="ij")
    parts = [k == i, k <= i, k > i, k >= i, k < i, np.ones((P, P)), i]
    tok = np.arange(P)[:, None] + P * np.arange(NT)[None]
    sel = np.stack([np.arange(P) % 32 == r for r in range(2)], 1)
    e = np.broadcast_to(np.arange(E)[None], (P, E))
    return np.concatenate([*parts, tok, sel, e, e * P, np.zeros((P, P))], 1).astype(np.float32)


def rope_array():
    half = HD // 2
    n = np.arange(SEQ)
    freqs = np.float32(10000.0) ** (-np.arange(0, half, 2, dtype=np.float32) / np.float32(half))
    row, col = (n // 64).astype(np.float32), (n % 64).astype(np.float32)
    ang = np.concatenate([row[:, None] * freqs, col[:, None] * freqs], 1).astype(np.float32)
    t = np.stack([np.cos(ang), np.sin(ang)]).astype(np.float32)
    return np.ascontiguousarray(t.reshape(2, NTL, P, half).transpose(2, 0, 1, 3))


def hybrid_block(nc, a, out):
    ctx = ExitStack()
    with ctx:
        def sem(name):
            return ctx.enter_context(nc.semaphore(name))

        def sb(name, shape, dt=F32):
            return ctx.enter_context(nc.sbuf_tensor(name, shape, dt))

        def dram(name, shape):
            return nc.dram_tensor(name, shape, F32, kind="Internal").ap()

        RING3 = 3 * SLOT
        mem = sb("mem", [P, RING3 + 38912])

        def region(at, size, pattern=None, parts=P, **dims):
            v = mem[0:parts, at:at + size]
            return v.rearrange(pattern, **dims) if pattern else v

        A0 = RING3
        A_XROW, A_AT, A_BCT, A_Y, A_H, A_WORK = A0, A0 + 8192, A0 + 12288, A0 + 18432, A0 + 26624, A0 + 30720

        ring_at = [0, SLOT, 2 * SLOT, A0, A0 + SLOT, A0 + 2 * SLOT]
        consts = sb("consts", [P, C_N])
        smalls = sb("smalls", [P, 512])
        sm_at = [0]

        def small(size, pattern=None, **dims):
            v = smalls[:, sm_at[0]:sm_at[0] + size]
            sm_at[0] += size
            assert sm_at[0] <= 512
            return v.rearrange(pattern, **dims) if pattern else v

        ident = consts[:, C_ID:C_ID + P]
        psum = [ctx.enter_context(nc.psum_tensor(f"bank{i}", [P, COLS], F32)) for i in range(8)]

        mod_dram = dram("mod_dram", [2, 2, NMOD * D])
        f_dram = dram("f_dram", [NT * P, D])

        U_MOD = [0, MODU + 6]
        U_XBC = MODU
        U_Z = U_MOD[1] + MODU
        U_WOUT = U_Z + 4
        U_MOE = [U_WOUT + 4, 0]
        U_QKV = U_MOE[0] + 3 * E
        U_WO = U_QKV + 3
        U_MOE[1] = U_WO + 2
        N_UNITS = U_MOE[1] + 3 * E
        first6 = U_MOE[0]
        order6 = [(first6 + j) % 3 for j in range(3)] + [3, 4, 5]

        def slot_of(n):
            return n % 3 if n < first6 else order6[(n - first6) % 6]

        use_of, seen, last_of, holder = [], [0] * 6, [], [None] * 6
        for n in range(N_UNITS):
            s = slot_of(n)
            seen[s] += 1
            use_of.append(seen[s])
            last_of.append(holder[s] if holder[s] is not None else (first6 - 1 if s >= 3 else None))
            holder[s] = n

        ring_in = [sem(f"ring_in{i}") for i in range(6)]
        mod_mm = sem("mod_mm")
        cv_mm = sem("cv_mm")
        z_mm = sem("z_mm")
        wout_mm = sem("wout_mm")
        qkv_mm = sem("qkv_mm")
        wo_mm = sem("wo_mm")
        moe_gate = sem("moe_gate")
        moe_up = sem("moe_up")
        moe_down = sem("moe_down")

        def used(n):
            for l in range(2):
                if U_MOD[l] <= n < U_MOD[l] + MODU:
                    return mod_mm, MODU * l + n - U_MOD[l] + 1
            if U_XBC <= n < U_MOD[1]:
                return cv_mm, 4 * (n - U_XBC + 1)
            if U_Z <= n < U_WOUT:
                return z_mm, NT * (n - U_Z + 1)
            if U_WOUT <= n < U_MOE[0]:
                return wout_mm, NT * (n - U_WOUT + 1)
            if U_QKV <= n < U_WO:
                return qkv_mm, [2, 4, 8][n - U_QKV]
            if U_WO <= n < U_MOE[1]:
                return wo_mm, NTL * (n - U_WO + 1)
            l = int(n >= U_MOE[1])
            which, b = moe_unit(n - U_MOE[l])
            return (moe_gate, moe_up, moe_down)[which], E * l + b + 1

        def moe_unit(j):
            if j < 2:
                return j, 0
            if j == 3 * E - 1:
                return 2, E - 1
            b, r = divmod(j - 2, 3)
            return (0, b + 1) if r == 0 else (1, b + 1) if r == 1 else (2, b)

        def unit(n, pattern="p (k n) -> p k n", **dims):
            dims = dims or {"k": KD}
            at = ring_at[slot_of(n)]
            return mem[:, at:at + SLOT].rearrange(pattern, **dims)

        def unit_wait(eng, n):
            eng.wait_ge(ring_in[slot_of(n)], 16 * use_of[n])

        def unit_source(n):
            if n < U_XBC or U_MOD[1] <= n < U_Z:
                l = 0 if n < U_XBC else 1
                c = (n - U_MOD[l]) * COLS
                return a["mod_w"][l, :, c:c + COLS].rearrange("(p k) n -> p k n", k=KD)
            if n < U_MOD[1]:
                c = DI + (n - U_XBC) * COLS
                return a["ssd_w_in"][0, :, c:c + COLS].rearrange("(p k) n -> p k n", k=KD)
            if n < U_WOUT:
                c = (n - U_Z) * COLS
                return a["ssd_w_in"][0, :, c:c + COLS].rearrange("(p k) n -> p k n", k=KD)
            if n < U_MOE[0]:
                half, part = divmod(n - U_WOUT, 2)
                return a["ssd_w_out"][0, part * 1024:(part + 1) * 1024, half * COLS:(half + 1) * COLS].rearrange(
                    "(c p) n -> p c n", p=P)
            if U_QKV <= n < U_WO:
                c = (n - U_QKV) * COLS
                return a["att_w_qkv"][0, :, c:c + COLS].rearrange("(p k) n -> p k n", k=KD)
            if U_WO <= n < U_MOE[1]:
                c = (n - U_WO) * COLS
                return a["att_w_o"][0, :, c:c + COLS].rearrange("(p k) n -> p k n", k=KD)
            l = int(n >= U_MOE[1])
            return moe_source(l, *moe_unit(n - U_MOE[l]))

        def moe_source(l, which, e):
            w = a[("moe_w_gate", "moe_w_up", "moe_w_down")[which]]
            return w[l, e].rearrange("(p k) n -> p k n", k=(KD, KD, F // P)[which])

        def load_unit(sp, n):
            if last_of[n] is not None:
                sp.wait_ge(*used(last_of[n]))
            src = unit_source(n)
            sp.dma_start(unit(n, k=src.shape[1]), src).then_inc(ring_in[slot_of(n)], 16)

        silu_c = small(16, "p (k r) -> p k r", k=KD)
        craw = small(16, "p (r k) -> p r k", r=2)
        modcol = small(48, "p (s w k) -> p s w k", s=2, w=3)
        gcol = small(8)
        ss = small(4)
        ms = small(4)
        rstd = small(4)
        mhalf = small(4)

        s_const = sem("s_const")
        s_c = sem("s_c")
        s_silu_c = sem("s_silu_c")
        s_init = sem("s_init")
        dve_chain = sem("dve_chain")
        chain = [0]

        def bc(v, axis, n):
            v = v.unsqueeze(axis)
            return v.to_broadcast([n if i == axis else m for i, m in enumerate(v.shape)])

        def link(dve, ins):
            chain[0] += 1
            ins.then_inc(dve_chain, 1)
            dve.wait_ge(dve_chain, chain[0])

        msum = region(A_Y, 1024, "p (b n) -> p b n", b=2)
        mrow = region(A_Y + 1024, 1024, "p (b n) -> p b n", parts=2, b=2)
        mbias = region(A_Y + 2048, 1024, "p (b n) -> p b n", parts=2, b=2)
        mod_zero = sem("mod_zero")
        mod_ev = sem("mod_ev")
        mod_sum = sem("mod_sum")
        mod_row = sem("mod_row")
        mod_b_in = [sem(f"mod_b_in{i}") for i in range(2)]
        mod_st = [sem(f"mod_st{i}") for i in range(2)]

        def mod_pe(pe, l):
            for n in range(MODU + 1):
                q = MODU * l + n
                if n < MODU:
                    unit_wait(pe, U_MOD[l] + n)
                    if n == 0:
                        pe.wait_ge(mod_zero, 2 * l + 2)
                    if n >= 2:
                        pe.wait_ge(mod_ev, q - 1)
                    w = unit(U_MOD[l] + n)
                    for k in range(KD):
                        j = 32 * (k % 4)
                        mm = nc.tensor.matmul(psum[q % 2][j:j + 2, :], lhsT=silu_c[:, k, :], rhs=w[:, k, :],
                                              start=(k < 4), stop=(k >= 4), skip_group_check=True)
                    mm.then_inc(mod_mm, 1)
                if n >= 1:
                    pe.wait_ge(mod_ev, q)
                    if n >= 3:
                        pe.wait_ge(mod_row, q - 2)
                    nc.tensor.matmul(psum[2 + (q - 1) % 2][0:2, :], lhsT=consts[:, C_SEL:C_SEL + 2],
                                     rhs=msum[:, (q - 1) % 2, :], start=True, stop=True).then_inc(mod_sum, 1)

        def mod_act(act, l):
            for n in range(MODU + 1):
                q = MODU * l + n
                if n < MODU:
                    if q >= 2:
                        act.wait_ge(mod_row, q - 1)
                    act.dma_start(mbias[:, q % 2, :], a["mod_b"][l:l + 1, n * COLS:(n + 1) * COLS].to_broadcast(
                        [2, COLS])).then_inc(mod_b_in[q % 2], 16)
                    act.wait_ge(mod_mm, q + 1)
                    if q >= 2:
                        act.wait_ge(mod_sum, q - 1)
                    nc.scalar.activation(msum[:, q % 2, :], psum[q % 2][:, :], ACT.Copy).then_inc(mod_ev, 1)
                if n >= 1:
                    act.wait_ge(mod_row, q)
                    act.dma_start(mod_dram[l, :, (n - 1) * COLS:n * COLS], mrow[:, (q - 1) % 2, :]).then_inc(
                        mod_st[(q - 1) % 2], 16)

        def mod_dve(dve, l):
            for b in range(2):
                nc.vector.memset(psum[b][:, :], 0.0).then_inc(mod_zero, 1)
            for n in range(MODU):
                q = MODU * l + n
                dve.wait_ge(mod_sum, q + 1)
                dve.wait_ge(mod_b_in[q % 2], 16 * (q // 2 + 1))
                if q >= 2:
                    dve.wait_ge(mod_st[q % 2], 16 * (q // 2))
                nc.vector.tensor_tensor(mrow[:, q % 2, :], psum[2 + q % 2][0:2, :], mbias[:, q % 2, :],
                                        ALU.add).then_inc(mod_row, 1)

        def mod_wait(eng, l, units):
            q = MODU * l + units
            eng.wait_ge(mod_st[0], 16 * ((q + 1) // 2))
            eng.wait_ge(mod_st[1], 16 * (q // 2))

        xin = region(A_H, NT * D, "p (t d) -> p t d", t=NT)
        xn = [region(at, 4096, "p (t d) -> p t d", t=NT) for at in (A_Y + 4096, A_WORK)]
        aT = [region(at, 4096, "p (k n) -> p k n", k=KD) for at in (A_AT, A_BCT + 6144)]
        x_in = sem("x_in")
        n1_cols = sem("n1_cols")
        n1_A = sem("n1_A")
        n1_ss = sem("n1_ss")
        n1_ms = sem("n1_ms")
        n1_rstd = sem("n1_rstd")
        n1_xn = sem("n1_xn")
        n1_tp = sem("n1_tp")
        n1_ea = sem("n1_ea")
        n1_ed = sem("n1_ed")

        def norm1_pool(pool, l):
            mod_wait(pool, l, 4)
            if l:
                pool.wait_ge(n1_ed, 4)
                pool.wait_ge(n1_ea, 4)
            for s in range(2):
                for w in range(2):
                    pool.dma_start(modcol[:, s, w, :], mod_dram[l, s, w * D:(w + 1) * D].rearrange(
                        "(p k) -> p k", k=KD)).then_inc(n1_cols, 16)
            pool.dma_start(gcol[:, :], a["norm1_g"][l].rearrange("(p k) -> p k", k=KD)).then_inc(n1_cols, 16)

        def norm1_rstd_pool(pool, l):
            pool.wait_ge(n1_ms, l + 1)
            nc.gpsimd.tensor_tensor(rstd[:, :], ms[:, :], mhalf[:, :], ALU.pow).then_inc(n1_rstd, 1)

        def norm1_square_act(act, l):
            if l == 0:
                act.wait_ge(x_in, 32)
            else:
                act.wait_ge(cb_x, NT)
            for t in range(NT):
                nc.scalar.activation(xn[l][:, t, :], xin[:, t, :], ACT.Square, accum_out=ss[:, t:t + 1]).then_inc(
                    n1_ss, 1)

        def norm1_act(act, l):
            act.wait_ge(n1_A, 2 * l + 2)
            for i in range(0, 8, 2):
                s, kp = divmod(i, 4)
                act.wait_ge(n1_tp, 8 * l + i + 1)
                for kk in range(2):
                    k = 2 * kp + kk
                    ev = nc.scalar.activation(aT[l][:, k, s * SEQ:(s + 1) * SEQ], psum[4][:, kk * SEQ:(kk + 1) * SEQ],
                                              ACT.Identity, bias=modcol[:, s, 0, k:k + 1], scale=modcol[:, s, 2, k:k + 1])
                ev.then_inc(n1_ea, 1)

        def norm1_scale_dve(dve, l):
            dve.wait_ge(n1_ss, NT * (l + 1))
            nc.vector.tensor_scalar(ms[:, :], ss[:, :], 1.0 / D, EPS, ALU.mult, ALU.add).then_inc(n1_ms, 1)
            dve.wait_ge(n1_rstd, l + 1)
            for t in range(NT):
                nc.vector.tensor_scalar(xn[l][:, t, :], xin[:, t, :], rstd[:, t:t + 1], None, ALU.mult).then_inc(
                    n1_xn, 1)

        def norm1_dve(dve, l):
            dve.wait_ge(n1_cols, 80 * (l + 1))
            for s in range(2):
                nc.vector.scalar_tensor_tensor(modcol[:, s, 2, :], modcol[:, s, 1, :], 1.0, gcol[:, :],
                                               ALU.add, ALU.mult).then_inc(n1_A, 1)
            dve.wait_ge(n1_A, 2 * l + 2)
            for i in range(1, 8, 2):
                s, kp = divmod(i, 4)
                dve.wait_ge(n1_tp, 8 * l + i + 1)
                for kk in range(2):
                    k = 2 * kp + kk
                    ev = nc.vector.tensor_scalar(aT[l][:, k, s * SEQ:(s + 1) * SEQ], psum[5][:, kk * SEQ:(kk + 1) * SEQ],
                                                 modcol[:, s, 2, k:k + 1], modcol[:, s, 0, k:k + 1], ALU.mult, ALU.add)
                ev.then_inc(n1_ed, 1)

        def norm1_pe(pe, l):
            if l:
                pe.wait_ge(moe_out, 1)
            for i in range(8):
                s, kp = divmod(i, 4)
                pe.wait_ge(n1_xn, NT * l + 2 * s + 2)
                if i >= 2:
                    pe.wait_ge((n1_ea, n1_ed)[i % 2], 4 * l + i // 2)
                for kk in range(2):
                    for t in range(2):
                        c = kk * SEQ + t * P
                        tp = nc.tensor.transpose(psum[4 + i % 2][:, c:c + P], xn[l][:, 2 * s + t, 2 * kp + kk::KD], ident)
                tp.then_inc(n1_tp, 1)

        xrow = region(A_XROW, 8192, "p (t c) -> p t c", t=NT)
        BT = region(A_BCT, 2048, "p (g n) -> p g n", g=GROUPS)
        CT = region(A_BCT + 2048, 2048, "p (g n) -> p g n", g=GROUPS)
        Brow = region(A_BCT + 4096, 2048, "p (t g n) -> p t g n", t=NT, g=GROUPS)
        PADW = SEQ + TAPS - 1
        cin = region(A_WORK, 4 * PADW, "p (b s n) -> p b s n", b=2, s=2)
        cacc = region(A_WORK + 1040, 1024, "p (b n) -> p b n", b=2)
        cxT = region(A_WORK + 2064, 1024, "p (b n) -> p b n", b=2)
        convw = region(A_WORK + 3088, NCH * TAPS, "p (c j) -> p c j", c=NCH)
        convb = region(A_WORK + 3208, NCH)
        wdt = region(A_Y + 3072, KD * 64, "p (k n) -> p k n", k=KD)
        sw_in = sem("sw_in")
        cv_pad = sem("cv_pad")
        cv_in = sem("cv_in")
        cv_out = sem("cv_out")
        cv_silu = sem("cv_silu")
        cv_tp = sem("cv_tp")
        cv_row = sem("cv_row")
        NROW = 20

        def conv_pe(pe):
            def transposes(c):
                pe.wait_ge(cv_silu, c + 1)
                if c >= 2:
                    pe.wait_ge(cv_row, c - 1)
                for t in range(NT):
                    src = cxT[:, c % 2, t * P:(t + 1) * P] if c < 16 else BT[:, c - 16, t * P:(t + 1) * P]
                    tp = nc.tensor.transpose(psum[4 + c % 2][:, t * P:(t + 1) * P], src, ident)
                tp.then_inc(cv_tp, 1)

            pe.wait_ge(n1_ea, 4)
            pe.wait_ge(n1_ed, 4)
            for c in range(NCH):
                if c % 4 == 0:
                    unit_wait(pe, U_XBC + c // 4)
                w = unit(U_XBC + c // 4)
                if c >= 2:
                    pe.wait_ge(cv_in, c - 1)
                for k in range(KD):
                    mm = nc.tensor.matmul(psum[c % 2][:, :], lhsT=w[:, k, (c % 4) * P:(c % 4 + 1) * P],
                                          rhs=aT[0][:, k, :], start=(k == 0), stop=(k == KD - 1))
                mm.then_inc(cv_mm, 1)
                if 2 <= c < NROW + 2:
                    transposes(c - 2)

        def conv_act(act):
            act.wait_ge(cv_pad, 2)
            for c in range(NCH + 3):
                if c < NCH:
                    act.wait_ge(cv_mm, c + 1)
                    if c >= 2:
                        act.wait_ge(cv_out, c - 1)
                    nc.scalar.activation(cin[:, c % 2, :, 2:2 + SEQ], psum[c % 2][:, :].rearrange(
                        "p (s n) -> p s n", s=2), ACT.Copy).then_inc(cv_in, 1)
                if 1 <= c < NCH + 1:
                    d = c - 1
                    act.wait_ge(cv_out, d + 1)
                    if 2 <= d < 16:
                        act.wait_ge(cv_tp, d - 1)
                    to = cxT[:, d % 2, :] if d < 16 else BT[:, d - 16, :] if d < 20 else CT[:, d - 20, :]
                    nc.scalar.activation(to, cacc[:, d % 2, :], ACT.Silu, bias=convb[:, d:d + 1]).then_inc(cv_silu, 1)
                if 3 <= c < NROW + 3:
                    d = c - 3
                    act.wait_ge(cv_tp, d + 1)
                    to = xrow[:, :, d * P:(d + 1) * P] if d < 16 else Brow[:, :, d - 16, :]
                    nc.scalar.activation(to, psum[4 + d % 2][:, :].rearrange("p (t n) -> p t n", t=NT),
                                         ACT.Copy).then_inc(cv_row, 1)

        def conv_dve(dve):
            for b in range(2):
                nc.vector.memset(cin[:, b, :, :], 0.0).then_inc(cv_pad, 1)
            dve.wait_ge(sw_in, 16 * 5)
            for c in range(NCH):
                dve.wait_ge(cv_in, c + 1)
                if c >= 2:
                    dve.wait_ge(cv_silu, c - 1)
                acc = cacc[:, c % 2, :].rearrange("p (s n) -> p s n", s=2)
                link(dve, nc.vector.tensor_scalar(acc, cin[:, c % 2, :, 0:SEQ], convw[:, c, 0:1], None, ALU.mult))
                for j in range(1, TAPS):
                    st = nc.vector.scalar_tensor_tensor(acc, cin[:, c % 2, :, j:j + SEQ], convw[:, c, j:j + 1], acc,
                                                        ALU.mult, ALU.add)
                    if j < TAPS - 1:
                        link(dve, st)
                st.then_inc(cv_out, 1)

        dtT = A_WORK + 6144
        dt = region(dtT, 256, "p (t d h) -> p t d h", t=NT, d=2)
        dtA = region(dtT + 256, 256, "p (t d h) -> p t d h", t=NT, d=2)
        EX = region(dtT + 512, 768, "p (d t w h) -> p d t w h", d=2, t=NT, w=3)
        wend = region(dtT + 1280, 256, "p (d t h) -> p d t h", d=2, t=NT)
        tmp6 = [region(A_WORK + 4096 + 256 * i, 256) for i in range(6)]
        dtb = region(A_WORK + 5632, 64)
        alog = region(A_WORK + 5696, 64)
        nega = region(A_WORK + 5760, 64)
        dt_mm = sem("dt_mm")
        dt_x = sem("dt_x")
        dt_u = sem("dt_u")
        dt_w = sem("dt_w")
        dt_l = sem("dt_l")
        dt_A = sem("dt_A")
        ex_mm = sem("ex_mm")
        ex_ev = sem("ex_ev")
        wend_ok = sem("wend_ok")

        def dt_pe(pe):
            pe.wait_ge(sw_in, 16 * 5)
            for t in range(NT):
                for k in range(KD):
                    mm = nc.tensor.matmul(psum[6][:, t * 64:(t + 1) * 64], lhsT=aT[0][:, k, t * P:(t + 1) * P],
                                          rhs=wdt[:, k, :], start=(k == 0), stop=(k == KD - 1))
            mm.then_inc(dt_mm, 1)

        def dt_dve(dve):
            x, r, w, m, u, lg = tmp6
            dve.wait_ge(dt_mm, 1)
            link(dve, nc.vector.tensor_tensor(x.rearrange("p (t n) -> p t n", t=NT),
                                              psum[6][:, 0:256].rearrange("p (t n) -> p t n", t=NT),
                                              bc(dtb, 1, NT), ALU.add))
            nc.vector.tensor_scalar(r, x, 0.0, None, ALU.max)
            nc.vector.scalar_tensor_tensor(w, x, -1.0, x, ALU.mult, ALU.max).then_inc(dt_x, 1)
            dve.wait_ge(dt_u, 2)
            link(dve, nc.vector.tensor_scalar(w, u, 1.0, None, ALU.add))
            nc.vector.tensor_scalar(m, w, 1.0, None, ALU.is_equal).then_inc(dt_w, 1)
            dve.wait_ge(dt_w, 1)
            dve.wait_ge(dt_l, 1)
            link(dve, nc.vector.scalar_tensor_tensor(w, w, -1.0, m, ALU.add, ALU.add))
            link(dve, nc.vector.reciprocal(w, w))
            link(dve, nc.vector.tensor_tensor(w, w, lg, ALU.mult))
            link(dve, nc.vector.tensor_tensor(w, w, m, ALU.add))
            link(dve, nc.vector.tensor_tensor(w, w, u, ALU.mult))
            dtf = dt.rearrange("p t d h -> p (t d h)")
            link(dve, nc.vector.tensor_tensor(dtf, w, r, ALU.add))
            link(dve, nc.vector.tensor_scalar(nega, nega, -1.0, None, ALU.mult))
            nc.vector.tensor_tensor(dtA.rearrange("p t d h -> p t (d h)"), dt.rearrange("p t d h -> p t (d h)"),
                                    bc(nega, 1, NT), ALU.mult).then_inc(dt_A, 1)

        def decay_dve(dve):
            dve.wait_ge(ex_ev, 2)
            for d in range(2):
                nc.vector.tensor_tensor(wend[:, d], EX[:, d, :, 1, :], dt[:, :, d, :], ALU.mult).then_inc(wend_ok, 1)

        def dt_act(act):
            x, r, w, m, u, lg = tmp6
            act.wait_ge(sw_in, 16 * 5)
            nc.scalar.activation(nega, alog, ACT.Exp).then_inc(dt_u, 1)
            act.wait_ge(dt_x, 1)
            nc.scalar.activation(u, w, ACT.Exp, scale=-1.0).then_inc(dt_u, 1)
            act.wait_ge(dt_w, 1)
            nc.scalar.activation(lg, w, ACT.Ln).then_inc(dt_l, 1)

        def decay_act(act):
            for d in range(2):
                act.wait_ge(ex_mm, d + 1)
                nc.scalar.activation(EX[:, d].rearrange("p t w h -> p (t w h)"), psum[6 + d][:, 0:384],
                                     ACT.Exp).then_inc(ex_ev, 1)

        def decay_pe(pe):
            pe.wait_ge(dt_A, 1)
            for d in range(2):
                upto, after = ((C_LE, C_GT), (C_GE, C_LT))[d]
                for t in range(NT):
                    for w, c in enumerate((upto, after, C_ONE)):
                        at = (t * 3 + w) * HEADS
                        mm = nc.tensor.matmul(psum[6 + d][:, at:at + HEADS], lhsT=consts[:, c:c + P],
                                              rhs=dtA[:, t, d, :], start=True, stop=True)
                mm.then_inc(ex_mm, 1)

        y = region(A_Y, 8192, "p (t c) -> p t c", t=NT)
        h = region(A_H, 4096, "p (d g n) -> p d g n", d=2, g=GROUPS)
        RU = region(A_WORK, 2048, "p (b r n) -> p b r n", b=2, r=HG)
        EB = region(A_WORK + 2048, 2048, "p (b r n) -> p b r n", b=2, r=HG)
        xdt = region(A_WORK + 4096, 1024, "p (b r n) -> p b r n", b=2, r=HG)
        xw = region(A_WORK + 5120, 1024, "p (b r n) -> p b r n", b=2, r=HG)
        cbm = sb("cbm", [P, P])
        ytmp = region(A_WORK + 7680, COLS)
        STEPS = [(0, 2), (1, 3), (0, 3), (1, 2), (0, 0), (1, 1), (0, 1), (1, 0)]
        ITEMS = [(d, t, g, s) for s, (d, t) in enumerate(STEPS) for g in range(GROUPS)]
        sc_ru = sem("sc_ru")
        sc_xdt = sem("sc_xdt")
        sc_xw = sem("sc_xw")
        sc_seg = sem("sc_seg")
        sc_cb = sem("sc_cb")
        sc_e = sem("sc_e")
        sc_cbm = sem("sc_cbm")
        sc_mix = sem("sc_mix")
        sc_y = sem("sc_y")
        sc_st = sem("sc_st")
        sc_yev = sem("sc_yev")
        sc_h = sem("sc_h")
        NI = len(ITEMS)
        NST = NI - 2 * GROUPS

        def heads(v, g):
            return v[:, g * HG:(g + 1) * HG]

        def scan_pool(pool):
            pool.wait_ge(cv_row, NROW)
            pool.wait_ge(wend_ok, 2)
            for i, (d, t, g, s) in enumerate(ITEMS):
                b = i % 2
                x_g = xrow[:, t, g * GW:(g + 1) * GW].rearrange("p (r n) -> p r n", r=HG)
                if i >= 2:
                    pool.wait_ge(sc_seg, i - 1)
                tri = (C_LE, C_GE)[d]
                nc.gpsimd.tensor_tensor(RU[:, b], bc(heads(dtA[:, t, d], g), 2, P), bc(consts[:, tri:tri + P], 1, HG),
                                        ALU.mult).then_inc(sc_ru, 1)
                if i >= 2:
                    pool.wait_ge(sc_y, i - 1)
                nc.gpsimd.tensor_tensor(xdt[:, b], x_g, bc(heads(dt[:, t, d], g), 2, HD), ALU.mult).then_inc(sc_xdt, 1)
                if i < NST:
                    if i >= 2:
                        pool.wait_ge(sc_st, i - 1)
                    nc.gpsimd.tensor_tensor(xw[:, b], x_g, bc(heads(wend[:, d, t], g), 2, HD), ALU.mult).then_inc(
                        sc_xw, 1)

        def scan_pe(pe):
            def head(i):
                d, t, g, s = ITEMS[i]
                b = i % 2
                pe.wait_ge(sc_ru, i + 1)
                if i >= 2:
                    pe.wait_ge(sc_e, 2 * (i - 1))
                c = (C_GT, C_LT)[d]
                for q in range(2):
                    mm = nc.tensor.matmul(psum[2 * b + q][:, :], lhsT=consts[:, c:c + P],
                                          rhs=RU[:, b, 4 * q:4 * q + 4, :].rearrange("p r n -> p (r n)"),
                                          start=True, stop=True)
                mm.then_inc(sc_seg, 1)
                if i >= 1:
                    pe.wait_ge(sc_cbm, i)
                nc.tensor.matmul(psum[4][:, 0:P], lhsT=BT[:, g, t * P:(t + 1) * P], rhs=CT[:, g, t * P:(t + 1) * P],
                                 start=True, stop=True).then_inc(sc_cb, 1)

            pe.wait_ge(cv_silu, NCH)
            pe.wait_ge(cv_row, NROW)
            pe.wait_ge(ex_ev, 2)
            pe.wait_ge(mod_row, 2 * MODU)
            head(0)
            for i, (d, t, g, s) in enumerate(ITEMS):
                if i + 1 < NI:
                    head(i + 1)
                b = i % 2
                pe.wait_ge(sc_mix, i + 1)
                pe.wait_ge(sc_xdt, i + 1)
                if i >= 1:
                    pe.wait_ge(sc_yev, i)
                if s >= 2:
                    pe.wait_ge(sc_h, i - 8 + 1)
                    nc.tensor.matmul(psum[6][:, :], lhsT=CT[:, g, t * P:(t + 1) * P], rhs=h[:, d, g, :],
                                     start=True, stop=True)
                for r in range(HG):
                    mm = nc.tensor.matmul(psum[5][:, r * HD:(r + 1) * HD], lhsT=EB[:, b, r, :], rhs=xdt[:, b, r, :],
                                          start=True, stop=True)
                mm.then_inc(sc_y, 1)
                if i < NST:
                    pe.wait_ge(sc_xw, i + 1)
                    if i >= 1:
                        pe.wait_ge(sc_h, i)
                    nc.tensor.matmul(psum[7][:, :], lhsT=Brow[:, t, g, :],
                                     rhs=xw[:, b].rearrange("p r n -> p (r n)"), start=True, stop=True).then_inc(
                        sc_st, 1)

        def scan_act(act):
            for i in range(NI):
                b = i % 2
                act.wait_ge(sc_seg, i + 1)
                if i >= 2:
                    act.wait_ge(sc_y, i - 1)
                for q in range(2):
                    nc.scalar.activation(EB[:, b, 4 * q:4 * q + 4, :].rearrange("p r n -> p (r n)"),
                                         psum[2 * b + q][:, :], ACT.Exp).then_inc(sc_e, 1)

        def scan_dve(dve):
            def tail(i):
                d, t, g, s = ITEMS[i]
                first = s in (0, 1, 4, 5)
                y_g = y[:, t, g * GW:(g + 1) * GW]
                dve.wait_ge(sc_y, i + 1)
                if s < 2:
                    nc.vector.tensor_copy(y_g, psum[5][:, :]).then_inc(sc_yev, 1)
                else:
                    link(dve, nc.vector.tensor_tensor(ytmp.rearrange("p (r n) -> p r n", r=HG),
                                                      psum[6][:, :].rearrange("p (r n) -> p r n", r=HG),
                                                      bc(heads(EX[:, d, t, 0], g), 2, HD), ALU.mult))
                    nc.vector.tensor_tensor(y_g if first else ytmp, ytmp, psum[5][:, :],
                                            ALU.add).then_inc(sc_yev, 1)
                    dve.wait_ge(sc_yev, i + 1)
                    if not first:
                        link(dve, nc.vector.tensor_tensor(y_g, y_g, ytmp, ALU.add))
                if i < NST:
                    dve.wait_ge(sc_st, i + 1)
                    if s < 2:
                        nc.vector.tensor_copy(h[:, d, g, :], psum[7][:, :]).then_inc(sc_h, 1)
                    else:
                        hv = h[:, d, g, :].rearrange("p (r n) -> p r n", r=HG)
                        link(dve, nc.vector.tensor_tensor(hv, hv, bc(heads(EX[:, d, t, 2], g), 2, HD), ALU.mult))
                        nc.vector.tensor_tensor(h[:, d, g, :], h[:, d, g, :], psum[7][:, :], ALU.add).then_inc(sc_h, 1)

            for i, (d, t, g, s) in enumerate(ITEMS):
                b = i % 2
                dve.wait_ge(sc_cb, i + 1)
                if i >= 1:
                    dve.wait_ge(sc_mix, i)
                m = (C_LE, C_GE)[d]
                nc.vector.tensor_tensor(cbm[:, :], psum[4][:, 0:P], consts[:, m:m + P], ALU.mult).then_inc(sc_cbm, 1)
                dve.wait_ge(sc_cbm, i + 1)
                dve.wait_ge(sc_e, 2 * i + 2)
                nc.vector.tensor_tensor(EB[:, b], EB[:, b], bc(cbm[:, :], 1, HG), ALU.mult).then_inc(sc_mix, 1)
                if i >= 1:
                    tail(i - 1)
            tail(NI - 1)

        yT = region(A_XROW, 8192, "p (c n) -> p c n", c=16)
        zs = region(A_WORK, 1024, "p (b n) -> p b n", b=2)
        dskip = region(A_WORK + 1024, HEADS)
        ngain = region(A_WORK + 1056, 16)
        gss = region(A_WORK + 1072, 16, "p (g t) -> p g t", g=GROUPS)
        gms = region(A_WORK + 1088, 16, "p (g t) -> p g t", g=GROUPS)
        grs = region(A_WORK + 1104, 16, "p (g t) -> p g t", g=GROUPS)
        gjunk = region(A_WORK + 4096, NT * COLS, "p (t n) -> p t n", t=NT)
        otmp = region(A_WORK + 2048, 1024, "p (b n) -> p b n", b=2)
        gate1 = region(A_BCT, 2048, "p (s d) -> p s d", s=2)
        fin_in = sem("fin_in")
        fin_xd = sem("fin_xd")
        fin_add = sem("fin_add")
        z_silu = sem("z_silu")
        z_mul = sem("z_mul")
        gn_ss = sem("gn_ss")
        gn_ms = sem("gn_ms")
        gn_rs = sem("gn_rs")
        gn_y = sem("gn_y")
        gn_tp = sem("gn_tp")
        gn_T = sem("gn_T")
        m1_x = sem("m1_x")

        def finish_pool(pool):
            pool.wait_ge(sc_mix, NI)
            pool.wait_ge(sc_xdt, NI)
            pool.dma_start(dskip, a["ssd_d"].to_broadcast([P, HEADS])).then_inc(fin_in, 16)
            pool.dma_start(ngain, a["norm_cols"]).then_inc(fin_in, 16)
            pool.wait_ge(fin_in, 32)
            for t in range(NT):
                xv = xrow[:, t, :].rearrange("p (r n) -> p r n", r=HEADS)
                nc.gpsimd.tensor_tensor(xv, xv, bc(dskip, 2, HD), ALU.mult).then_inc(fin_xd, 1)
            pool.wait_ge(sc_y, NI)
            pool.wait_ge(sc_h, NST)
            for s, name in enumerate(("x", "ctx")):
                pool.dma_start(xin[:, 2 * s:2 * s + 2, :], a[name][0].rearrange("(t p) d -> p t d", p=P)).then_inc(
                    fin_in, 16)
                pool.dma_start(gate1[:, s, :], mod_dram[0, s:s + 1, 2 * D:3 * D].to_broadcast([P, D])).then_inc(
                    fin_in, 16)
            for g in range(GROUPS):
                pool.wait_ge(gn_ms, g + 1)
                nc.gpsimd.tensor_tensor(grs[:, g, :], gms[:, g, :], mhalf[:, :], ALU.pow).then_inc(gn_rs, 1)

        def finish_pe(pe):
            def gate(g):
                unit_wait(pe, U_Z + g)
                w = unit(U_Z + g)
                for t in range(NT):
                    i = NT * g + t
                    if i >= 2:
                        pe.wait_ge(z_silu, i - 1)
                    for k in range(KD):
                        mm = nc.tensor.matmul(psum[i % 2][:, :], lhsT=aT[0][:, k, t * P:(t + 1) * P], rhs=w[:, k, :],
                                              start=(k == 0), stop=(k == KD - 1))
                    mm.then_inc(z_mm, 1)

            def turn(g):
                pe.wait_ge(gn_y, NT * (g + 1))
                for q in range(4):
                    i = 4 * g + q
                    if i >= 2:
                        pe.wait_ge(gn_T, i - 1)
                    for t in range(NT):
                        tp = nc.tensor.transpose(psum[2 + i % 2][:, t * P:(t + 1) * P],
                                                 y[:, t, g * GW + q * P:g * GW + (q + 1) * P], ident)
                    tp.then_inc(gn_tp, 1)

            pe.wait_ge(sc_e, 2 * NI)
            gate(0)
            for g in range(GROUPS):
                if g + 1 < GROUPS:
                    gate(g + 1)
                turn(g)
            pe.wait_ge(gn_T, 16)
            pe.wait_ge(z_silu, 16)
            pe.wait_ge(sc_yev, NI)
            pe.wait_ge(sc_h, NST)
            for n in range(4):
                half, part = divmod(n, 2)
                unit_wait(pe, U_WOUT + n)
                w = unit(U_WOUT + n)
                for t in range(NT):
                    for c in range(8):
                        mm = nc.tensor.matmul(psum[4 - 4 * half + t][:, :], lhsT=yT[:, 8 * part + c, t * P:(t + 1) * P],
                                              rhs=w[:, c, :], start=(part == 0 and c == 0), stop=(part == 1 and c == 7))
                    mm.then_inc(wout_mm, 1)

        def finish_act(act):
            def square(g):
                act.wait_ge(z_mul, NT * (g + 1))
                if g:
                    act.wait_ge(gn_ss, NT * g)
                for t in range(NT):
                    nc.scalar.activation(gjunk[:, t], y[:, t, g * GW:(g + 1) * GW], ACT.Square,
                                         accum_out=gss[:, g, t:t + 1]).then_inc(gn_ss, 1)

            def evac(g):
                for i in range(4 * g, 4 * g + 4):
                    act.wait_ge(gn_tp, i + 1)
                    nc.scalar.activation(yT[:, i, :], psum[2 + i % 2][:, :], ACT.Identity,
                                         scale=ngain[:, i:i + 1]).then_inc(gn_T, 1)

            act.wait_ge(fin_in, 32)
            act.wait_ge(sc_mix, NI)
            act.wait_ge(sc_seg, NI)
            for g in range(GROUPS):
                for t in range(NT):
                    i = NT * g + t
                    act.wait_ge(z_mm, i + 1)
                    if i >= 2:
                        act.wait_ge(z_mul, i - 1)
                    nc.scalar.activation(zs[:, i % 2, :], psum[i % 2][:, :], ACT.Silu).then_inc(z_silu, 1)
                if g == 0:
                    act.wait_ge(fin_add, NT)
                square(g)
                if g >= 1:
                    evac(g - 1)
            evac(GROUPS - 1)

        def finish_dve(dve):
            for t in range(NT):
                dve.wait_ge(fin_xd, t + 1)
                nc.vector.tensor_tensor(y[:, t, :], y[:, t, :], xrow[:, t, :], ALU.add).then_inc(fin_add, 1)
            dve.wait_ge(fin_add, NT)

            def mul(g):
                for t in range(NT):
                    i = NT * g + t
                    dve.wait_ge(z_silu, i + 1)
                    y_g = y[:, t, g * GW:(g + 1) * GW]
                    nc.vector.tensor_tensor(y_g, y_g, zs[:, i % 2, :], ALU.mult).then_inc(z_mul, 1)

            def norm(g):
                dve.wait_ge(gn_ss, NT * (g + 1))
                nc.vector.tensor_scalar(gms[:, g, :], gss[:, g, :], 1.0 / GW, EPS, ALU.mult, ALU.add).then_inc(gn_ms, 1)
                dve.wait_ge(gn_rs, g + 1)
                for t in range(NT):
                    y_g = y[:, t, g * GW:(g + 1) * GW]
                    nc.vector.tensor_scalar(y_g, y_g, grs[:, g, t:t + 1], None, ALU.mult).then_inc(gn_y, 1)

            mul(0)
            for g in range(GROUPS):
                norm(g)
                if g + 1 < GROUPS:
                    mul(g + 1)
            dve.wait_ge(fin_in, 16 * 6)
            for i in range(2 * NT):
                half, t = divmod(i, NT)
                cs = slice(half * COLS, (half + 1) * COLS)
                dve.wait_ge(wout_mm, 2 * NT * half + NT + t + 1)
                link(dve, nc.vector.tensor_tensor(otmp[:, i % 2, :], psum[4 - 4 * half + t][:, :], gate1[:, t // 2, cs],
                                                  ALU.mult))
                nc.vector.tensor_tensor(xin[:, t, cs], xin[:, t, cs], otmp[:, i % 2, :], ALU.add).then_inc(m1_x, 1)

        M0 = A_BCT
        gate2 = region(M0, 2048, "p (s d) -> p s d", s=2)
        mA = region(M0 + 2048, 2048, "p (s d) -> p s d", s=2)
        mB = region(M0 + 4096, 2048, "p (s d) -> p s d", s=2)
        gain2 = region(M0 + 6144, D)
        frow = region(M0 + 7168, 2048, "p (b d) -> p b d", b=2)
        fT = region(M0 + 9216, 2048, "p (b k n) -> p b k n", b=2, k=KD)
        wrt = region(M0 + 11264, KD * (EG + E), "p (k n) -> p k n", k=KD)
        brt = region(M0 + 11552, EG + E)
        NR = EG + E
        r_at = [M0 + 11600]

        def route_tile(size, pattern=None, **dims):
            v = region(r_at[0], size, pattern, **dims)
            r_at[0] += size
            assert r_at[0] <= M0 + 14336
            return v

        t_n = dict(t=NT)
        r_lg = route_tile(NT * NR, "p (t n) -> p t n", **t_n)
        r_gp = route_tile(NT * 8, "p (t n) -> p t n", **t_n)
        r_gm = route_tile(NT * 8, "p (t n) -> p t n", **t_n)
        r_gi = route_tile(NT * 8, "p (t n) -> p t n", **t_n).bitcast(U32)
        r_gf = route_tile(NT)
        r_g1 = route_tile(NT * EG, "p (t n) -> p t n", **t_n)
        r_ge = route_tile(NT * EG, "p (t n) -> p t n", **t_n)
        r_gs = route_tile(NT)
        r_es = route_tile(NT * 8, "p (t n) -> p t n", **t_n)
        r_em = route_tile(NT * 8, "p (t n) -> p t n", **t_n)
        r_ei = route_tile(NT * 8, "p (t n) -> p t n", **t_n).bitcast(U32)
        r_ef = route_tile(NT * 2, "p (t n) -> p t n", **t_n)
        r_d = route_tile(NT)
        r_w = route_tile(2 * NT, "p (k t) -> p k t", k=2)
        r_one = route_tile(2 * NT * E, "p (k t n) -> p k t n", k=2, t=NT)
        r_m = route_tile(NT * E, "p (t n) -> p t n", **t_n)
        r_r = route_tile(NT * E, "p (t n) -> p t n", **t_n)
        r_q = route_tile(NT * E, "p (t n) -> p t n", **t_n)
        r_tmp = region(M0 + 6144, NT * E, "p (t n) -> p t n", **t_n)
        r_tmp2 = region(M0 + 6144 + 256, EG * NT * 8, "p (t g n) -> p t g n", t=NT, g=EG)
        r_slot = route_tile(2 * NT, "p (k t) -> p k t", k=2)
        r_sloti = route_tile(2 * NT, "p (k t) -> p k t", k=2).bitcast(U32)
        r_pos = route_tile(2 * NT, "p (k t) -> p k t", k=2)
        r_posi = route_tile(2 * NT, "p (k t) -> p k t", k=2).bitcast(U32)
        r_blk = route_tile(2 * NT, "p (k t) -> p k t", k=2)
        r_ov = route_tile(E)
        r_ovc = route_tile(E)
        r_b1 = route_tile(E)
        r_zero = route_tile(E)
        NOVM = overflow_blocks(NT * P)
        r_ove = route_tile(NOVM)
        r_ovi = route_tile(NOVM + 1).bitcast(I32)
        NBM = E + NOVM
        r_tok = route_tile(NBM).bitcast(U32)
        r_ovidx = route_tile(1).bitcast(U32)
        r_Q = region(M0 + 9216, 2 * P, "p (b n) -> p b n", b=2)
        r_R = region(M0 + 9216 + 2 * P, 2 * NBM, "p (b n) -> p b n", b=2)

        n2_in = sem("n2_in")
        n2_g2 = sem("n2_g2")
        n2_ss = sem("n2_ss")
        n2_ms = sem("n2_ms")
        n2_rstd = sem("n2_rstd")
        n2_A = sem("n2_A")
        n2_f = sem("n2_f")
        n2_tp = sem("n2_tp")
        n2_ea = sem("n2_ea")
        n2_ed = sem("n2_ed")
        n2_st = [sem(f"n2_st{i}") for i in range(2)]
        rt_lg = sem("rt_lg")
        rt_d1 = sem("rt_d1")
        rt_e1 = sem("rt_e1")
        rt_m = sem("rt_m")
        rt_rank = sem("rt_rank")
        rt_qr = sem("rt_qr")
        rt_tokp = sem("rt_tokp")
        rt_slot = sem("rt_slot")
        tiles = [NT, NTL]
        base_t = [0, NT]

        def mixer_done(eng, l, t):
            if l == 0:
                eng.wait_ge(m1_x, NT + t + 1)
            else:
                eng.wait_ge(a1_x, 2 * NTL)

        def norm2_pool(pool, l):
            ns = (2, 1)[l]
            if l == 0:
                pool.wait_ge(sc_y, NI)
                pool.wait_ge(sc_st, NST)
                pool.wait_ge(gn_tp, 16)
            else:
                pool.wait_ge(at_otp, 4)
            mod_wait(pool, l, MODU)
            for s in range(ns):
                pool.dma_start(mA[:, s, :], mod_dram[l, s:s + 1, 4 * D:5 * D].to_broadcast([P, D])).then_inc(n2_in, 16)
                pool.dma_start(mB[:, s, :], mod_dram[l, s:s + 1, 3 * D:4 * D].to_broadcast([P, D])).then_inc(n2_in, 16)
            pool.dma_start(gain2, a["norm2_g"][l:l + 1, :].to_broadcast([P, D])).then_inc(n2_in, 16)
            pool.dma_start(wrt[:, :, 0:EG], a["moe_w_group"][l].rearrange("(p k) n -> p k n", k=KD)).then_inc(n2_in, 16)
            pool.dma_start(wrt[:, :, EG:], a["moe_w_router"][l].rearrange("(p k) n -> p k n", k=KD)).then_inc(n2_in, 16)
            pool.dma_start(brt[:, 0:EG], a["moe_b_group"][l:l + 1, :].to_broadcast([P, EG])).then_inc(n2_in, 16)
            pool.dma_start(brt[:, EG:], a["moe_b_router"][l:l + 1, :].to_broadcast([P, E])).then_inc(n2_in, 16)
            pool.wait_ge(n2_ms, l + 1)
            nc.gpsimd.tensor_tensor(rstd[:, :], ms[:, :], mhalf[:, :], ALU.pow).then_inc(n2_rstd, 1)
            for s in range(ns):
                pool.dma_start(gate2[:, s, :], mod_dram[l, s:s + 1, 5 * D:6 * D].to_broadcast([P, D])).then_inc(n2_g2, 16)

        N2_IN = [16 * 9, 16 * 16]

        def norm2_act(act, l):
            nt, t0 = tiles[l], base_t[l]
            for t in range(nt):
                mixer_done(act, l, t)
                if t == 0 and l == 0:
                    act.wait_ge(gn_tp, 16)
                if t >= 2:
                    act.wait_ge(n2_ss, t0 + t - 1)
                nc.scalar.activation(frow[:, t % 2, :], xin[:, t, :], ACT.Square, accum_out=ss[:, t:t + 1]).then_inc(
                    n2_ss, 1)
            for t in range(nt):
                act.wait_ge(n2_f, t0 + t + 1)
                act.dma_start(f_dram[t * P:(t + 1) * P, :], frow[:, t % 2, :]).then_inc(n2_st[t % 2], 16)
                act.wait_ge(n2_tp, 2 * (t0 + t) + 1)
                nc.scalar.activation(fT[:, t % 2, 0:4, :].rearrange("p k n -> p (k n)"), psum[4][:, :],
                                     ACT.Copy).then_inc(n2_ea, 1)
            act.wait_ge(rt_d1, 2 * l + 1)
            nc.scalar.activation(r_ge[:, 0:nt], r_ge[:, 0:nt], ACT.Exp).then_inc(rt_e1, 1)
            act.wait_ge(rt_d1, 2 * l + 2)
            nc.scalar.activation(r_d[:, 0:nt], r_d[:, 0:nt], ACT.Exp).then_inc(rt_e1, 1)

        def norm2_pe(pe, l):
            nt, t0 = tiles[l], base_t[l]
            if l == 0:
                pe.wait_ge(m1_x, NT)
            else:
                pe.wait_ge(a1_x, 2 * NTL)

            def logits(t):
                pe.wait_ge(n2_in, N2_IN[l])
                pe.wait_ge(n2_ea, t0 + t + 1)
                pe.wait_ge(n2_ed, t0 + t + 1)
                for k in range(KD):
                    mm = nc.tensor.matmul(psum[6][:, t * NR:(t + 1) * NR], lhsT=fT[:, t % 2, k, :], rhs=wrt[:, k, :],
                                          start=(k == 0), stop=(k == KD - 1))
                mm.then_inc(rt_lg, 1)

            for t in range(nt):
                pe.wait_ge(n2_f, t0 + t + 1)
                for half in range(2):
                    if t >= 1:
                        pe.wait_ge((n2_ea, n2_ed)[half], t0 + t)
                    for k in range(4):
                        tp = nc.tensor.transpose(psum[4 + half][:, k * P:(k + 1) * P], frow[:, t % 2, 4 * half + k::KD],
                                                 ident)
                    tp.then_inc(n2_tp, 1)
                if t >= 1:
                    logits(t - 1)
            logits(nt - 1)
            pe.wait_ge(rt_m, l + 1)
            for t in range(nt):
                for u in range(t + 1):
                    c = C_LT if u == t else C_ONE
                    nc.tensor.matmul(psum[7][:, t * E:(t + 1) * E], lhsT=consts[:, c:c + P], rhs=r_m[:, u, :],
                                     start=(u == 0), stop=(u == t))
            for u in range(nt):
                mm = nc.tensor.matmul(psum[7][:, nt * E:(nt + 1) * E], lhsT=consts[:, C_ONE:C_ONE + P],
                                      rhs=r_m[:, u, :], start=(u == 0), stop=(u == nt - 1))
            mm.then_inc(rt_rank, 1)
            nb = E + overflow_blocks(nt * P)
            for i in range(2 * nt):
                pe.wait_ge(rt_qr, 2 * t0 + i + 1)
                mm = nc.tensor.matmul(psum[6][:, 256:256 + nb], lhsT=r_Q[:, i % 2, :], rhs=r_R[:, i % 2, 0:nb],
                                      start=(i == 0), stop=(i == 2 * nt - 1))
                mm.then_inc(rt_tokp, 1)

        def norm2_dve(dve, l):
            nt, t0 = tiles[l], base_t[l]
            ns = (2, 1)[l]
            nov = overflow_blocks(nt * P)
            nb = E + nov
            V = nc.vector
            dve.wait_ge(n2_ss, t0 + nt)
            V.tensor_scalar(ms[:, 0:nt], ss[:, 0:nt], 1.0 / D, EPS, ALU.mult, ALU.add).then_inc(n2_ms, 1)
            dve.wait_ge(n2_in, N2_IN[l])
            for s in range(ns):
                V.scalar_tensor_tensor(mA[:, s, :], mA[:, s, :], 1.0, gain2, ALU.add, ALU.mult).then_inc(n2_A, 1)
            dve.wait_ge(n2_A, (2, 3)[l])
            dve.wait_ge(n2_rstd, l + 1)
            for t in range(nt + 1):
                if t < nt:
                    if t >= 2:
                        dve.wait_ge(n2_st[t % 2], 16 * (base_t[l] // 2 + t // 2))
                        dve.wait_ge(n2_tp, 2 * (t0 + t - 1))
                    fr = frow[:, t % 2, :]
                    link(dve, V.scalar_tensor_tensor(fr, xin[:, t, :], rstd[:, t:t + 1], mA[:, t // 2, :],
                                                     ALU.mult, ALU.mult))
                    V.tensor_tensor(fr, fr, mB[:, t // 2, :], ALU.add).then_inc(n2_f, 1)
                if t >= 1:
                    u = t - 1
                    dve.wait_ge(n2_tp, 2 * (t0 + u) + 2)
                    if u >= 2:
                        dve.wait_ge(rt_lg, t0 + u - 1)
                    V.tensor_copy(fT[:, u % 2, 4:8, :].rearrange("p k n -> p (k n)"), psum[5][:, :]).then_inc(n2_ed, 1)

            T = slice(0, nt)
            V.memset(r_zero, 0.0)
            link(dve, V.memset(r_gp, -3.0e38))
            dve.wait_ge(rt_lg, t0 + nt)
            link(dve, V.tensor_tensor(r_lg[:, T], psum[6][:, 0:nt * NR].rearrange("p (t n) -> p t n", t=nt),
                                      bc(brt, 1, nt), ALU.add))
            link(dve, V.tensor_copy(r_gp[:, T, 0:EG], r_lg[:, T, 0:EG]))
            for t in range(nt):
                ins = V.max(r_gm[:, t], r_gp[:, t])
            link(dve, ins)
            for t in range(nt):
                ins = V.max_index(r_gi[:, t], r_gm[:, t], r_gp[:, t])
            link(dve, ins)
            V.tensor_tensor(r_ge[:, T], r_lg[:, T, 0:EG], r_gm[:, T, 0:1].to_broadcast([P, nt, EG]),
                            ALU.subtract).then_inc(rt_d1, 1)
            link(dve, V.tensor_copy(r_gf[:, T], r_gi[:, T, 0]))
            link(dve, V.tensor_tensor(r_g1[:, T], bc(consts[:, C_E:C_E + EG], 1, nt), bc(r_gf[:, T], 2, EG),
                                      ALU.is_equal))
            link(dve, V.tensor_tensor(r_tmp2[:, T], r_lg[:, T, EG:].rearrange("p t (g n) -> p t g n", g=EG),
                                      bc(r_g1[:, T], 3, EPG), ALU.mult))
            link(dve, V.tensor_reduce(r_es[:, T], r_tmp2[:, T].rearrange("p t g n -> p t n g"), AX, ALU.add))
            for t in range(nt):
                ins = V.max(r_em[:, t], r_es[:, t])
            link(dve, ins)
            for t in range(nt):
                ins = V.max_index(r_ei[:, t], r_em[:, t], r_es[:, t])
            link(dve, ins)
            V.tensor_tensor(r_d[:, T], r_em[:, T, 1], r_em[:, T, 0], ALU.subtract).then_inc(rt_d1, 1)
            link(dve, V.tensor_copy(r_ef[:, T], r_ei[:, T, 0:2]))
            for k in range(2):
                ins = V.scalar_tensor_tensor(r_pos[:, k, T], r_gf[:, T], float(EPG), r_ef[:, T, k], ALU.mult, ALU.add)
            link(dve, ins)
            for k in range(2):
                ins = V.tensor_tensor(r_one[:, k, T], bc(consts[:, C_E:C_E + E], 1, nt), bc(r_pos[:, k, T], 2, E),
                                      ALU.is_equal)
            link(dve, ins)
            V.tensor_tensor(r_m[:, T], r_one[:, 0, T], r_one[:, 1, T], ALU.add).then_inc(rt_m, 1)
            dve.wait_ge(rt_e1, 2 * l + 2)
            link(dve, V.tensor_reduce(r_gs[:, T], r_ge[:, T], AX, ALU.add))
            link(dve, V.scalar_tensor_tensor(r_gs[:, T], r_d[:, T], 1.0, r_gs[:, T], ALU.add, ALU.mult))
            link(dve, V.reciprocal(r_w[:, 0, T], r_gs[:, T]))
            link(dve, V.tensor_tensor(r_w[:, 1, T], r_w[:, 0, T], r_d[:, T], ALU.mult))
            dve.wait_ge(rt_rank, l + 1)
            cnt = psum[7][:, nt * E:(nt + 1) * E]
            link(dve, V.tensor_scalar(r_ov, cnt, float(P), None, ALU.is_gt))
            for c in range(2, nt):
                link(dve, V.scalar_tensor_tensor(r_ov, cnt, float(c * P), r_ov, ALU.is_gt, ALU.add))
            link(dve, V.tensor_tensor_scan(r_ovc, r_ov, r_zero, 0.0, ALU.add, ALU.add))
            link(dve, V.tensor_copy(r_r[:, T], psum[7][:, 0:nt * E].rearrange("p (t n) -> p t n", t=nt)))
            link(dve, V.tensor_tensor(r_b1, r_ovc, r_ov, ALU.subtract))
            link(dve, V.tensor_scalar(r_b1, r_b1, float(P), float((E - 1) * P), ALU.mult, ALU.add))
            link(dve, V.tensor_tensor(r_b1, r_b1, consts[:, C_B0:C_B0 + E], ALU.subtract))
            link(dve, V.tensor_scalar(r_q[:, T], r_r[:, T], float(P), None, ALU.is_ge))
            link(dve, V.tensor_tensor(r_q[:, T], r_q[:, T], bc(r_b1, 1, nt), ALU.mult))
            link(dve, V.tensor_tensor(r_r[:, T], r_r[:, T], bc(consts[:, C_B0:C_B0 + E], 1, nt), ALU.add))
            link(dve, V.tensor_tensor(r_r[:, T], r_r[:, T], r_q[:, T], ALU.add))
            for k in range(2):
                link(dve, V.tensor_tensor(r_tmp[:, T], r_one[:, k, T], r_r[:, T], ALU.mult))
                link(dve, V.tensor_reduce(r_slot[:, k, T], r_tmp[:, T], AX, ALU.add))
            link(dve, V.tensor_copy(r_sloti[:, :, T], r_slot[:, :, T]))
            link(dve, V.tensor_scalar(r_posi[:, :, T], r_sloti[:, :, T], P - 1, None, ALU.bitwise_and))
            link(dve, V.tensor_copy(r_pos[:, :, T], r_posi[:, :, T]))
            link(dve, V.tensor_tensor(r_blk[:, :, T], r_slot[:, :, T], r_pos[:, :, T], ALU.subtract))
            link(dve, V.tensor_scalar(r_blk[:, :, T], r_blk[:, :, T], 1.0 / P, None, ALU.mult))
            for i in range(2 * nt):
                k, t = divmod(i, nt)
                if i >= 2:
                    dve.wait_ge(rt_tokp, 2 * t0 + i - 1)
                V.tensor_scalar(r_Q[:, i % 2, :], consts[:, C_IOTA:C_IOTA + P], r_pos[:, k, t:t + 1], None,
                                ALU.is_equal)
                V.tensor_scalar(r_R[:, i % 2, 0:nb], consts[:, C_IOTA:C_IOTA + nb], r_blk[:, k, t:t + 1],
                                consts[:, C_TOK + t:C_TOK + t + 1], ALU.is_equal, ALU.mult).then_inc(rt_qr, 1)
            for m in range(nov):
                link(dve, V.tensor_scalar(r_tmp[0:1, 0, :], r_ovc[0:1, :], float(m), None, ALU.is_le))
                link(dve, V.tensor_reduce(r_ove[0:1, m:m + 1], r_tmp[0:1, 0, :], AX, ALU.add))
            link(dve, V.tensor_scalar(r_ove[0:1, 0:nov], r_ove[0:1, 0:nov], float(E - 1), None, ALU.min))
            V.tensor_copy(r_ovi[0:1, 0:nov], r_ove[0:1, 0:nov])
            V.tensor_copy(r_ovi[0:1, NOVM:NOVM + 1], r_ovc[0:1, E - 1:E])
            dve.wait_ge(rt_tokp, 2 * (t0 + nt))
            V.tensor_copy(r_tok[:, 0:nb], psum[6][:, 256:256 + nb]).then_inc(rt_slot, 1)

        ys_dram = [dram(f"ys_dram{l}", [(E + overflow_blocks(tiles[l] * P)) * P, D]) for l in range(2)]
        xg = region(A_WORK, 2048, "p (b d) -> p b d", b=2)
        xgT = region(A_WORK + 2048, 2048, "p (b k n) -> p b k n", b=2, k=KD)
        yb = region(A_WORK + 4096, 2048, "p (b d) -> p b d", b=2)
        sil = region(A_WORK + 6144, F)
        hid = region(A_WORK + 6656, F)
        hT = region(A_WORK + 7168, 1024, "p (b k n) -> p b k n", b=2, k=F // P)
        KF = F // P
        moe_xg = [sem(f"moe_xg{i}") for i in range(2)]
        moe_xT = sem("moe_xT")
        moe_xa = sem("moe_xa")
        moe_xd = sem("moe_xd")
        moe_sil = sem("moe_sil")
        moe_h = sem("moe_h")
        moe_hT = sem("moe_hT")
        moe_hc = sem("moe_hc")
        moe_ya = sem("moe_ya")
        moe_yd = sem("moe_yd")
        moe_ys = [sem(f"moe_ys{i}") for i in range(2)]
        ov_step = [sem(f"ov_step{l}") for l in range(2)]
        ov_xg = [sem(f"ov_xg{l}") for l in range(2)]
        ov_w = [sem(f"ov_w{l}") for l in range(2)]
        ov_st = [sem(f"ov_st{l}") for l in range(2)]
        ov_list = sem("ov_list")
        OVN = 11
        moe_out = sem("moe_out")
        cb_in = [sem(f"cb_in{i}") for i in range(2)]
        cb_x = sem("cb_x")
        ys_zero = sem("ys_zero")
        PRE = 3
        LOOP = (E - 1 - PRE) // 2
        assert PRE + 2 * LOOP == E - 1

        def rounds(eng, body):
            for j in range(PRE):
                body(j, j % 2, j // 2, (j + 1) // 2)
            with eng.Fori(0, LOOP) as i:
                for j in (PRE, PRE + 1):
                    body(i * 2 + j, j % 2, i + j // 2, i + (j + 1) // 2)

        def clear_overflow_sp(sp):
            zero = bc(consts[:, C_ZERO:C_ZERO + P], 1, KD)
            sp.wait_ge(s_const, 16)
            for l in range(2):
                for m in range(overflow_blocks(tiles[l] * P)):
                    sp.dma_start(ys_dram[l][(E + m) * P:(E + m + 1) * P, :].rearrange("p (k n) -> p k n", k=KD),
                                 zero).then_inc(ys_zero, 16)

        N_ZERO = 16 * sum(overflow_blocks(n * P) for n in tiles)

        def moe_sp(sp, l):
            n0 = U_MOE[l]
            for n in range(n0, n0 + 2 + 3 * PRE):
                load_unit(sp, n)
            at = n0 + 2 + 3 * PRE
            with sp.Fori(0, LOOP) as i:
                for u in range(6):
                    which, e = moe_unit(at + u - n0)
                    used_sem, v = used(at + u - 6)
                    sp.wait_ge(used_sem, i * 2 + v)
                    w = a[("moe_w_gate", "moe_w_up", "moe_w_down")[which]]
                    k = (KD, KD, KF)[which]
                    src = w[l, bass.ds(i * 2 + e, 1)].rearrange("e (p k) n -> (e p) k n", k=k)
                    sp.dma_start(unit(at + u, k=k), src).then_inc(ring_in[slot_of(at + u)], 16)
            load_unit(sp, n0 + 3 * E - 1)
            sp.wait_ge(moe_down, E * l + E)
            n_ov = ov_count(sp, l)
            with sp.If(n_ov > 0):
                with sp.Fori(0, n_ov) as i:
                    e = sp.value_load(r_ovi[0:1, bass.ds(i, 1)], min_val=0, max_val=E - 1)
                    sp.wait_ge(ov_step[l], i * OVN + 1)
                    for which in range(3):
                        w = a[("moe_w_gate", "moe_w_up", "moe_w_down")[which]]
                        k = (KD, KD, KF)[which]
                        src = w[l, bass.ds(e, 1)].rearrange("e (p k) n -> (e p) k n", k=k)
                        sp.dma_start(ov_unit(which), src).then_inc(ov_w[l], 16)

        def ov_unit(which):
            return mem[:, which * SLOT:(which + 1) * SLOT].rearrange("p (k n) -> p k n", k=(KD, KD, KF)[which])

        def ov_count(eng, l):
            eng.wait_ge(rt_slot, l + 1)
            return eng.value_load(r_ovi[0:1, NOVM:NOVM + 1], min_val=0, max_val=overflow_blocks(tiles[l] * P))

        def moe_pool(pool, l):
            nt, t0 = tiles[l], base_t[l]
            pool.wait_ge(rt_slot, l + 1)
            for i in range(2):
                pool.wait_ge(n2_st[i], 16 * ((t0 + nt) // 2))

            def gather(e, i):
                pool.indirect_dma_start(xg[:, i, :], None, f_dram, bass.IndirectOffsetOnAxis(r_tok[:, e:e + 1], 0)
                                        ).then_inc(moe_xg[i], 16)

            for e in range(E):
                if e >= 2:
                    pool.wait_ge(moe_xT, E * l + e - 1)
                gather(e, e % 2)
            n_ov = ov_count(pool, l)
            with pool.If(n_ov > 0):
                with pool.Fori(0, n_ov) as i:
                    pool.wait_ge(ov_step[l], i * OVN + 2)
                    pool.sem_inc(ov_list, 1)
                    pool.indirect_dma_start(xg[:, 0, :], None, f_dram, bass.IndirectOffsetOnAxis(r_ovidx, 0)
                                            ).then_inc(ov_xg[l], 16)
                pool.wait_ge(ov_st[l], n_ov * 16)
            pool.wait_ge(moe_xT, E * l + E)
            for i in range(2):
                pool.wait_ge(moe_ys[i], 8 * E * (l + 1))
            pool.wait_ge(moe_out, l + 1)
            pool.wait_ge(ys_zero, N_ZERO)
            for t in range(nt):
                q = t0 + t
                if t >= 2:
                    pool.wait_ge(cb_x, q - 1)
                for k, buf in enumerate((xg, yb)):
                    pool.indirect_dma_start(buf[:, t % 2, :], None, ys_dram[l],
                                            bass.IndirectOffsetOnAxis(r_sloti[:, k, t:t + 1], 0)).then_inc(
                        cb_in[t % 2], 16)

        def moe_pe(pe, l):
            n0 = U_MOE[l]

            def ring(n, i):
                pe.wait_ge(ring_in[slot_of(n)], 16 * use_of[n] if i is None else (i + use_of[n]) * 16)

            def x_side(b, p, hb, n, i=None):
                pe.wait_ge(moe_xg[p], (hb + (E // 2 * l + 1)) * 16)
                if not (isinstance(b, int) and b == 0):
                    pe.wait_ge(moe_xa, E * l + b)
                    pe.wait_ge(moe_xd, E * l + b)
                if not (isinstance(b, int) and b < 2):
                    pe.wait_ge(moe_hc, E * l + b - 1)
                for k in range(KD):
                    tp = nc.tensor.transpose(psum[6 + k // 4][:, (k % 4) * P:(k % 4 + 1) * P], xg[:, p, k::KD], ident)
                tp.then_inc(moe_xT, 1)
                pe.wait_ge(moe_xa, E * l + b + 1)
                pe.wait_ge(moe_xd, E * l + b + 1)
                if not (isinstance(b, int) and b < 2):
                    pe.wait_ge(moe_h, E * l + b - 1)
                for which, done in enumerate((moe_gate, moe_up)):
                    ring(n + which, i)
                    w = unit(n + which)
                    for k in range(KD):
                        mm = nc.tensor.matmul(psum[2 * p + which][:, :], lhsT=xgT[:, p, k, :], rhs=w[:, k, :],
                                              start=(k == 0), stop=(k == KD - 1))
                    mm.then_inc(done, 1)

            def h_side(j, p, n, i=None):
                pe.wait_ge(moe_h, E * l + j + 1)
                for k in range(KF):
                    tp = nc.tensor.transpose(psum[6][:, k * P:(k + 1) * P], hid[:, k::KF], ident)
                tp.then_inc(moe_hT, 1)
                ring(n, i)
                pe.wait_ge(moe_hc, E * l + j + 1)
                if not (isinstance(j, int) and j == 0):
                    pe.wait_ge(moe_ya, E * l + j)
                    pe.wait_ge(moe_yd, E * l + j)
                w = unit(n, k=KF)
                for half in range(2):
                    for k in range(KF):
                        mm = nc.tensor.matmul(psum[4 + half][:, :], lhsT=hT[:, p, k, :],
                                              rhs=w[:, k, half * COLS:(half + 1) * COLS], start=(k == 0), stop=(k == KF - 1))
                mm.then_inc(moe_down, 1)

            x_side(0, 0, 0, n0)
            for j in range(PRE):
                x_side(j + 1, (j + 1) % 2, (j + 1) // 2, n0 + 2 + 3 * j)
                h_side(j, j % 2, n0 + 4 + 3 * j)
            with pe.Fori(0, LOOP) as i:
                for j in (PRE, PRE + 1):
                    x_side(i * 2 + j + 1, (j + 1) % 2, i + (j + 1) // 2, n0 + 2 + 3 * j, i)
                    h_side(i * 2 + j, j % 2, n0 + 4 + 3 * j, i)
            h_side(E - 1, (E - 1) % 2, n0 + 3 * E - 1)
            n_ov = ov_count(pe, l)
            with pe.If(n_ov > 0):
                with pe.Fori(0, n_ov) as i:
                    pe.wait_ge(ov_xg[l], (i + 1) * 16)
                    for k in range(KD):
                        tp = nc.tensor.transpose(psum[6 + k // 4][:, (k % 4) * P:(k % 4 + 1) * P], xg[:, 0, k::KD], ident)
                    tp.then_inc(ov_step[l], 1)
                    pe.wait_ge(ov_step[l], i * OVN + 4)
                    pe.wait_ge(ov_w[l], (i + 1) * 48)
                    for which in range(2):
                        for k in range(KD):
                            mm = nc.tensor.matmul(psum[which][:, :], lhsT=xgT[:, 0, k, :], rhs=ov_unit(which)[:, k, :],
                                                  start=(k == 0), stop=(k == KD - 1))
                    mm.then_inc(ov_step[l], 1)
                    pe.wait_ge(ov_step[l], i * OVN + 7)
                    for k in range(KF):
                        tp = nc.tensor.transpose(psum[6][:, k * P:(k + 1) * P], hid[:, k::KF], ident)
                    tp.then_inc(ov_step[l], 1)
                    pe.wait_ge(ov_step[l], i * OVN + 9)
                    for half in range(2):
                        for k in range(KF):
                            mm = nc.tensor.matmul(psum[4 + half][:, :], lhsT=hT[:, 0, k, :],
                                                  rhs=ov_unit(2)[:, k, half * COLS:(half + 1) * COLS],
                                                  start=(k == 0), stop=(k == KF - 1))
                    mm.then_inc(ov_step[l], 1)

        def moe_act(act, l):
            def x_evac(b, p):
                act.wait_ge(moe_xT, E * l + b + 1)
                nc.scalar.activation(xgT[:, p, 0:4, :].rearrange("p k n -> p (k n)"), psum[6][:, :],
                                     ACT.Copy).then_inc(moe_xa, 1)

            def silu(b, p):
                act.wait_ge(moe_gate, E * l + b + 1)
                if not (isinstance(b, int) and b == 0):
                    act.wait_ge(moe_h, E * l + b)
                nc.scalar.activation(sil, psum[2 * p][:, :], ACT.Silu).then_inc(moe_sil, 1)

            def out(j, p, hj, static):
                act.wait_ge(moe_hT, E * l + j + 1)
                nc.scalar.activation(hT[:, p].rearrange("p k n -> p (k n)"), psum[6][:, :], ACT.Copy).then_inc(
                    moe_hc, 1)
                act.wait_ge(moe_down, E * l + j + 1)
                if not (isinstance(j, int) and j < 2):
                    act.wait_ge(moe_ys[p], (hj + E // 2 * l) * 16)
                nc.scalar.activation(yb[:, p, 0:COLS], psum[4][:, :], ACT.Copy).then_inc(moe_ya, 1)
                act.wait_ge(moe_ya, E * l + j + 1)
                act.wait_ge(moe_yd, E * l + j + 1)
                dst = ys_dram[l].rearrange("(b p) d -> b p d", p=P)
                dst = dst[j] if isinstance(j, int) else dst[bass.ds(j, 1)].rearrange("b p d -> (b p) d")
                act.dma_start(dst, yb[:, p, :]).then_inc(moe_ys[p], 16)

            def body(j, p, hj, hb):
                x_evac(j + 1, 1 - p)
                silu(j + 1, 1 - p)
                out(j, p, hj, None)

            x_evac(0, 0)
            silu(0, 0)
            rounds(act, body)
            out(E - 1, (E - 1) % 2, (E - 1) // 2, None)
            act.nop().then_inc(ov_step[l], 1)
            n_ov = ov_count(act, l)
            with act.If(n_ov > 0):
                act.wait_ge(ys_zero, N_ZERO)
                for i in range(2):
                    act.wait_ge(moe_ys[i], 8 * E * (l + 1))
                with act.Fori(0, n_ov) as i:
                    act.wait_ge(ov_step[l], i * OVN + 3)
                    for half in range(2):
                        ev = nc.scalar.activation(xgT[:, 0, 4 * half:4 * half + 4, :].rearrange("p k n -> p (k n)"),
                                                  psum[6 + half][:, :], ACT.Copy)
                    ev.then_inc(ov_step[l], 1)
                    act.wait_ge(ov_step[l], i * OVN + 5)
                    nc.scalar.activation(sil, psum[0][:, :], ACT.Silu).then_inc(ov_step[l], 1)
                    act.wait_ge(ov_step[l], i * OVN + 8)
                    nc.scalar.activation(hT[:, 0].rearrange("p k n -> p (k n)"), psum[6][:, :], ACT.Copy).then_inc(
                        ov_step[l], 1)
                    act.wait_ge(ov_step[l], i * OVN + 10)
                    for half in range(2):
                        ev = nc.scalar.activation(yb[:, 0, half * COLS:(half + 1) * COLS], psum[4 + half][:, :], ACT.Copy)
                    ev.then_inc(ov_step[l], 1)
                    act.wait_ge(ov_step[l], i * OVN + 11)
                    dst = ys_dram[l].rearrange("(b p) d -> b p d", p=P)[bass.ds(i + E, 1)].rearrange("b p d -> (b p) d")
                    act.dma_start(dst, yb[:, 0, :]).then_inc(ov_st[l], 16)
                    act.wait_ge(ov_st[l], (i + 1) * 16)
                    act.nop().then_inc(ov_step[l], 1)
            act.nop().then_inc(moe_out, 1)

        def moe_dve(dve, l):
            def x_evac(b, p):
                dve.wait_ge(moe_xT, E * l + b + 1)
                nc.vector.tensor_copy(xgT[:, p, 4:8, :].rearrange("p k n -> p (k n)"), psum[7][:, :]).then_inc(
                    moe_xd, 1)

            def mul(b, p):
                dve.wait_ge(moe_sil, E * l + b + 1)
                dve.wait_ge(moe_up, E * l + b + 1)
                if not (isinstance(b, int) and b == 0):
                    dve.wait_ge(moe_hT, E * l + b)
                nc.vector.tensor_tensor(hid, sil, psum[2 * p + 1][:, :], ALU.mult).then_inc(moe_h, 1)

            def out(j, p, hj):
                dve.wait_ge(moe_down, E * l + j + 1)
                if not (isinstance(j, int) and j < 2):
                    dve.wait_ge(moe_ys[p], (hj + E // 2 * l) * 16)
                nc.vector.tensor_copy(yb[:, p, COLS:], psum[5][:, :]).then_inc(moe_yd, 1)

            def body(j, p, hj, hb):
                x_evac(j + 1, 1 - p)
                mul(j + 1, 1 - p)
                out(j, p, hj)

            x_evac(0, 0)
            mul(0, 0)
            rounds(dve, body)
            out(E - 1, (E - 1) % 2, (E - 1) // 2)
            n_ov = ov_count(dve, l)
            with dve.If(n_ov > 0):
                with dve.Fori(0, n_ov) as i:
                    dve.wait_ge(ov_step[l], i * OVN + 1)
                    nc.vector.tensor_copy(r_ovidx, r_tok[:, bass.ds(i + E, 1)]).then_inc(ov_step[l], 1)
                    dve.wait_ge(ov_step[l], i * OVN + 6)
                    nc.vector.tensor_tensor(hid, sil, psum[1][:, :], ALU.mult).then_inc(ov_step[l], 1)
            nt, t0 = tiles[l], base_t[l]
            dve.wait_ge(n2_g2, (16 * 2, 16 * 3)[l])
            for t in range(nt):
                b = t % 2
                dve.wait_ge(cb_in[b], 32 * (t0 // 2 + t // 2 + 1))
                link(dve, nc.vector.tensor_scalar(xg[:, b], xg[:, b], r_w[:, 0, t:t + 1], None, ALU.mult))
                link(dve, nc.vector.scalar_tensor_tensor(xg[:, b], yb[:, b], r_w[:, 1, t:t + 1], xg[:, b],
                                                         ALU.mult, ALU.add))
                link(dve, nc.vector.tensor_tensor(xg[:, b], xg[:, b], gate2[:, t // 2], ALU.mult))
                nc.vector.tensor_tensor(xin[:, t], xin[:, t], xg[:, b], ALU.add).then_inc(cb_x, 1)

        A1 = M0
        gate1a = region(A1, D)
        at_small = [A1 + D]

        def attn_tile(size, pattern=None, **dims):
            v = region(at_small[0], size, pattern, **dims)
            at_small[0] += size
            assert at_small[0] <= A1 + 2 * D
            return v

        rope = attn_tile(2 * NTL * 32, "p (w t n) -> p w t n", w=2, t=NTL)
        qgain = attn_tile(HD)
        kgain = attn_tile(HD)
        NQ, NK = NTL * QH, NT * KVH
        qk_ss = attn_tile(NQ + NK)
        qk_ms = attn_tile(NQ + NK)
        qk_rs = attn_tile(NQ + NK)
        qk_half = attn_tile(NQ + NK)
        amax = attn_tile(32)
        abias = attn_tile(32)
        asum = attn_tile(32)
        ainv = attn_tile(32)
        rtmp = [region(A1 + 2048 + 1024 * i, 1024) for i in range(4)]
        qrow = region(A_WORK, 2048, "p (t n) -> p t n", t=NTL)
        kv = region(A_WORK + 2048, 2048, "p (t n) -> p t n", t=NT)
        kdup = region(A_WORK + 4096, 2048, "p (t j c n) -> p t j c n", t=NT, j=KVH, c=2)
        prob = region(A_WORK + 6144, 1024, "p (b n) -> p b n", b=2)
        probT = region(A_WORK + 7168, 1024, "p (b k n) -> p b k n", b=2, k=NT)
        orow = region(A1 + 6144, 2048, "p (t n) -> p t n", t=NTL)
        oT = region(A1 + 8192, 2048, "p (k n) -> p k n", k=KD)
        qT = region(A1 + 10240, 2048, "p (r n) -> p r n", r=QH // 2)
        kT = region(A1 + 12288, 2048, "p (j n) -> p j n", j=KVH)
        SCALE = HD ** -0.5
        at_in = sem("at_in")
        at_qe = sem("at_qe")
        at_ke = sem("at_ke")
        at_ms = sem("at_ms")
        at_rs = sem("at_rs")
        at_q = sem("at_q")
        at_k = sem("at_k")
        at_kd = sem("at_kd")
        at_tp = sem("at_tp")
        at_te = sem("at_te")
        at_s = sem("at_s")
        at_m = sem("at_m")
        at_p = sem("at_p")
        at_pt = sem("at_pt")
        at_pe = sem("at_pe")
        at_pv = sem("at_pv")
        at_o = sem("at_o")
        at_otp = sem("at_otp")
        at_oe = sem("at_oe")
        a1_x = sem("a1_x")
        AI = [(t, h) for t in range(NTL) for h in range(QH)]

        def attn_pool(pool):
            pool.wait_ge(cb_x, NT)
            pool.dma_start(gate1a, mod_dram[1, 0:1, 2 * D:3 * D].to_broadcast([P, D])).then_inc(at_in, 16)
            pool.dma_start(rope, a["rope"]).then_inc(at_in, 16)
            pool.dma_start(qgain, a["att_q_gain"][0:1, :].to_broadcast([P, HD])).then_inc(at_in, 16)
            pool.dma_start(kgain, a["att_k_gain"][0:1, :].to_broadcast([P, HD])).then_inc(at_in, 16)
            pool.wait_ge(at_ms, 1)
            nc.gpsimd.tensor_tensor(qk_rs, qk_ms, qk_half, ALU.pow).then_inc(at_rs, 1)

        def attn_pe(pe):
            pe.wait_ge(n1_ea, 8)
            pe.wait_ge(n1_ed, 8)
            for u in range(3):
                unit_wait(pe, U_QKV + u)
                w = unit(U_QKV + u)
                for t in range(NTL if u < 2 else NT):
                    for k in range(KD):
                        mm = nc.tensor.matmul(psum[2 * u + t][:, :], lhsT=aT[1][:, k, t * P:(t + 1) * P], rhs=w[:, k, :],
                                              start=(k == 0), stop=(k == KD - 1))
                    mm.then_inc(qkv_mm, 1)
            pe.wait_ge(at_qe, 4)
            pe.wait_ge(at_kd, 2)
            for i in range(8):
                if i == 4:
                    pe.wait_ge(at_q, 1)
                if i >= 2:
                    pe.wait_ge(at_te, i - 1)
                for r in range(4):
                    if i < 4:
                        src = kdup[:, r, i].rearrange("p c n -> p (c n)")
                    else:
                        pair, t = 2 * (i - 4) + r // 2, r % 2
                        src = qrow[:, t, pair * P:(pair + 1) * P]
                    tp = nc.tensor.transpose(psum[6 + i % 2][:, r * P:(r + 1) * P], src, ident)
                tp.then_inc(at_tp, 1)
            pe.wait_ge(at_te, 8)

            def scores(i):
                t, h = AI[i]
                lo = HD * (h % 2)
                if i >= 2:
                    pe.wait_ge(at_p, i - 1)
                nc.tensor.matmul(psum[i % 2][:, :], lhsT=qT[lo:lo + HD, h // 2, t * P:(t + 1) * P],
                                 rhs=kT[lo:lo + HD, h // 4, :], start=True, stop=True).then_inc(at_s, 1)

            def turn(i):
                pe.wait_ge(at_p, i + 1)
                if i >= 2:
                    pe.wait_ge(at_pe, i - 1)
                for k in range(NT):
                    tp = nc.tensor.transpose(psum[2 + i % 2][:, k * P:(k + 1) * P], prob[:, i % 2, k * P:(k + 1) * P], ident)
                tp.then_inc(at_pt, 1)

            def values(i):
                t, h = AI[i]
                pe.wait_ge(at_pe, i + 1)
                if i >= 16 and i % 8 == 0:
                    pe.wait_ge(at_o, i // 8 - 1)
                c = HD * (h % 8)
                v = (KVH + h // 4) * HD
                for k in range(NT):
                    mm = nc.tensor.matmul(psum[4 + i // 8 % 2][:, c:c + HD], lhsT=probT[:, i % 2, k, :],
                                          rhs=kv[:, k, v:v + HD], start=(k == 0), stop=(k == NT - 1))
                mm.then_inc(at_pv, 1)

            scores(0)
            for i in range(len(AI) + 1):
                if i + 1 < len(AI):
                    scores(i + 1)
                if i < len(AI):
                    turn(i)
                if i >= 1:
                    values(i - 1)
            pe.wait_ge(at_o, 4)
            for i in range(4):
                if i >= 2:
                    pe.wait_ge(at_oe, i - 1)
                for r in range(4):
                    k, t = 2 * i + r // 2, r % 2
                    tp = nc.tensor.transpose(psum[6 + i % 2][:, r * P:(r + 1) * P], orow[:, t, k::KD], ident)
                tp.then_inc(at_otp, 1)
            pe.wait_ge(at_oe, 4)
            pe.wait_ge(at_p, len(AI))
            for u in range(2):
                unit_wait(pe, U_WO + u)
                w = unit(U_WO + u)
                for t in range(NTL):
                    for k in range(KD):
                        mm = nc.tensor.matmul(psum[2 * u + t][:, :], lhsT=oT[:, k, t * P:(t + 1) * P], rhs=w[:, k, :],
                                              start=(k == 0), stop=(k == KD - 1))
                    mm.then_inc(wo_mm, 1)

        def attn_act(act):
            for i in range(4):
                act.wait_ge(qkv_mm, i + 1)
                u, t = divmod(i, 2)
                nc.scalar.activation(qrow[:, t, u * COLS:(u + 1) * COLS], psum[i][:, :], ACT.Copy).then_inc(at_qe, 1)
            act.wait_ge(at_k, 1)
            for c in range(2):
                nc.scalar.activation(kdup[:, :, :, c, :],
                                     kv[:, :, 0:KVH * HD].rearrange("p t (j n) -> p t j n", j=KVH),
                                     ACT.Copy).then_inc(at_kd, 1)
            for i in range(8):
                act.wait_ge(at_tp, i + 1)
                to = kT[:, i, :] if i < 4 else qT[:, 2 * (i - 4):2 * (i - 4) + 2, :].rearrange("p r n -> p (r n)")
                nc.scalar.activation(to, psum[6 + i % 2][:, :], ACT.Copy).then_inc(at_te, 1)
            for i in range(len(AI)):
                act.wait_ge(at_m, i + 1)
                if i >= 2:
                    act.wait_ge(at_pt, i - 1)
                nc.scalar.activation(prob[:, i % 2, :], psum[i % 2][:, :], ACT.Exp, bias=abias[:, i:i + 1], scale=SCALE,
                                     accum_out=asum[:, i:i + 1]).then_inc(at_p, 1)
            for i in range(4):
                act.wait_ge(at_otp, i + 1)
                nc.scalar.activation(oT[:, 2 * i:2 * i + 2, :].rearrange("p k n -> p (k n)"), psum[6 + i % 2][:, :],
                                     ACT.Copy).then_inc(at_oe, 1)

        def attn_dve(dve):
            V = nc.vector
            for t in range(NT):
                dve.wait_ge(qkv_mm, 5 + t)
                V.tensor_copy(kv[:, t, :], psum[4 + t][:, :]).then_inc(at_ke, 1)
            dve.wait_ge(at_ke, NT)
            V.memset(qk_half, -0.5)
            k4 = kv[:, :, 0:KVH * HD].rearrange("p t (j n) -> p t j n", j=KVH)
            q3 = qrow.rearrange("p t (h n) -> p (t h) n", n=HD)
            ksq = rtmp[2].rearrange("p (t j n) -> p t j n", t=NT, j=KVH)
            qsq = region(A1 + 2048, 2048, "p (h n) -> p h n", n=HD)
            link(dve, V.tensor_tensor(ksq, k4, k4, ALU.mult))
            V.tensor_reduce(qk_ss[:, NQ:], ksq.rearrange("p t j n -> p (t j) n"), AX, ALU.add)
            dve.wait_ge(at_qe, 4)
            link(dve, V.tensor_tensor(qsq, q3, q3, ALU.mult))
            link(dve, V.tensor_reduce(qk_ss[:, 0:NQ], qsq, AX, ALU.add))
            V.tensor_scalar(qk_ms, qk_ss, 1.0 / HD, EPS, ALU.mult, ALU.add).then_inc(at_ms, 1)
            dve.wait_ge(at_in, 64)
            dve.wait_ge(at_rs, 1)
            cos, sin = rope[:, 0], rope[:, 1]

            def turn_pairs(x, heads, tmp):
                n = NTL * heads * HD // 2
                T = [v[:, 0:n].rearrange("p (t h n) -> p t h n", t=NTL, h=heads) for v in tmp]
                c, s = bc(cos, 2, heads), bc(sin, 2, heads)
                V.tensor_tensor(T[0], x[:, :, :, 0::2], c, ALU.mult)
                V.tensor_tensor(T[1], x[:, :, :, 1::2], s, ALU.mult)
                V.tensor_tensor(T[2], x[:, :, :, 0::2], s, ALU.mult)
                link(dve, V.tensor_tensor(T[3], x[:, :, :, 1::2], c, ALU.mult))
                V.tensor_tensor(x[:, :, :, 0::2], T[0], T[1], ALU.subtract)
                return V.tensor_tensor(x[:, :, :, 1::2], T[2], T[3], ALU.add)

            for t in range(NT):
                ins = V.tensor_tensor(k4[:, t], k4[:, t], bc(qk_rs[:, NQ + KVH * t:NQ + KVH * (t + 1)], 2, HD), ALU.mult)
            link(dve, ins)
            for t in range(NT):
                ins = V.tensor_tensor(k4[:, t], k4[:, t], bc(kgain, 1, KVH), ALU.mult)
            link(dve, ins)
            turn_pairs(k4[:, 0:NTL], KVH, rtmp).then_inc(at_k, 1)
            dve.wait_ge(at_k, 1)
            link(dve, V.tensor_tensor(q3, q3, bc(qk_rs[:, 0:NQ], 2, HD), ALU.mult))
            link(dve, V.tensor_tensor(q3, q3, bc(qgain, 1, NQ), ALU.mult))
            turn_pairs(qrow.rearrange("p t (h n) -> p t h n", n=HD), QH, rtmp).then_inc(at_q, 1)

            def evac(i):
                dve.wait_ge(at_pt, i + 1)
                if i >= 2:
                    dve.wait_ge(at_pv, i - 1)
                V.tensor_copy(probT[:, i % 2].rearrange("p k n -> p (k n)"), psum[2 + i % 2][:, :]).then_inc(at_pe, 1)

            def output(q):
                dve.wait_ge(at_pv, 8 * q + 8)
                dve.wait_ge(at_p, 8 * q + 8)
                link(dve, V.reciprocal(ainv[:, 8 * q:8 * q + 8], asum[:, 8 * q:8 * q + 8]))
                t, hh = divmod(q, 2)
                V.tensor_tensor(orow[:, t, hh * COLS:(hh + 1) * COLS].rearrange("p (h n) -> p h n", h=8),
                                psum[4 + q % 2][:, :].rearrange("p (h n) -> p h n", h=8),
                                bc(ainv[:, 8 * q:8 * q + 8], 2, HD), ALU.mult).then_inc(at_o, 1)

            for i in range(len(AI) + 1):
                if i < len(AI):
                    dve.wait_ge(at_s, i + 1)
                    link(dve, V.tensor_reduce(amax[:, i:i + 1], psum[i % 2][:, :], AX, ALU.max))
                    V.tensor_scalar(abias[:, i:i + 1], amax[:, i:i + 1], -SCALE, None, ALU.mult).then_inc(at_m, 1)
                if i >= 1:
                    evac(i - 1)
                if i >= 10 and i % 8 == 2:
                    output(i // 8 - 1)
            output(3)
            for i in range(2 * NTL):
                u, t = divmod(i, NTL)
                cs = slice(u * COLS, (u + 1) * COLS)
                dve.wait_ge(wo_mm, i + 1)
                tmp = region(A_WORK + i % 2 * COLS, COLS)
                link(dve, V.tensor_tensor(tmp, psum[2 * u + t][:, :], gate1a[:, cs], ALU.mult))
                V.tensor_tensor(xin[:, t, cs], xin[:, t, cs], tmp, ALU.add).then_inc(a1_x, 1)

        out_st = sem("out_st")
        block = ctx.enter_context(nc.Block())

        @block.vector
        def _(dve):
            nc.vector.memset(mhalf[:, :], -0.5).then_inc(s_init, 1)
            norm1_scale_dve(dve, 0)
            mod_dve(dve, 0)
            norm1_dve(dve, 0)
            conv_dve(dve)
            dt_dve(dve)
            mod_dve(dve, 1)
            decay_dve(dve)
            mod_wait(dve, 1, MODU)
            scan_dve(dve)
            finish_dve(dve)
            norm2_dve(dve, 0)
            moe_dve(dve, 0)
            norm1_scale_dve(dve, 1)
            norm1_dve(dve, 1)
            attn_dve(dve)
            norm2_dve(dve, 1)
            moe_dve(dve, 1)

        @block.sync
        def _(sp):
            sp.dma_start(consts[:, :], a["consts"]).then_inc(s_const, 16)
            sp.dma_start(craw[:, 0, :], a["c"][0].rearrange("(p k) -> p k", k=KD)).then_inc(s_c, 16)
            sp.dma_start(craw[:, 1, :], a["c_ctx"].rearrange("(p k) -> p k", k=KD)).then_inc(s_c, 16)
            for n in range(U_MOE[0]):
                load_unit(sp, n)
                if n == U_MOD[1] + MODU - 1:
                    clear_overflow_sp(sp)
            moe_sp(sp, 0)
            for n in range(U_QKV, U_MOE[1]):
                load_unit(sp, n)
            moe_sp(sp, 1)
            for t in range(NTL):
                sp.wait_ge(cb_x, NT + t + 1)
                sp.dma_start(out[0, t * P:(t + 1) * P, :], xin[:, t, :]).then_inc(out_st, 16)
            sp.wait_ge(out_st, 16 * NTL)

        @block.gpsimd
        def _(pool):
            pool.dma_start(xin[:, 0:2, :], a["x"][0].rearrange("(t p) d -> p t d", p=P)).then_inc(x_in, 16)
            pool.dma_start(xin[:, 2:4, :], a["ctx"][0].rearrange("(t p) d -> p t d", p=P)).then_inc(x_in, 16)
            pool.dma_start(wdt, a["ssd_w_in"][0, :, DI + XBC:].rearrange("(p k) n -> p k n", k=KD)).then_inc(sw_in, 16)
            pool.dma_start(convw, a["conv_w"]).then_inc(sw_in, 16)
            pool.dma_start(convb, a["conv_b"]).then_inc(sw_in, 16)
            for v, name in ((dtb, "ssd_dt_bias"), (alog, "ssd_a_log")):
                pool.dma_start(v, a[name].rearrange("a d h -> a (d h)").to_broadcast([P, 64])).then_inc(sw_in, 16)
            norm1_rstd_pool(pool, 0)
            norm1_pool(pool, 0)
            scan_pool(pool)
            finish_pool(pool)
            norm2_pool(pool, 0)
            moe_pool(pool, 0)
            norm1_pool(pool, 1)
            norm1_rstd_pool(pool, 1)
            attn_pool(pool)
            norm2_pool(pool, 1)
            moe_pool(pool, 1)

        @block.scalar
        def _(act):
            act.wait_ge(s_c, 32)
            for r in range(2):
                nc.scalar.activation(silu_c[:, :, r], craw[:, r, :], ACT.Silu).then_inc(s_silu_c, 1)
            norm1_square_act(act, 0)
            mod_act(act, 0)
            norm1_act(act, 0)
            conv_act(act)
            dt_act(act)
            mod_act(act, 1)
            decay_act(act)
            scan_act(act)
            finish_act(act)
            norm2_act(act, 0)
            moe_act(act, 0)
            norm1_square_act(act, 1)
            norm1_act(act, 1)
            attn_act(act)
            norm2_act(act, 1)
            moe_act(act, 1)

        @block.tensor
        def _(pe):
            pe.wait_ge(s_const, 16)
            pe.wait_ge(s_silu_c, 2)
            mod_pe(pe, 0)
            norm1_pe(pe, 0)
            conv_pe(pe)
            dt_pe(pe)
            mod_pe(pe, 1)
            decay_pe(pe)
            scan_pe(pe)
            finish_pe(pe)
            norm2_pe(pe, 0)
            moe_pe(pe, 0)
            norm1_pe(pe, 1)
            attn_pe(pe)
            norm2_pe(pe, 1)
            moe_pe(pe, 1)


def kernel(**inputs):
    import concourse.bacc as _bacc
    from concourse.bass_utils import run_bass_kernel_spmd as _run

    host = dict(inputs)
    conv_w, conv_b, norm_g = (host.pop(n) for n in ("ssd_conv_w", "ssd_conv_b", "ssd_norm_g"))
    host["conv_w"] = conv_w[0].T.reshape(NCH, P, TAPS).transpose(1, 0, 2)
    host["conv_b"] = conv_b[0].reshape(NCH, P).T
    host["norm_cols"] = norm_g[0].reshape(DI // P, P).T
    host["consts"] = consts_array()
    host["rope"] = rope_array()
    nc = _bacc.Bacc("TRN2", target_bir_lowering=False, num_devices=1)
    arrays, a = {}, {}
    for name, v in host.items():
        v = np.ascontiguousarray(v)
        arrays[f"in_{name}_dram"] = v
        a[name] = nc.dram_tensor(f"in_{name}_dram", v.shape, mybir.dt.from_np(v.dtype), kind="ExternalInput").ap()
    out = nc.dram_tensor("out_0_dram", (1, SEQ, D), F32, kind="ExternalOutput").ap()
    hybrid_block(nc, a, out)
    r = _run(nc, [arrays], core_ids=[0])
    return r.results[0]["out_0_dram"]
```

```python
from contextlib import ExitStack

import numpy as np
import concourse.bass as bass
from concourse import mybir

ALU = mybir.AluOpType
ACT = mybir.ActivationFunctionType
AX = mybir.AxisListType.X
F32 = mybir.dt.float32
I32 = mybir.dt.int32
U32 = mybir.dt.uint32

P = 128
D = 1024
KD = D // P
SEQ = 256
NT = 2 * SEQ // P
NTL = SEQ // P
EPS = 1e-6
NMOD = 6
SLOT = 4096
COLS = 512
MODU = NMOD * D // COLS

DI = 2048
HEADS, HD, GROUPS, NS = 32, 64, 4, 128
HG = HEADS // GROUPS
TAPS = 5
XBC = DI + 2 * GROUPS * NS
NCH = XBC // P
GW = DI // GROUPS

QH, KVH = 16, 4
E, EG, EPG, F = 32, 4, 8, 512
BR = 64

C_ID, C_LE, C_GT, C_GE, C_LT, C_ONE, C_IOTA = (i * P for i in range(7))
C_TOK = 7 * P
C_SEL = C_TOK + NT
C_E = C_SEL + 2
C_B0 = C_E + E
C_ZERO = C_B0 + E
C_N = C_ZERO + P


def overflow_blocks(tokens):
    return (2 * tokens - 1) // BR


def consts_array():
    k, i = np.meshgrid(np.arange(P), np.arange(P), indexing="ij")
    parts = [k == i, k <= i, k > i, k >= i, k < i, np.ones((P, P)), i]
    tok = np.arange(P)[:, None] + P * np.arange(NT)[None]
    sel = np.stack([np.arange(P) % 32 == r for r in range(2)], 1)
    e = np.broadcast_to(np.arange(E)[None], (P, E))
    return np.concatenate([*parts, tok, sel, e, e * BR, np.zeros((P, P))], 1).astype(np.float32)


def rope_array():
    half = HD // 2
    n = np.arange(SEQ)
    freqs = np.float32(10000.0) ** (-np.arange(0, half, 2, dtype=np.float32) / np.float32(half))
    row, col = (n // 64).astype(np.float32), (n % 64).astype(np.float32)
    ang = np.concatenate([row[:, None] * freqs, col[:, None] * freqs], 1).astype(np.float32)
    t = np.stack([np.cos(ang), np.sin(ang)]).astype(np.float32)
    return np.ascontiguousarray(t.reshape(2, NTL, P, half).transpose(2, 0, 1, 3))


def hybrid_block(nc, a, out):
    ctx = ExitStack()
    with ctx:
        def sem(name):
            return ctx.enter_context(nc.semaphore(name))

        def sb(name, shape, dt=F32):
            return ctx.enter_context(nc.sbuf_tensor(name, shape, dt))

        def dram(name, shape):
            return nc.dram_tensor(name, shape, F32, kind="Internal").ap()

        RING3 = 3 * SLOT
        mem = sb("mem", [P, RING3 + 38912])

        def region(at, size, pattern=None, parts=P, **dims):
            v = mem[0:parts, at:at + size]
            return v.rearrange(pattern, **dims) if pattern else v

        A0 = RING3
        A_XROW, A_AT, A_BCT, A_Y, A_H, A_WORK = A0, A0 + 8192, A0 + 12288, A0 + 18432, A0 + 26624, A0 + 30720

        ring_at = [0, SLOT, 2 * SLOT, A0, A0 + SLOT, A0 + 2 * SLOT]
        consts = sb("consts", [P, C_N])
        smalls = sb("smalls", [P, 512])
        sm_at = [0]

        def small(size, pattern=None, **dims):
            v = smalls[:, sm_at[0]:sm_at[0] + size]
            sm_at[0] += size
            assert sm_at[0] <= 512
            return v.rearrange(pattern, **dims) if pattern else v

        ident = consts[:, C_ID:C_ID + P]
        psum = [ctx.enter_context(nc.psum_tensor(f"bank{i}", [P, COLS], F32)) for i in range(8)]

        mod_dram = dram("mod_dram", [2, 2, NMOD * D])
        f_dram = dram("f_dram", [NT * P, D])

        MOD_FIRST = 4
        early = [("mod", q) for q in range(MOD_FIRST)]
        early_slots = [1, 2, 0, 1]
        for u in range(XBC // COLS):
            mine, other = (0, 2) if u % 2 == 0 else (2, 0)
            at = MOD_FIRST + 4 * u
            early += [("xbc", u)] + [("mod", q) for q in range(at, min(at + 4, 2 * MODU))]
            early_slots += [mine, other, 1, other, 1]
        U_EARLY = {unit: n for n, unit in enumerate(early)}
        U_Z = len(early)
        U_WOUT = U_Z + 4
        U_MOE = [U_WOUT + 4, 0]
        U_QKV = U_MOE[0] + 3 * E
        U_WO = U_QKV + 3
        U_MOE[1] = U_WO + 2
        N_UNITS = U_MOE[1] + 3 * E
        first6 = U_MOE[0]
        order3 = [1, 0, 2]
        order6 = [order3[(first6 - U_Z + j) % 3] for j in range(3)] + [3, 4, 5]

        def slot_of(n):
            if n < U_Z:
                return early_slots[n]
            return order3[(n - U_Z) % 3] if n < first6 else order6[(n - first6) % 6]

        use_of, seen, last_of, holder = [], [0] * 6, [], [None] * 6
        for n in range(N_UNITS):
            s = slot_of(n)
            seen[s] += 1
            use_of.append(seen[s])
            last_of.append(holder[s] if holder[s] is not None else (first6 - 1 if s >= 3 else None))
            holder[s] = n

        ring_in = [sem(f"ring_in{i}") for i in range(6)]
        mod_mm = sem("mod_mm")
        cv_mm = sem("cv_mm")
        z_mm = sem("z_mm")
        wout_mm = sem("wout_mm")
        qkv_mm = sem("qkv_mm")
        wo_mm = sem("wo_mm")
        moe_gate = sem("moe_gate")
        moe_up = sem("moe_up")
        moe_down = sem("moe_down")

        def used(n):
            if n < U_Z:
                kind, m = early[n]
                return (mod_mm, m + 1) if kind == "mod" else (cv_mm, 4 * (m + 1))
            if U_Z <= n < U_WOUT:
                return z_mm, NT * (n - U_Z + 1)
            if U_WOUT <= n < U_MOE[0]:
                return wout_mm, NT * (n - U_WOUT + 1)
            if U_QKV <= n < U_WO:
                return qkv_mm, [2, 4, 8][n - U_QKV]
            if U_WO <= n < U_MOE[1]:
                return wo_mm, NTL * (n - U_WO + 1)
            l = int(n >= U_MOE[1])
            which, b = moe_unit(n - U_MOE[l])
            return (moe_gate, moe_up, moe_down)[which], E * l + b + 1

        def moe_unit(j):
            if j < 2:
                return j, 0
            if j == 3 * E - 1:
                return 2, E - 1
            b, r = divmod(j - 2, 3)
            return (0, b + 1) if r == 0 else (1, b + 1) if r == 1 else (2, b)

        def unit(n, pattern="p (k n) -> p k n", **dims):
            dims = dims or {"k": KD}
            at = ring_at[slot_of(n)]
            return mem[:, at:at + SLOT].rearrange(pattern, **dims)

        def unit_wait(eng, n):
            eng.wait_ge(ring_in[slot_of(n)], 16 * use_of[n])

        def unit_source(n):
            if n < U_Z:
                kind, m = early[n]
                if kind == "mod":
                    l, c = m // MODU, m % MODU * COLS
                    return a["mod_w"][l, :, c:c + COLS].rearrange("(p k) n -> p k n", k=KD)
                c = DI + m * COLS
                return a["ssd_w_in"][0, :, c:c + COLS].rearrange("(p k) n -> p k n", k=KD)
            if n < U_WOUT:
                c = (n - U_Z) * COLS
                return a["ssd_w_in"][0, :, c:c + COLS].rearrange("(p k) n -> p k n", k=KD)
            if n < U_MOE[0]:
                half, part = divmod(n - U_WOUT, 2)
                return a["ssd_w_out"][0, part * 1024:(part + 1) * 1024, half * COLS:(half + 1) * COLS].rearrange(
                    "(c p) n -> p c n", p=P)
            if U_QKV <= n < U_WO:
                c = (n - U_QKV) * COLS
                return a["att_w_qkv"][0, :, c:c + COLS].rearrange("(p k) n -> p k n", k=KD)
            if U_WO <= n < U_MOE[1]:
                c = (n - U_WO) * COLS
                return a["att_w_o"][0, :, c:c + COLS].rearrange("(p k) n -> p k n", k=KD)
            l = int(n >= U_MOE[1])
            return moe_source(l, *moe_unit(n - U_MOE[l]))

        def moe_source(l, which, e):
            w = a[("moe_w_gate", "moe_w_up", "moe_w_down")[which]][l, e]
            return w.rearrange("(k p) n -> p k n", p=P) if which == 2 else w.rearrange("(p k) n -> p k n", k=KD)

        def load_unit(sp, n):
            if last_of[n] is not None:
                sp.wait_ge(*used(last_of[n]))
            src = unit_source(n)
            sp.dma_start(unit(n, k=src.shape[1]), src).then_inc(ring_in[slot_of(n)], 16)

        silu_c = small(16, "p (k r) -> p k r", k=KD)
        craw = small(16, "p (r k) -> p r k", r=2)
        modcol = small(48, "p (s w k) -> p s w k", s=2, w=3)
        gcol = small(8)
        ss = small(4)
        ms = small(4)
        rstd = small(4)
        mhalf = small(4)

        s_const = sem("s_const")
        s_c = sem("s_c")
        s_silu_c = sem("s_silu_c")
        s_init = sem("s_init")
        dve_chain = sem("dve_chain")
        chain = [0]

        def bc(v, axis, n):
            v = v.unsqueeze(axis)
            return v.to_broadcast([n if i == axis else m for i, m in enumerate(v.shape)])

        def link(dve, ins):
            chain[0] += 1
            ins.then_inc(dve_chain, 1)
            dve.wait_ge(dve_chain, chain[0])

        msum = region(A_Y, 1024, "p (b n) -> p b n", b=2)
        mrow = region(A_Y + 1024, 1024, "p (b n) -> p b n", parts=2, b=2)
        mbias = region(A_Y + 2048, 1024, "p (b n) -> p b n", parts=2, b=2)
        mod_zero = sem("mod_zero")
        mod_ev = sem("mod_ev")
        mod_sum = sem("mod_sum")
        mod_row = sem("mod_row")
        mod_b_in = [sem(f"mod_b_in{i}") for i in range(2)]
        mod_st = [sem(f"mod_st{i}") for i in range(2)]

        def mod_bank(q):
            return (q % 2, 2 + q % 2) if q < MOD_FIRST else (2 + q % 2, 6)

        def mod_new(q):
            return q < 2 or MOD_FIRST <= q < MOD_FIRST + 2

        def mod_steps(step, units):
            for q in units:
                step(q, q != MOD_FIRST and q > 0, True)
                if q + 1 in (MOD_FIRST, 2 * MODU):
                    step(q + 1, True, False)

        def mod_pe(pe, units):
            def step(q, last, this):
                if this:
                    n = U_EARLY["mod", q]
                    unit_wait(pe, n)
                    if mod_new(q):
                        pe.wait_ge(mod_zero, 2 if q < MOD_FIRST else 4)
                    else:
                        pe.wait_ge(mod_ev, q - 1)
                    w = unit(n)
                    for k in range(KD):
                        j = 32 * (k % 4)
                        mm = nc.tensor.matmul(psum[mod_bank(q)[0]][j:j + 2, :], lhsT=silu_c[:, k, :], rhs=w[:, k, :],
                                              start=(k < 4), stop=(k >= 4), skip_group_check=True)
                    mm.then_inc(mod_mm, 1)
                if last:
                    r = q - 1
                    pe.wait_ge(mod_ev, q)
                    if 2 <= r < MOD_FIRST:
                        pe.wait_ge(mod_row, r - 1)
                    elif r > MOD_FIRST:
                        pe.wait_ge(mod_row, r)
                    nc.tensor.matmul(psum[mod_bank(r)[1]][0:2, :], lhsT=consts[:, C_SEL:C_SEL + 2],
                                     rhs=msum[:, r % 2, :], start=True, stop=True).then_inc(mod_sum, 1)

            mod_steps(step, units)

        def mod_act(act, units):
            def step(q, last, this):
                if this:
                    l, n = divmod(q, MODU)
                    if q >= 2:
                        act.wait_ge(mod_row, q - 1)
                    act.dma_start(mbias[:, q % 2, :], a["mod_b"][l:l + 1, n * COLS:(n + 1) * COLS].to_broadcast(
                        [2, COLS])).then_inc(mod_b_in[q % 2], 16)
                    act.wait_ge(mod_mm, q + 1)
                    if q >= 2:
                        act.wait_ge(mod_sum, q - 1)
                    nc.scalar.activation(msum[:, q % 2, :], psum[mod_bank(q)[0]][:, :], ACT.Copy).then_inc(mod_ev, 1)
                if last:
                    l, n = divmod(q - 1, MODU)
                    act.wait_ge(mod_row, q)
                    act.dma_start(mod_dram[l, :, n * COLS:(n + 1) * COLS], mrow[:, (q - 1) % 2, :]).then_inc(
                        mod_st[(q - 1) % 2], 16)

            mod_steps(step, units)

        def mod_clear_dve(banks):
            for b in banks:
                nc.vector.memset(psum[b][:, :], 0.0).then_inc(mod_zero, 1)

        def mod_dve(dve, units):
            def step(q, last, this):
                if last:
                    r = q - 1
                    dve.wait_ge(mod_sum, r + 1)
                    dve.wait_ge(mod_b_in[r % 2], 16 * (r // 2 + 1))
                    if r >= 2:
                        dve.wait_ge(mod_st[r % 2], 16 * (r // 2))
                    nc.vector.tensor_tensor(mrow[:, r % 2, :], psum[mod_bank(r)[1]][0:2, :], mbias[:, r % 2, :],
                                            ALU.add).then_inc(mod_row, 1)

            mod_steps(step, units)

        def mod_after(c):
            return range(MOD_FIRST + c, min(MOD_FIRST + c + 1, 2 * MODU))

        def mod_wait(eng, l, units):
            q = MODU * l + units
            eng.wait_ge(mod_st[0], 16 * ((q + 1) // 2))
            eng.wait_ge(mod_st[1], 16 * (q // 2))

        xin = region(A_H, NT * D, "p (t d) -> p t d", t=NT)
        xn = [region(at, 4096, "p (t d) -> p t d", t=NT) for at in (A_Y + 4096, A_WORK)]
        aT = [region(at, 4096, "p (k n) -> p k n", k=KD) for at in (A_AT, A_BCT + 6144)]
        x_in = sem("x_in")
        n1_cols = sem("n1_cols")
        n1_A = sem("n1_A")
        n1_ss = sem("n1_ss")
        n1_ms = sem("n1_ms")
        n1_rstd = sem("n1_rstd")
        n1_xn = sem("n1_xn")
        n1_tp = sem("n1_tp")
        n1_ea = sem("n1_ea")
        n1_ed = sem("n1_ed")

        def norm1_pool(pool, l):
            if l:
                pool.wait_ge(n1_ed, 4)
                pool.wait_ge(n1_ea, 4)
            pool.dma_start(gcol[:, :], a["norm1_g"][l].rearrange("(p k) -> p k", k=KD)).then_inc(n1_cols, 16)
            mod_wait(pool, l, 4)
            for s in range(2):
                pool.dma_start(modcol[:, s, 0:2, :], mod_dram[l, s, 0:2 * D].rearrange("(w p k) -> p w k", w=2, k=KD)
                               ).then_inc(n1_cols, 16)

        def norm1_rstd_pool(pool, l):
            pool.wait_ge(n1_ms, l + 1)
            nc.gpsimd.tensor_tensor(rstd[:, :], ms[:, :], mhalf[:, :], ALU.pow).then_inc(n1_rstd, 1)

        def norm1_square_act(act, l):
            if l == 0:
                act.wait_ge(x_in, 32)
                for t in range(NT):
                    nc.scalar.activation(xn[0][:, t, :], xin[:, t, :], ACT.Square, accum_out=ss[:, t:t + 1]).then_inc(
                        n1_ss, 1)
                return
            junk = region(A_WORK + 4096, 2048, "p (b d) -> p b d", b=2)
            for t in range(NT):
                act.wait_ge(cb_x, t + 1)
                if t >= 2:
                    act.wait_ge(n1_ss, NT + t - 1)
                nc.scalar.activation(junk[:, t % 2, :], xin[:, t, :], ACT.Square, accum_out=ss[:, t:t + 1]).then_inc(
                    n1_ss, 1)

        def norm1_act(act, l):
            act.wait_ge(n1_A, 2 * l + 2)
            for i in range(0, 8, 2):
                s, kp = divmod(i, 4)
                act.wait_ge(n1_tp, 8 * l + i + 1)
                for kk in range(2):
                    k = 2 * kp + kk
                    ev = nc.scalar.activation(aT[l][:, k, s * SEQ:(s + 1) * SEQ], psum[4][:, kk * SEQ:(kk + 1) * SEQ],
                                              ACT.Identity, bias=modcol[:, s, 0, k:k + 1], scale=modcol[:, s, 2, k:k + 1])
                ev.then_inc(n1_ea, 1)

        def norm1_scale_dve(dve, l):
            dve.wait_ge(n1_ss, NT * (l + 1))
            nc.vector.tensor_scalar(ms[:, :], ss[:, :], 1.0 / D, EPS, ALU.mult, ALU.add).then_inc(n1_ms, 1)
            dve.wait_ge(n1_rstd, l + 1)
            for t in range(NT):
                nc.vector.tensor_scalar(xn[l][:, t, :], xin[:, t, :], rstd[:, t:t + 1], None, ALU.mult).then_inc(
                    n1_xn, 1)

        def norm1_dve(dve, l):
            dve.wait_ge(n1_cols, 48 * (l + 1))
            for s in range(2):
                nc.vector.scalar_tensor_tensor(modcol[:, s, 2, :], modcol[:, s, 1, :], 1.0, gcol[:, :],
                                               ALU.add, ALU.mult).then_inc(n1_A, 1)
            dve.wait_ge(n1_A, 2 * l + 2)
            for i in range(1, 8, 2):
                s, kp = divmod(i, 4)
                dve.wait_ge(n1_tp, 8 * l + i + 1)
                for kk in range(2):
                    k = 2 * kp + kk
                    ev = nc.vector.tensor_scalar(aT[l][:, k, s * SEQ:(s + 1) * SEQ], psum[5][:, kk * SEQ:(kk + 1) * SEQ],
                                                 modcol[:, s, 2, k:k + 1], modcol[:, s, 0, k:k + 1], ALU.mult, ALU.add)
                ev.then_inc(n1_ed, 1)

        def norm1_pe(pe, l):
            if l:
                pe.wait_ge(moe_out, 1)
            for i in range(8):
                s, kp = divmod(i, 4)
                pe.wait_ge(n1_xn, NT * l + 2 * s + 2)
                if i >= 2:
                    pe.wait_ge((n1_ea, n1_ed)[i % 2], 4 * l + i // 2)
                for kk in range(2):
                    for t in range(2):
                        c = kk * SEQ + t * P
                        tp = nc.tensor.transpose(psum[4 + i % 2][:, c:c + P], xn[l][:, 2 * s + t, 2 * kp + kk::KD], ident)
                tp.then_inc(n1_tp, 1)

        xrow = region(A_XROW, 8192, "p (t c) -> p t c", t=NT)
        BT = region(A_BCT, 2048, "p (g n) -> p g n", g=GROUPS)
        CT = region(A_BCT + 2048, 2048, "p (g n) -> p g n", g=GROUPS)
        Brow = region(A_BCT + 4096, 2048, "p (t g n) -> p t g n", t=NT, g=GROUPS)
        PADW = SEQ + TAPS - 1
        cin = region(A_WORK, 4 * PADW, "p (b s n) -> p b s n", b=2, s=2)
        cacc = region(A_WORK + 1040, 1024, "p (b n) -> p b n", b=2)
        cxT = region(A_WORK + 2064, 1024, "p (b n) -> p b n", b=2)
        convw = region(A_WORK + 3088, NCH * TAPS, "p (c j) -> p c j", c=NCH)
        convb = region(A_WORK + 3208, NCH)
        wdt = region(A_Y + 3072, KD * 64, "p (k n) -> p k n", k=KD)
        sw_in = sem("sw_in")
        cv_pad = sem("cv_pad")
        cv_in = sem("cv_in")
        cv_out = sem("cv_out")
        cv_silu = sem("cv_silu")
        cv_tp = sem("cv_tp")
        cv_row = sem("cv_row")
        DECAYS_AT = 3
        NROW = 20

        def conv_pe(pe):
            def transposes(c):
                pe.wait_ge(cv_silu, c + 1)
                if c >= 2:
                    pe.wait_ge(cv_row, c - 1)
                for t in range(NT):
                    src = cxT[:, c % 2, t * P:(t + 1) * P] if c < 16 else BT[:, c - 16, t * P:(t + 1) * P]
                    tp = nc.tensor.transpose(psum[4 + c % 2][:, t * P:(t + 1) * P], src, ident)
                tp.then_inc(cv_tp, 1)

            pe.wait_ge(n1_ea, 4)
            pe.wait_ge(n1_ed, 4)
            dt_pe(pe)
            for c in range(NCH):
                if c == DECAYS_AT:
                    decay_pe(pe)
                if c % 4 == 0:
                    unit_wait(pe, U_EARLY["xbc", c // 4])
                w = unit(U_EARLY["xbc", c // 4])
                if c >= 2:
                    pe.wait_ge(cv_in, c - 1)
                for k in range(KD):
                    mm = nc.tensor.matmul(psum[c % 2][:, :], lhsT=w[:, k, (c % 4) * P:(c % 4 + 1) * P],
                                          rhs=aT[0][:, k, :], start=(k == 0), stop=(k == KD - 1))
                mm.then_inc(cv_mm, 1)
                if 2 <= c < NROW + 2:
                    transposes(c - 2)
                mod_pe(pe, mod_after(c))

        def conv_act(act):
            act.wait_ge(cv_pad, 2)
            for c in range(NCH + 3):
                if c == DECAYS_AT:
                    decay_act(act)
                if c < NCH:
                    act.wait_ge(cv_mm, c + 1)
                    if c >= 2:
                        act.wait_ge(cv_out, c - 1)
                    nc.scalar.activation(cin[:, c % 2, :, 2:2 + SEQ], psum[c % 2][:, :].rearrange(
                        "p (s n) -> p s n", s=2), ACT.Copy).then_inc(cv_in, 1)
                if 1 <= c < NCH + 1:
                    d = c - 1
                    act.wait_ge(cv_out, d + 1)
                    if 2 <= d < 16:
                        act.wait_ge(cv_tp, d - 1)
                    to = cxT[:, d % 2, :] if d < 16 else BT[:, d - 16, :] if d < 20 else CT[:, d - 20, :]
                    nc.scalar.activation(to, cacc[:, d % 2, :], ACT.Silu, bias=convb[:, d:d + 1]).then_inc(cv_silu, 1)
                if 3 <= c < NROW + 3:
                    d = c - 3
                    act.wait_ge(cv_tp, d + 1)
                    to = xrow[:, :, d * P:(d + 1) * P] if d < 16 else Brow[:, :, d - 16, :]
                    nc.scalar.activation(to, psum[4 + d % 2][:, :].rearrange("p (t n) -> p t n", t=NT),
                                         ACT.Copy).then_inc(cv_row, 1)
                if c < NCH:
                    mod_act(act, mod_after(c))

        def conv_dve(dve):
            for b in range(2):
                nc.vector.memset(cin[:, b, :, :], 0.0).then_inc(cv_pad, 1)
            mod_clear_dve((2, 3))
            dve.wait_ge(sw_in, 16 * 5)
            for c in range(NCH):
                if c == DECAYS_AT:
                    decay_dve(dve)
                dve.wait_ge(cv_in, c + 1)
                if c >= 2:
                    dve.wait_ge(cv_silu, c - 1)
                acc = cacc[:, c % 2, :].rearrange("p (s n) -> p s n", s=2)
                link(dve, nc.vector.tensor_scalar(acc, cin[:, c % 2, :, 0:SEQ], convw[:, c, 0:1], None, ALU.mult))
                for j in range(1, TAPS):
                    st = nc.vector.scalar_tensor_tensor(acc, cin[:, c % 2, :, j:j + SEQ], convw[:, c, j:j + 1], acc,
                                                        ALU.mult, ALU.add)
                    if j < TAPS - 1:
                        link(dve, st)
                st.then_inc(cv_out, 1)
                mod_dve(dve, mod_after(c))

        dtT = A_WORK + 6144
        dt = region(dtT, 256, "p (t d h) -> p t d h", t=NT, d=2)
        dtA = region(dtT + 256, 256, "p (t d h) -> p t d h", t=NT, d=2)
        EX = region(dtT + 512, 768, "p (d t w h) -> p d t w h", d=2, t=NT, w=3)
        wend = region(dtT + 1280, 256, "p (d t h) -> p d t h", d=2, t=NT)
        tmp6 = [region(A_WORK + 4096 + 256 * i, 256) for i in range(6)]
        dtb = region(A_WORK + 5632, 64)
        alog = region(A_WORK + 5696, 64)
        nega = region(A_WORK + 5760, 64)
        dt_mm = sem("dt_mm")
        dt_x = sem("dt_x")
        dt_u = sem("dt_u")
        dt_w = sem("dt_w")
        dt_l = sem("dt_l")
        dt_A = sem("dt_A")
        ex_mm = sem("ex_mm")
        ex_ev = sem("ex_ev")
        wend_ok = sem("wend_ok")

        def dt_pe(pe):
            pe.wait_ge(sw_in, 16 * 5)
            for t in range(NT):
                for k in range(KD):
                    mm = nc.tensor.matmul(psum[7][:, t * 64:(t + 1) * 64], lhsT=aT[0][:, k, t * P:(t + 1) * P],
                                          rhs=wdt[:, k, :], start=(k == 0), stop=(k == KD - 1))
            mm.then_inc(dt_mm, 1)

        def dt_dve(dve):
            x, r, w, m, u, lg = tmp6
            dve.wait_ge(dt_mm, 1)
            link(dve, nc.vector.tensor_tensor(x.rearrange("p (t n) -> p t n", t=NT),
                                              psum[7][:, 0:256].rearrange("p (t n) -> p t n", t=NT),
                                              bc(dtb, 1, NT), ALU.add))
            nc.vector.tensor_scalar(r, x, 0.0, None, ALU.max)
            nc.vector.scalar_tensor_tensor(w, x, -1.0, x, ALU.mult, ALU.max).then_inc(dt_x, 1)
            dve.wait_ge(dt_u, 2)
            link(dve, nc.vector.tensor_scalar(w, u, 1.0, None, ALU.add))
            nc.vector.tensor_scalar(m, w, 1.0, None, ALU.is_equal).then_inc(dt_w, 1)
            dve.wait_ge(dt_w, 1)
            dve.wait_ge(dt_l, 1)
            link(dve, nc.vector.scalar_tensor_tensor(w, w, -1.0, m, ALU.add, ALU.add))
            link(dve, nc.vector.reciprocal(w, w))
            link(dve, nc.vector.tensor_tensor(w, w, lg, ALU.mult))
            link(dve, nc.vector.tensor_tensor(w, w, m, ALU.add))
            link(dve, nc.vector.tensor_tensor(w, w, u, ALU.mult))
            dtf = dt.rearrange("p t d h -> p (t d h)")
            link(dve, nc.vector.tensor_tensor(dtf, w, r, ALU.add))
            link(dve, nc.vector.tensor_scalar(nega, nega, -1.0, None, ALU.mult))
            nc.vector.tensor_tensor(dtA.rearrange("p t d h -> p t (d h)"), dt.rearrange("p t d h -> p t (d h)"),
                                    bc(nega, 1, NT), ALU.mult).then_inc(dt_A, 1)

        def decay_dve(dve):
            dve.wait_ge(ex_ev, 2)
            for d in range(2):
                nc.vector.tensor_tensor(wend[:, d], EX[:, d, :, 1, :], dt[:, :, d, :], ALU.mult).then_inc(wend_ok, 1)

        def dt_act(act):
            x, r, w, m, u, lg = tmp6
            act.wait_ge(sw_in, 16 * 5)
            nc.scalar.activation(nega, alog, ACT.Exp).then_inc(dt_u, 1)
            act.wait_ge(dt_x, 1)
            nc.scalar.activation(u, w, ACT.Exp, scale=-1.0).then_inc(dt_u, 1)
            act.wait_ge(dt_w, 1)
            nc.scalar.activation(lg, w, ACT.Ln).then_inc(dt_l, 1)

        def decay_act(act):
            for d in range(2):
                act.wait_ge(ex_mm, d + 1)
                nc.scalar.activation(EX[:, d].rearrange("p t w h -> p (t w h)"), psum[7][:, 0:384],
                                     ACT.Exp).then_inc(ex_ev, 1)

        def decay_pe(pe):
            pe.wait_ge(dt_A, 1)
            for d in range(2):
                if d:
                    pe.wait_ge(ex_ev, 1)
                upto, after = ((C_LE, C_GT), (C_GE, C_LT))[d]
                for t in range(NT):
                    for w, c in enumerate((upto, after, C_ONE)):
                        at = (t * 3 + w) * HEADS
                        mm = nc.tensor.matmul(psum[7][:, at:at + HEADS], lhsT=consts[:, c:c + P],
                                              rhs=dtA[:, t, d, :], start=True, stop=True)
                mm.then_inc(ex_mm, 1)

        y = region(A_Y, 8192, "p (t c) -> p t c", t=NT)
        h = region(A_H, 4096, "p (d g n) -> p d g n", d=2, g=GROUPS)
        RU = region(A_WORK, 2048, "p (b r n) -> p b r n", b=2, r=HG)
        EB = region(A_WORK + 2048, 2048, "p (b r n) -> p b r n", b=2, r=HG)
        xdt = region(A_WORK + 4096, 1024, "p (b r n) -> p b r n", b=2, r=HG)
        xw = region(A_WORK + 5120, 1024, "p (b r n) -> p b r n", b=2, r=HG)
        cbm = sb("cbm", [P, P])
        ytmp = region(A_WORK + 7680, COLS)
        STEPS = [(0, 2), (1, 3), (0, 3), (1, 2), (0, 0), (1, 1), (0, 1), (1, 0)]
        ITEMS = [(d, t, g, s) for s, (d, t) in enumerate(STEPS) for g in range(GROUPS)]
        sc_ru = sem("sc_ru")
        sc_xdt = sem("sc_xdt")
        sc_xw = sem("sc_xw")
        sc_seg = sem("sc_seg")
        sc_cb = sem("sc_cb")
        sc_e = sem("sc_e")
        sc_cbm = sem("sc_cbm")
        sc_mix = sem("sc_mix")
        sc_y = sem("sc_y")
        sc_st = sem("sc_st")
        sc_yev = sem("sc_yev")
        sc_h = sem("sc_h")
        NI = len(ITEMS)
        NST = NI - 2 * GROUPS

        def heads(v, g):
            return v[:, g * HG:(g + 1) * HG]

        def scan_pool(pool):
            pool.wait_ge(cv_row, NROW)
            pool.wait_ge(cv_silu, NCH)
            pool.wait_ge(wend_ok, 2)
            for i, (d, t, g, s) in enumerate(ITEMS):
                b = i % 2
                x_g = xrow[:, t, g * GW:(g + 1) * GW].rearrange("p (r n) -> p r n", r=HG)
                if i >= 2:
                    pool.wait_ge(sc_seg, i - 1)
                tri = (C_LE, C_GE)[d]
                nc.gpsimd.tensor_tensor(RU[:, b], bc(heads(dtA[:, t, d], g), 2, P), bc(consts[:, tri:tri + P], 1, HG),
                                        ALU.mult).then_inc(sc_ru, 1)
                if i >= 2:
                    pool.wait_ge(sc_y, i - 1)
                nc.gpsimd.tensor_tensor(xdt[:, b], x_g, bc(heads(dt[:, t, d], g), 2, HD), ALU.mult).then_inc(sc_xdt, 1)
                if i < NST:
                    if i >= 2:
                        pool.wait_ge(sc_st, i - 1)
                    nc.gpsimd.tensor_tensor(xw[:, b], x_g, bc(heads(wend[:, d, t], g), 2, HD), ALU.mult).then_inc(
                        sc_xw, 1)

        def scan_pe(pe):
            def head(i):
                d, t, g, s = ITEMS[i]
                b = i % 2
                pe.wait_ge(sc_ru, i + 1)
                if i >= 2:
                    pe.wait_ge(sc_e, 2 * (i - 1))
                c = (C_GT, C_LT)[d]
                for q in range(2):
                    mm = nc.tensor.matmul(psum[2 * b + q][:, :], lhsT=consts[:, c:c + P],
                                          rhs=RU[:, b, 4 * q:4 * q + 4, :].rearrange("p r n -> p (r n)"),
                                          start=True, stop=True)
                mm.then_inc(sc_seg, 1)
                if i >= 1:
                    pe.wait_ge(sc_cbm, i)
                nc.tensor.matmul(psum[4][:, 0:P], lhsT=BT[:, g, t * P:(t + 1) * P], rhs=CT[:, g, t * P:(t + 1) * P],
                                 start=True, stop=True).then_inc(sc_cb, 1)

            pe.wait_ge(cv_silu, NCH)
            pe.wait_ge(cv_row, NROW)
            pe.wait_ge(ex_ev, 2)
            pe.wait_ge(mod_ev, 2 * MODU)
            pe.wait_ge(cv_in, NCH)
            head(0)
            for i, (d, t, g, s) in enumerate(ITEMS):
                if i + 1 < NI:
                    head(i + 1)
                b = i % 2
                pe.wait_ge(sc_mix, i + 1)
                pe.wait_ge(sc_xdt, i + 1)
                if i >= 1:
                    pe.wait_ge(sc_yev, i)
                if s >= 2:
                    pe.wait_ge(sc_h, i - 8 + 1)
                    nc.tensor.matmul(psum[6][:, :], lhsT=CT[:, g, t * P:(t + 1) * P], rhs=h[:, d, g, :],
                                     start=True, stop=True)
                for r in range(HG):
                    mm = nc.tensor.matmul(psum[5][:, r * HD:(r + 1) * HD], lhsT=EB[:, b, r, :], rhs=xdt[:, b, r, :],
                                          start=True, stop=True)
                mm.then_inc(sc_y, 1)
                if i < NST:
                    pe.wait_ge(sc_xw, i + 1)
                    if i >= 1:
                        pe.wait_ge(sc_h, i)
                    nc.tensor.matmul(psum[7][:, :], lhsT=Brow[:, t, g, :],
                                     rhs=xw[:, b].rearrange("p r n -> p (r n)"), start=True, stop=True).then_inc(
                        sc_st, 1)

        def scan_act(act):
            for i in range(NI):
                b = i % 2
                act.wait_ge(sc_seg, i + 1)
                if i >= 2:
                    act.wait_ge(sc_y, i - 1)
                for q in range(2):
                    nc.scalar.activation(EB[:, b, 4 * q:4 * q + 4, :].rearrange("p r n -> p (r n)"),
                                         psum[2 * b + q][:, :], ACT.Exp).then_inc(sc_e, 1)

        def scan_dve(dve):
            def tail(i):
                d, t, g, s = ITEMS[i]
                first = s in (0, 1, 4, 5)
                y_g = y[:, t, g * GW:(g + 1) * GW]
                dve.wait_ge(sc_y, i + 1)
                if s < 2:
                    nc.vector.tensor_copy(y_g, psum[5][:, :]).then_inc(sc_yev, 1)
                else:
                    link(dve, nc.vector.tensor_tensor(ytmp.rearrange("p (r n) -> p r n", r=HG),
                                                      psum[6][:, :].rearrange("p (r n) -> p r n", r=HG),
                                                      bc(heads(EX[:, d, t, 0], g), 2, HD), ALU.mult))
                    nc.vector.tensor_tensor(y_g if first else ytmp, ytmp, psum[5][:, :],
                                            ALU.add).then_inc(sc_yev, 1)
                    dve.wait_ge(sc_yev, i + 1)
                    if not first:
                        link(dve, nc.vector.tensor_tensor(y_g, y_g, ytmp, ALU.add))
                if i < NST:
                    dve.wait_ge(sc_st, i + 1)
                    if s < 2:
                        nc.vector.tensor_copy(h[:, d, g, :], psum[7][:, :]).then_inc(sc_h, 1)
                    else:
                        hv = h[:, d, g, :].rearrange("p (r n) -> p r n", r=HG)
                        link(dve, nc.vector.tensor_tensor(hv, hv, bc(heads(EX[:, d, t, 2], g), 2, HD), ALU.mult))
                        nc.vector.tensor_tensor(h[:, d, g, :], h[:, d, g, :], psum[7][:, :], ALU.add).then_inc(sc_h, 1)

            for i, (d, t, g, s) in enumerate(ITEMS):
                b = i % 2
                dve.wait_ge(sc_cb, i + 1)
                if i >= 1:
                    dve.wait_ge(sc_mix, i)
                m = (C_LE, C_GE)[d]
                nc.vector.tensor_tensor(cbm[:, :], psum[4][:, 0:P], consts[:, m:m + P], ALU.mult).then_inc(sc_cbm, 1)
                dve.wait_ge(sc_cbm, i + 1)
                dve.wait_ge(sc_e, 2 * i + 2)
                nc.vector.tensor_tensor(EB[:, b], EB[:, b], bc(cbm[:, :], 1, HG), ALU.mult).then_inc(sc_mix, 1)
                if i >= 1:
                    tail(i - 1)
            tail(NI - 1)

        yT = region(A_XROW, 8192, "p (c n) -> p c n", c=16)
        zs = region(A_WORK, 1024, "p (b n) -> p b n", b=2)
        dskip = region(A_WORK + 1024, HEADS)
        ngain = region(A_WORK + 1056, 16)
        gss = region(A_WORK + 1072, 16, "p (g t) -> p g t", g=GROUPS)
        gms = region(A_WORK + 1088, 16, "p (g t) -> p g t", g=GROUPS)
        grs = region(A_WORK + 1104, 16, "p (g t) -> p g t", g=GROUPS)
        gjunk = region(A_WORK + 4096, NT * COLS, "p (t n) -> p t n", t=NT)
        otmp = region(A_WORK + 2048, 1024, "p (b n) -> p b n", b=2)
        gate1 = region(A_BCT, 2048, "p (s d) -> p s d", s=2)
        fin_in = sem("fin_in")
        fin_xd = sem("fin_xd")
        fin_add = sem("fin_add")
        z_silu = sem("z_silu")
        z_mul = sem("z_mul")
        gn_ss = sem("gn_ss")
        gn_ms = sem("gn_ms")
        gn_rs = sem("gn_rs")
        gn_y = sem("gn_y")
        gn_tp = sem("gn_tp")
        gn_T = sem("gn_T")
        m1_x = sem("m1_x")

        def finish_pool(pool):
            pool.wait_ge(sc_mix, NI)
            pool.wait_ge(sc_xdt, NI)
            pool.dma_start(dskip, a["ssd_d"].to_broadcast([P, HEADS])).then_inc(fin_in, 16)
            pool.dma_start(ngain, a["norm_cols"]).then_inc(fin_in, 16)
            pool.wait_ge(fin_in, 32)
            for t in range(NT):
                xv = xrow[:, t, :].rearrange("p (r n) -> p r n", r=HEADS)
                nc.gpsimd.tensor_tensor(xv, xv, bc(dskip, 2, HD), ALU.mult).then_inc(fin_xd, 1)
            pool.wait_ge(sc_y, NI)
            pool.wait_ge(sc_h, NST)
            for s, name in enumerate(("x", "ctx")):
                pool.dma_start(xin[:, 2 * s:2 * s + 2, :], a[name][0].rearrange("(t p) d -> p t d", p=P)).then_inc(
                    fin_in, 16)
                pool.dma_start(gate1[:, s, :], mod_dram[0, s:s + 1, 2 * D:3 * D].to_broadcast([P, D])).then_inc(
                    fin_in, 16)
            for g in range(GROUPS):
                pool.wait_ge(gn_ms, g + 1)
                nc.gpsimd.tensor_tensor(grs[:, g, :], gms[:, g, :], mhalf[:, :], ALU.pow).then_inc(gn_rs, 1)

        def finish_pe(pe):
            def gate(g):
                unit_wait(pe, U_Z + g)
                w = unit(U_Z + g)
                for t in range(NT):
                    i = NT * g + t
                    if i >= 2:
                        pe.wait_ge(z_silu, i - 1)
                    for k in range(KD):
                        mm = nc.tensor.matmul(psum[i % 2][:, :], lhsT=aT[0][:, k, t * P:(t + 1) * P], rhs=w[:, k, :],
                                              start=(k == 0), stop=(k == KD - 1))
                    mm.then_inc(z_mm, 1)

            def turn(g):
                pe.wait_ge(gn_y, NT * (g + 1))
                for q in range(4):
                    i = 4 * g + q
                    if i >= 2:
                        pe.wait_ge(gn_T, i - 1)
                    for t in range(NT):
                        tp = nc.tensor.transpose(psum[2 + i % 2][:, t * P:(t + 1) * P],
                                                 y[:, t, g * GW + q * P:g * GW + (q + 1) * P], ident)
                    tp.then_inc(gn_tp, 1)

            pe.wait_ge(sc_e, 2 * NI)
            gate(0)
            for g in range(GROUPS):
                if g + 1 < GROUPS:
                    gate(g + 1)
                turn(g)
            pe.wait_ge(gn_T, 16)
            pe.wait_ge(z_silu, 16)
            pe.wait_ge(sc_yev, NI)
            pe.wait_ge(sc_h, NST)
            for n in range(4):
                half, part = divmod(n, 2)
                unit_wait(pe, U_WOUT + n)
                w = unit(U_WOUT + n)
                for t in range(NT):
                    for c in range(8):
                        mm = nc.tensor.matmul(psum[4 - 4 * half + t][:, :], lhsT=yT[:, 8 * part + c, t * P:(t + 1) * P],
                                              rhs=w[:, c, :], start=(part == 0 and c == 0), stop=(part == 1 and c == 7))
                    mm.then_inc(wout_mm, 1)

        def finish_act(act):
            def square(g):
                act.wait_ge(z_mul, NT * (g + 1))
                if g:
                    act.wait_ge(gn_ss, NT * g)
                for t in range(NT):
                    nc.scalar.activation(gjunk[:, t], y[:, t, g * GW:(g + 1) * GW], ACT.Square,
                                         accum_out=gss[:, g, t:t + 1]).then_inc(gn_ss, 1)

            def evac(g):
                for i in range(4 * g, 4 * g + 4):
                    act.wait_ge(gn_tp, i + 1)
                    nc.scalar.activation(yT[:, i, :], psum[2 + i % 2][:, :], ACT.Identity,
                                         scale=ngain[:, i:i + 1]).then_inc(gn_T, 1)

            act.wait_ge(fin_in, 32)
            act.wait_ge(sc_mix, NI)
            act.wait_ge(sc_seg, NI)
            for g in range(GROUPS):
                for t in range(NT):
                    i = NT * g + t
                    act.wait_ge(z_mm, i + 1)
                    if i >= 2:
                        act.wait_ge(z_mul, i - 1)
                    nc.scalar.activation(zs[:, i % 2, :], psum[i % 2][:, :], ACT.Silu).then_inc(z_silu, 1)
                if g == 0:
                    act.wait_ge(fin_add, NT)
                square(g)
                if g >= 1:
                    evac(g - 1)
            evac(GROUPS - 1)

        def finish_dve(dve):
            for t in range(NT):
                dve.wait_ge(fin_xd, t + 1)
                nc.vector.tensor_tensor(y[:, t, :], y[:, t, :], xrow[:, t, :], ALU.add).then_inc(fin_add, 1)
            dve.wait_ge(fin_add, NT)

            def mul(g):
                for t in range(NT):
                    i = NT * g + t
                    dve.wait_ge(z_silu, i + 1)
                    y_g = y[:, t, g * GW:(g + 1) * GW]
                    nc.vector.tensor_tensor(y_g, y_g, zs[:, i % 2, :], ALU.mult).then_inc(z_mul, 1)

            def norm(g):
                dve.wait_ge(gn_ss, NT * (g + 1))
                nc.vector.tensor_scalar(gms[:, g, :], gss[:, g, :], 1.0 / GW, EPS, ALU.mult, ALU.add).then_inc(gn_ms, 1)
                dve.wait_ge(gn_rs, g + 1)
                for t in range(NT):
                    y_g = y[:, t, g * GW:(g + 1) * GW]
                    nc.vector.tensor_scalar(y_g, y_g, grs[:, g, t:t + 1], None, ALU.mult).then_inc(gn_y, 1)

            mul(0)
            for g in range(GROUPS):
                norm(g)
                if g + 1 < GROUPS:
                    mul(g + 1)
            dve.wait_ge(fin_in, 16 * 6)
            for i in range(2 * NT):
                half, t = divmod(i, NT)
                cs = slice(half * COLS, (half + 1) * COLS)
                dve.wait_ge(wout_mm, 2 * NT * half + NT + t + 1)
                link(dve, nc.vector.tensor_tensor(otmp[:, i % 2, :], psum[4 - 4 * half + t][:, :], gate1[:, t // 2, cs],
                                                  ALU.mult))
                nc.vector.tensor_tensor(xin[:, t, cs], xin[:, t, cs], otmp[:, i % 2, :], ALU.add).then_inc(m1_x, 1)

        M0 = A_BCT
        gate2 = region(M0, 2048, "p (s d) -> p s d", s=2)
        mA = region(M0 + 2048, 2048, "p (s d) -> p s d", s=2)
        mB = region(M0 + 4096, 2048, "p (s d) -> p s d", s=2)
        gain2 = region(M0 + 6144, D)
        frow = region(M0 + 7168, 2048, "p (b d) -> p b d", b=2)
        fT = region(M0 + 9216, 2048, "p (b k n) -> p b k n", b=2, k=KD)
        wrt = region(M0 + 11264, KD * (EG + E), "p (k n) -> p k n", k=KD)
        brt = region(M0 + 11552, EG + E)
        NR = EG + E
        r_at = [M0 + 11600]

        def route_tile(size, pattern=None, **dims):
            v = region(r_at[0], size, pattern, **dims)
            r_at[0] += size
            assert r_at[0] <= M0 + 14336
            return v

        t_n = dict(t=NT)
        r_lg = route_tile(NT * NR, "p (t n) -> p t n", **t_n)
        r_gp = route_tile(NT * 8, "p (t n) -> p t n", **t_n)
        r_gm = route_tile(NT * 8, "p (t n) -> p t n", **t_n)
        r_gi = route_tile(NT * 8, "p (t n) -> p t n", **t_n).bitcast(U32)
        r_gf = route_tile(NT)
        r_g1 = route_tile(NT * EG, "p (t n) -> p t n", **t_n)
        r_ge = route_tile(NT * EG, "p (t n) -> p t n", **t_n)
        r_gs = route_tile(NT)
        r_es = route_tile(NT * 8, "p (t n) -> p t n", **t_n)
        r_em = route_tile(NT * 8, "p (t n) -> p t n", **t_n)
        r_ei = route_tile(NT * 8, "p (t n) -> p t n", **t_n).bitcast(U32)
        r_ef = route_tile(NT * 2, "p (t n) -> p t n", **t_n)
        r_d = route_tile(NT)
        r_w = route_tile(2 * NT, "p (k t) -> p k t", k=2)
        r_one = route_tile(2 * NT * E, "p (k t n) -> p k t n", k=2, t=NT)
        r_m = route_tile(NT * E, "p (t n) -> p t n", **t_n)
        r_r = route_tile(NT * E, "p (t n) -> p t n", **t_n)
        r_q = route_tile(NT * E, "p (t n) -> p t n", **t_n)
        r_tmp = region(M0 + 6144, NT * E, "p (t n) -> p t n", **t_n)
        r_tmp2 = region(M0 + 6144 + 256, EG * NT * 8, "p (t g n) -> p t g n", t=NT, g=EG)
        r_slot = route_tile(2 * NT, "p (k t) -> p k t", k=2)
        r_sloti = route_tile(2 * NT, "p (k t) -> p k t", k=2).bitcast(U32)
        r_pos = route_tile(2 * NT, "p (k t) -> p k t", k=2)
        r_posi = route_tile(2 * NT, "p (k t) -> p k t", k=2).bitcast(U32)
        r_blk = route_tile(2 * NT, "p (k t) -> p k t", k=2)
        r_ov = route_tile(E)
        r_ovc = route_tile(E)
        r_b1 = route_tile(E)
        r_zero = route_tile(E)
        NOVM = overflow_blocks(NT * P)
        r_ove = route_tile(NOVM)
        r_ovi = route_tile(NOVM + 1).bitcast(I32)
        NBM = E // 2 + NOVM
        r_ovm = region(M0 + 6144 + 512, NOVM * E, "p (m e) -> p m e", parts=1, m=NOVM)
        r_tok = route_tile(NBM).bitcast(U32)
        r_ovidx = route_tile(1).bitcast(U32)
        r_Q = region(M0 + 9216, 2 * P, "p (b n) -> p b n", b=2)
        r_R = region(M0 + 9216 + 2 * P, 2 * NBM, "p (b n) -> p b n", b=2)

        n2_in = sem("n2_in")
        n2_g2 = sem("n2_g2")
        n2_ss = sem("n2_ss")
        n2_ms = sem("n2_ms")
        n2_rstd = sem("n2_rstd")
        n2_A = sem("n2_A")
        n2_f = sem("n2_f")
        n2_tp = sem("n2_tp")
        n2_ea = sem("n2_ea")
        n2_ed = sem("n2_ed")
        n2_st = [sem(f"n2_st{i}") for i in range(2)]
        rt_lg = sem("rt_lg")
        rt_d1 = sem("rt_d1")
        rt_e1 = sem("rt_e1")
        rt_m = sem("rt_m")
        rt_rank = sem("rt_rank")
        rt_qr = sem("rt_qr")
        rt_tokp = sem("rt_tokp")
        rt_slot = sem("rt_slot")
        tiles = [NT, NTL]
        base_t = [0, NT]

        def mixer_done(eng, l, t):
            if l == 0:
                eng.wait_ge(m1_x, NT + t + 1)
            else:
                eng.wait_ge(a1_x, 2 * NTL)

        def norm2_pool(pool, l):
            ns = (2, 1)[l]
            if l == 0:
                pool.wait_ge(sc_y, NI)
                pool.wait_ge(sc_st, NST)
                pool.wait_ge(gn_tp, 16)
            else:
                pool.wait_ge(at_otp, 4)
            mod_wait(pool, l, MODU)
            for s in range(ns):
                pool.dma_start(mA[:, s, :], mod_dram[l, s:s + 1, 4 * D:5 * D].to_broadcast([P, D])).then_inc(n2_in, 16)
                pool.dma_start(mB[:, s, :], mod_dram[l, s:s + 1, 3 * D:4 * D].to_broadcast([P, D])).then_inc(n2_in, 16)
            pool.dma_start(gain2, a["norm2_g"][l:l + 1, :].to_broadcast([P, D])).then_inc(n2_in, 16)
            pool.dma_start(wrt[:, :, 0:EG], a["moe_w_group"][l].rearrange("(p k) n -> p k n", k=KD)).then_inc(n2_in, 16)
            pool.dma_start(wrt[:, :, EG:], a["moe_w_router"][l].rearrange("(p k) n -> p k n", k=KD)).then_inc(n2_in, 16)
            pool.dma_start(brt[:, 0:EG], a["moe_b_group"][l:l + 1, :].to_broadcast([P, EG])).then_inc(n2_in, 16)
            pool.dma_start(brt[:, EG:], a["moe_b_router"][l:l + 1, :].to_broadcast([P, E])).then_inc(n2_in, 16)
            pool.wait_ge(n2_ms, l + 1)
            nc.gpsimd.tensor_tensor(rstd[:, :], ms[:, :], mhalf[:, :], ALU.pow).then_inc(n2_rstd, 1)
            for s in range(ns):
                pool.dma_start(gate2[:, s, :], mod_dram[l, s:s + 1, 5 * D:6 * D].to_broadcast([P, D])).then_inc(n2_g2, 16)

        N2_IN = [16 * 9, 16 * 16]

        def norm2_act(act, l):
            nt, t0 = tiles[l], base_t[l]
            for t in range(nt):
                mixer_done(act, l, t)
                if t == 0 and l == 0:
                    act.wait_ge(gn_tp, 16)
                if t >= 2:
                    act.wait_ge(n2_ss, t0 + t - 1)
                nc.scalar.activation(frow[:, t % 2, :], xin[:, t, :], ACT.Square, accum_out=ss[:, t:t + 1]).then_inc(
                    n2_ss, 1)
            for t in range(nt):
                act.wait_ge(n2_f, t0 + t + 1)
                act.dma_start(f_dram[t * P:(t + 1) * P, :], frow[:, t % 2, :]).then_inc(n2_st[t % 2], 16)
                act.wait_ge(n2_tp, 2 * (t0 + t) + 1)
                nc.scalar.activation(fT[:, t % 2, 0:4, :].rearrange("p k n -> p (k n)"), psum[4][:, :],
                                     ACT.Copy).then_inc(n2_ea, 1)
            act.wait_ge(rt_d1, 2 * l + 1)
            nc.scalar.activation(r_ge[:, 0:nt], r_ge[:, 0:nt], ACT.Exp).then_inc(rt_e1, 1)
            act.wait_ge(rt_d1, 2 * l + 2)
            nc.scalar.activation(r_d[:, 0:nt], r_d[:, 0:nt], ACT.Exp).then_inc(rt_e1, 1)

        def norm2_pe(pe, l):
            nt, t0 = tiles[l], base_t[l]
            if l == 0:
                pe.wait_ge(m1_x, NT)
            else:
                pe.wait_ge(a1_x, 2 * NTL)

            def logits(t):
                pe.wait_ge(n2_in, N2_IN[l])
                pe.wait_ge(n2_ea, t0 + t + 1)
                pe.wait_ge(n2_ed, t0 + t + 1)
                for k in range(KD):
                    mm = nc.tensor.matmul(psum[6][:, t * NR:(t + 1) * NR], lhsT=fT[:, t % 2, k, :], rhs=wrt[:, k, :],
                                          start=(k == 0), stop=(k == KD - 1))
                mm.then_inc(rt_lg, 1)

            for t in range(nt):
                pe.wait_ge(n2_f, t0 + t + 1)
                for half in range(2):
                    if t >= 1:
                        pe.wait_ge((n2_ea, n2_ed)[half], t0 + t)
                    for k in range(4):
                        tp = nc.tensor.transpose(psum[4 + half][:, k * P:(k + 1) * P], frow[:, t % 2, 4 * half + k::KD],
                                                 ident)
                    tp.then_inc(n2_tp, 1)
                if t >= 1:
                    logits(t - 1)
            logits(nt - 1)
            pe.wait_ge(rt_m, l + 1)
            for t in range(nt):
                for u in range(t + 1):
                    c = C_LT if u == t else C_ONE
                    nc.tensor.matmul(psum[7][:, t * E:(t + 1) * E], lhsT=consts[:, c:c + P], rhs=r_m[:, u, :],
                                     start=(u == 0), stop=(u == t))
            for u in range(nt):
                mm = nc.tensor.matmul(psum[7][:, nt * E:(nt + 1) * E], lhsT=consts[:, C_ONE:C_ONE + P],
                                      rhs=r_m[:, u, :], start=(u == 0), stop=(u == nt - 1))
            mm.then_inc(rt_rank, 1)
            nb = E // 2 + overflow_blocks(nt * P)
            for i in range(2 * nt):
                pe.wait_ge(rt_qr, 2 * t0 + i + 1)
                mm = nc.tensor.matmul(psum[6][:, 256:256 + nb], lhsT=r_Q[:, i % 2, :], rhs=r_R[:, i % 2, 0:nb],
                                      start=(i == 0), stop=(i == 2 * nt - 1))
                mm.then_inc(rt_tokp, 1)

        def norm2_dve(dve, l):
            nt, t0 = tiles[l], base_t[l]
            ns = (2, 1)[l]
            nov = overflow_blocks(nt * P)
            nb = E // 2 + nov
            V = nc.vector
            dve.wait_ge(n2_ss, t0 + nt)
            V.tensor_scalar(ms[:, 0:nt], ss[:, 0:nt], 1.0 / D, EPS, ALU.mult, ALU.add).then_inc(n2_ms, 1)
            dve.wait_ge(n2_in, N2_IN[l])
            for s in range(ns):
                V.scalar_tensor_tensor(mA[:, s, :], mA[:, s, :], 1.0, gain2, ALU.add, ALU.mult).then_inc(n2_A, 1)
            dve.wait_ge(n2_A, (2, 3)[l])
            dve.wait_ge(n2_rstd, l + 1)
            for t in range(nt + 1):
                if t < nt:
                    if t >= 2:
                        dve.wait_ge(n2_st[t % 2], 16 * (base_t[l] // 2 + t // 2))
                        dve.wait_ge(n2_tp, 2 * (t0 + t - 1))
                    fr = frow[:, t % 2, :]
                    link(dve, V.scalar_tensor_tensor(fr, xin[:, t, :], rstd[:, t:t + 1], mA[:, t // 2, :],
                                                     ALU.mult, ALU.mult))
                    V.tensor_tensor(fr, fr, mB[:, t // 2, :], ALU.add).then_inc(n2_f, 1)
                if t >= 1:
                    u = t - 1
                    dve.wait_ge(n2_tp, 2 * (t0 + u) + 2)
                    if u >= 2:
                        dve.wait_ge(rt_lg, t0 + u - 1)
                    V.tensor_copy(fT[:, u % 2, 4:8, :].rearrange("p k n -> p (k n)"), psum[5][:, :]).then_inc(n2_ed, 1)

            T = slice(0, nt)
            V.memset(r_zero, 0.0)
            link(dve, V.memset(r_gp, -3.0e38))
            dve.wait_ge(rt_lg, t0 + nt)
            link(dve, V.tensor_tensor(r_lg[:, T], psum[6][:, 0:nt * NR].rearrange("p (t n) -> p t n", t=nt),
                                      bc(brt, 1, nt), ALU.add))
            link(dve, V.tensor_copy(r_gp[:, T, 0:EG], r_lg[:, T, 0:EG]))
            for t in range(nt):
                ins = V.max(r_gm[:, t], r_gp[:, t])
            link(dve, ins)
            for t in range(nt):
                ins = V.max_index(r_gi[:, t], r_gm[:, t], r_gp[:, t])
            link(dve, ins)
            V.tensor_tensor(r_ge[:, T], r_lg[:, T, 0:EG], r_gm[:, T, 0:1].to_broadcast([P, nt, EG]),
                            ALU.subtract).then_inc(rt_d1, 1)
            link(dve, V.tensor_copy(r_gf[:, T], r_gi[:, T, 0]))
            link(dve, V.tensor_tensor(r_g1[:, T], bc(consts[:, C_E:C_E + EG], 1, nt), bc(r_gf[:, T], 2, EG),
                                      ALU.is_equal))
            link(dve, V.tensor_tensor(r_tmp2[:, T], r_lg[:, T, EG:].rearrange("p t (g n) -> p t g n", g=EG),
                                      bc(r_g1[:, T], 3, EPG), ALU.mult))
            link(dve, V.tensor_reduce(r_es[:, T], r_tmp2[:, T].rearrange("p t g n -> p t n g"), AX, ALU.add))
            for t in range(nt):
                ins = V.max(r_em[:, t], r_es[:, t])
            link(dve, ins)
            for t in range(nt):
                ins = V.max_index(r_ei[:, t], r_em[:, t], r_es[:, t])
            link(dve, ins)
            V.tensor_tensor(r_d[:, T], r_em[:, T, 1], r_em[:, T, 0], ALU.subtract).then_inc(rt_d1, 1)
            link(dve, V.tensor_copy(r_ef[:, T], r_ei[:, T, 0:2]))
            for k in range(2):
                ins = V.scalar_tensor_tensor(r_pos[:, k, T], r_gf[:, T], float(EPG), r_ef[:, T, k], ALU.mult, ALU.add)
            link(dve, ins)
            for k in range(2):
                ins = V.tensor_tensor(r_one[:, k, T], bc(consts[:, C_E:C_E + E], 1, nt), bc(r_pos[:, k, T], 2, E),
                                      ALU.is_equal)
            link(dve, ins)
            V.tensor_tensor(r_m[:, T], r_one[:, 0, T], r_one[:, 1, T], ALU.add).then_inc(rt_m, 1)
            dve.wait_ge(rt_e1, 2 * l + 2)
            link(dve, V.tensor_reduce(r_gs[:, T], r_ge[:, T], AX, ALU.add))
            link(dve, V.scalar_tensor_tensor(r_gs[:, T], r_d[:, T], 1.0, r_gs[:, T], ALU.add, ALU.mult))
            link(dve, V.reciprocal(r_w[:, 0, T], r_gs[:, T]))
            link(dve, V.tensor_tensor(r_w[:, 1, T], r_w[:, 0, T], r_d[:, T], ALU.mult))
            dve.wait_ge(rt_rank, l + 1)
            cnt = psum[7][:, nt * E:(nt + 1) * E]
            link(dve, V.tensor_scalar(r_ov, cnt, float(BR), None, ALU.is_gt))
            for c in range(2, nt * P // BR):
                link(dve, V.scalar_tensor_tensor(r_ov, cnt, float(c * BR), r_ov, ALU.is_gt, ALU.add))
            link(dve, V.tensor_tensor_scan(r_ovc, r_ov, r_zero, 0.0, ALU.add, ALU.add))
            link(dve, V.tensor_copy(r_r[:, T], psum[7][:, 0:nt * E].rearrange("p (t n) -> p t n", t=nt)))
            link(dve, V.tensor_tensor(r_b1, r_ovc, r_ov, ALU.subtract))
            link(dve, V.tensor_scalar(r_b1, r_b1, float(BR), float((E - 1) * BR), ALU.mult, ALU.add))
            link(dve, V.tensor_tensor(r_b1, r_b1, consts[:, C_B0:C_B0 + E], ALU.subtract))
            link(dve, V.tensor_scalar(r_q[:, T], r_r[:, T], float(BR), None, ALU.is_ge))
            link(dve, V.tensor_tensor(r_q[:, T], r_q[:, T], bc(r_b1, 1, nt), ALU.mult))
            link(dve, V.tensor_tensor(r_r[:, T], r_r[:, T], bc(consts[:, C_B0:C_B0 + E], 1, nt), ALU.add))
            link(dve, V.tensor_tensor(r_r[:, T], r_r[:, T], r_q[:, T], ALU.add))
            for k in range(2):
                link(dve, V.tensor_tensor(r_tmp[:, T], r_one[:, k, T], r_r[:, T], ALU.mult))
                link(dve, V.tensor_reduce(r_slot[:, k, T], r_tmp[:, T], AX, ALU.add))

            def split(n):
                link(dve, V.tensor_copy(r_sloti[:, :, T], r_slot[:, :, T]))
                link(dve, V.tensor_scalar(r_posi[:, :, T], r_sloti[:, :, T], n - 1, None, ALU.bitwise_and))
                link(dve, V.tensor_copy(r_pos[:, :, T], r_posi[:, :, T]))
                link(dve, V.tensor_tensor(r_blk[:, :, T], r_slot[:, :, T], r_pos[:, :, T], ALU.subtract))
                link(dve, V.tensor_scalar(r_blk[:, :, T], r_blk[:, :, T], 1.0 / n, None, ALU.mult))

            split(BR)
            link(dve, V.tensor_scalar(r_blk[:, :, T], r_blk[:, :, T], -float(E), 0.0, ALU.add, ALU.max))
            link(dve, V.scalar_tensor_tensor(r_slot[:, :, T], r_blk[:, :, T], float(BR), r_slot[:, :, T],
                                             ALU.mult, ALU.add))
            split(P)
            for i in range(2 * nt):
                k, t = divmod(i, nt)
                if i >= 2:
                    dve.wait_ge(rt_tokp, 2 * t0 + i - 1)
                V.tensor_scalar(r_Q[:, i % 2, :], consts[:, C_IOTA:C_IOTA + P], r_pos[:, k, t:t + 1], None,
                                ALU.is_equal)
                V.tensor_scalar(r_R[:, i % 2, 0:nb], consts[:, C_IOTA:C_IOTA + nb], r_blk[:, k, t:t + 1],
                                consts[:, C_TOK + t:C_TOK + t + 1], ALU.is_equal, ALU.mult).then_inc(rt_qr, 1)
            link(dve, V.tensor_tensor(r_ovm[:, 0:nov], bc(r_ovc[0:1, :], 1, nov), bc(consts[0:1, C_IOTA:C_IOTA + nov], 2, E),
                                      ALU.is_le))
            link(dve, V.tensor_reduce(r_ove[0:1, 0:nov], r_ovm[:, 0:nov], AX, ALU.add))
            link(dve, V.tensor_scalar(r_ove[0:1, 0:nov], r_ove[0:1, 0:nov], float(E - 1), None, ALU.min))
            V.tensor_copy(r_ovi[0:1, 0:nov], r_ove[0:1, 0:nov])
            V.tensor_copy(r_ovi[0:1, NOVM:NOVM + 1], r_ovc[0:1, E - 1:E])
            dve.wait_ge(rt_tokp, 2 * (t0 + nt))
            V.tensor_copy(r_tok[:, 0:nb], psum[6][:, 256:256 + nb]).then_inc(rt_slot, 1)

        YS = [(E // 2 + overflow_blocks(n * P)) * P for n in tiles]
        ys_dram = [dram(f"ys_dram{l}", [YS[l], D]) for l in range(2)]
        HF = F // 2
        KF = F // P
        xg = region(A_WORK, 2048, "p (b d) -> p b d", b=2)
        xgT = region(A_WORK + 2048, 2048, "p (b k n) -> p b k n", b=2, k=KD)
        yb = region(A_WORK + 4096, 1024, "p (b d) -> p b d", b=2)
        sil = region(A_WORK + 5120, HF)
        hid = region(A_WORK + 5376, HF)
        hT = region(A_WORK + 5632, 512, "p (b c m) -> p b c m", b=2, c=2)
        cy = [region(at, 2048, "p (b d) -> p b d", b=2) for at in (A_WORK, A_WORK + 6144)]
        moe_xg = [sem(f"moe_xg{i}") for i in range(2)]
        moe_xT = sem("moe_xT")
        moe_xa = sem("moe_xa")
        moe_xd = sem("moe_xd")
        moe_sil = sem("moe_sil")
        moe_h = sem("moe_h")
        moe_hT = sem("moe_hT")
        moe_hc = sem("moe_hc")
        moe_ya = sem("moe_ya")
        moe_ys = [sem(f"moe_ys{i}") for i in range(2)]
        ov_step = [sem(f"ov_step{l}") for l in range(2)]
        ov_xg = [sem(f"ov_xg{l}") for l in range(2)]
        ov_w = [sem(f"ov_w{l}") for l in range(2)]
        ov_st = [sem(f"ov_st{l}") for l in range(2)]
        ov_list = sem("ov_list")
        OVN = 11
        moe_out = sem("moe_out")
        cb_in = [sem(f"cb_in{i}") for i in range(2)]
        cb_s = sem("cb_s")
        cb_x = sem("cb_x")
        ys_zero = sem("ys_zero")
        PRE = 3
        BODIES = 4
        LOOP = (E - 1 - PRE) // BODIES
        assert PRE + BODIES * LOOP == E - 1

        def at_round(i, per_round, first):
            return first if i is None else i * per_round + first

        def rounds(eng, body):
            for j in range(PRE):
                body(j, None)
            with eng.Fori(0, LOOP) as i:
                for j in range(PRE, PRE + BODIES):
                    body(j, i)

        def clear_overflow_sp(sp):
            zero = bc(consts[:, C_ZERO:C_ZERO + P], 1, KD)
            sp.wait_ge(sc_mix, 4)
            for l in range(2):
                for m in range(E // 2, YS[l] // P):
                    sp.dma_start(ys_dram[l][m * P:(m + 1) * P, :].rearrange("p (k n) -> p k n", k=KD),
                                 zero).then_inc(ys_zero, 16)

        N_ZERO = 16 * sum(overflow_blocks(n * P) for n in tiles)

        def expert_source(l, which, e):
            w = a[("moe_w_gate", "moe_w_up", "moe_w_down")[which]][l, bass.ds(e, 1)]
            return (w.rearrange("e (k p) n -> (e p) k n", p=P) if which == 2 else
                    w.rearrange("e (p k) n -> (e p) k n", k=KD))

        def moe_sp(sp, l):
            n0 = U_MOE[l]
            for n in range(n0, n0 + 2 + 3 * PRE):
                load_unit(sp, n)
            at = n0 + 2 + 3 * PRE
            with sp.Fori(0, LOOP) as i:
                for u in range(3 * BODIES):
                    which, e = moe_unit(at + u - n0)
                    used_sem, v = used(at + u - 6)
                    sp.wait_ge(used_sem, i * BODIES + v)
                    sp.dma_start(unit(at + u, k=(KD, KD, KF)[which]), expert_source(l, which, i * BODIES + e)
                                 ).then_inc(ring_in[slot_of(at + u)], 16)
            load_unit(sp, n0 + 3 * E - 1)
            n_ov = ov_count(sp, l)
            with sp.If(n_ov > 0):
                for which in range(3):
                    last = max(n for n in range(n0, n0 + 3 * E) if slot_of(n) == which)
                    sp.wait_ge(*used(last))
                with sp.Fori(0, n_ov) as i:
                    e = sp.value_load(r_ovi[0:1, bass.ds(i, 1)], min_val=0, max_val=E - 1)
                    sp.wait_ge(ov_step[l], i * OVN + 1)
                    for which in range(3):
                        sp.dma_start(ov_unit(which), expert_source(l, which, e)).then_inc(ov_w[l], 16)
                sp.wait_ge(moe_out, l + 1)

        def ov_unit(which):
            return mem[:, which * SLOT:(which + 1) * SLOT].rearrange("p (k n) -> p k n", k=(KD, KD, KF)[which])

        def ov_count(eng, l):
            eng.wait_ge(rt_slot, l + 1)
            return eng.value_load(r_ovi[0:1, NOVM:NOVM + 1], min_val=0, max_val=overflow_blocks(tiles[l] * P))

        def moe_pool(pool, l):
            nt, t0 = tiles[l], base_t[l]
            pool.wait_ge(rt_slot, l + 1)
            for i in range(2):
                pool.wait_ge(n2_st[i], 16 * ((t0 + nt) // 2))

            for q in range(E // 2):
                if q >= 2:
                    pool.wait_ge(moe_xT, 2 * (E // 2 * l + q - 1))
                pool.indirect_dma_start(xg[:, q % 2, :], None, f_dram, bass.IndirectOffsetOnAxis(r_tok[:, q:q + 1], 0)
                                        ).then_inc(moe_xg[q % 2], 16)
            n_ov = ov_count(pool, l)
            with pool.If(n_ov > 0):
                with pool.Fori(0, n_ov) as i:
                    pool.wait_ge(ov_step[l], i * OVN + 3)
                    pool.sem_inc(ov_list, 1)
                    pool.indirect_dma_start(xg[:, 0, :], None, f_dram, bass.IndirectOffsetOnAxis(r_ovidx, 0)
                                            ).then_inc(ov_xg[l], 16)
                pool.wait_ge(ov_st[l], n_ov * 32)
            pool.wait_ge(moe_xT, E * (l + 1))
            for i in range(2):
                pool.wait_ge(moe_ys[i], 16 * E * (l + 1))
            pool.wait_ge(moe_out, l + 1)
            pool.wait_ge(ys_zero, N_ZERO)
            for t in range(nt):
                q = t0 + t
                if t >= 2:
                    pool.wait_ge(cb_x, q - 1)
                for k, buf in enumerate(cy):
                    pool.indirect_dma_start(buf[:, t % 2, :], None, ys_dram[l],
                                            bass.IndirectOffsetOnAxis(r_sloti[:, k, t:t + 1], 0)).then_inc(
                        cb_in[t % 2], 16)

        def moe_pe(pe, l):
            n0 = U_MOE[l]

            def ring(n, i):
                pe.wait_ge(ring_in[slot_of(n)], at_round(i, 16 * 3 * BODIES // 6, 16 * use_of[n]))

            def turn_x(p, half):
                for k in range(4):
                    tp = nc.tensor.transpose(psum[5 + half][:, k * P:(k + 1) * P], xg[:, p, 4 * half + k::KD], ident)
                return tp

            def gate_or_up(bank, x, w):
                for k in range(KD):
                    for half in range(2):
                        mm = nc.tensor.matmul(bank[half * BR:(half + 1) * BR, 0:HF], lhsT=x[:, k],
                                              rhs=w[:, k, half * HF:(half + 1) * HF], start=(k == 0),
                                              stop=(k == KD - 1), skip_group_check=True)
                return mm

            def turn_h():
                for c in range(2):
                    tp = nc.tensor.transpose(psum[7][:, c * P:(c + 1) * P], hid[:, c * P:(c + 1) * P], ident)
                return tp

            def down(bank, ht, w):
                for k in range(KF):
                    for half in range(2):
                        mm = nc.tensor.matmul(bank[half * BR:(half + 1) * BR, :],
                                              lhsT=ht[:, k % 2, k // 2 * BR:(k // 2 + 1) * BR],
                                              rhs=w[:, k, half * COLS:(half + 1) * COLS], start=(k == 0),
                                              stop=(k == KF - 1), skip_group_check=True)
                return mm

            def x_side(b, i=None):
                q, n = b // 2, n0 + (3 * b - 1 if b else 0)
                pairs = at_round(i, BODIES // 2, E // 2 * l + q)
                if b % 2 == 0:
                    pe.wait_ge(moe_xg[q % 2], at_round(i, 16 * BODIES // 4, 16 * (E // 4 * l + q // 2 + 1)))
                    for half, out in enumerate((moe_xa, moe_xd)):
                        if b:
                            pe.wait_ge(out, pairs)
                        turn_x(q % 2, half).then_inc(moe_xT, 1)
                    pe.wait_ge(moe_xa, pairs + 1)
                    pe.wait_ge(moe_xd, pairs + 1)
                if b >= 2:
                    pe.wait_ge(moe_h, at_round(i, BODIES, E * l + b - 1))
                rows = slice(b % 2 * BR, (b % 2 + 1) * BR)
                for which, done in enumerate((moe_gate, moe_up)):
                    ring(n + which, i)
                    gate_or_up(psum[2 * (b % 2) + which], xgT[:, q % 2, :, rows],
                               unit(n + which)).then_inc(done, 1)

            def h_side(j, i=None):
                n = n0 + min(4 + 3 * j, 3 * E - 1)
                pe.wait_ge(moe_h, at_round(i, BODIES, E * l + j + 1))
                if j:
                    pe.wait_ge(moe_hc, at_round(i, BODIES, E * l + j))
                turn_h().then_inc(moe_hT, 1)
                ring(n, i)
                pe.wait_ge(moe_hc, at_round(i, BODIES, E * l + j + 1))
                if j:
                    pe.wait_ge(moe_ya, at_round(i, BODIES, E * l + j))
                down(psum[4], hT[:, j % 2], unit(n, k=KF)).then_inc(moe_down, 1)

            def body(j, i):
                x_side(j + 1, i)
                h_side(j, i)

            x_side(0)
            rounds(pe, body)
            h_side(E - 1)
            n_ov = ov_count(pe, l)
            with pe.If(n_ov > 0):
                with pe.Fori(0, n_ov) as i:
                    pe.wait_ge(ov_xg[l], (i + 1) * 16)
                    for half in range(2):
                        tp = turn_x(0, half)
                    tp.then_inc(ov_step[l], 1)
                    pe.wait_ge(ov_step[l], i * OVN + 5)
                    pe.wait_ge(ov_w[l], (i + 1) * 48)
                    gate_or_up(psum[0], xgT[:, 0, :, 0:BR], ov_unit(0))
                    gate_or_up(psum[1], xgT[:, 0, :, 0:BR], ov_unit(1)).then_inc(ov_step[l], 1)
                    pe.wait_ge(ov_step[l], i * OVN + 8)
                    turn_h().then_inc(ov_step[l], 1)
                    pe.wait_ge(ov_step[l], i * OVN + 10)
                    down(psum[4], hT[:, 0], ov_unit(2)).then_inc(ov_step[l], 1)

        def moe_act(act, l):
            def turned(p, half):
                return nc.scalar.activation(xgT[:, p, 4 * half:4 * half + 4].rearrange("p k n -> p (k n)"),
                                            psum[5 + half][:, :], ACT.Copy)

            def store(dst, p, done):
                for half in range(2):
                    act.dma_start(dst[:, half * COLS:(half + 1) * COLS],
                                  yb[half * BR:(half + 1) * BR, p, :]).then_inc(done, 16)

            def rows_of(size, n):
                ys = ys_dram[l].rearrange("(b r) d -> b r d", r=size)
                return (ys[n] if isinstance(n, int) else ys[bass.ds(n, 1)].rearrange("b r d -> (b r) d"))[0:BR]

            def x_side(b, i=None):
                if b % 2 == 0:
                    act.wait_ge(moe_xT, at_round(i, BODIES, 2 * (E // 2 * l + b // 2) + 1))
                    turned(b // 2 % 2, 0).then_inc(moe_xa, 1)
                act.wait_ge(moe_gate, at_round(i, BODIES, E * l + b + 1))
                if b:
                    act.wait_ge(moe_h, at_round(i, BODIES, E * l + b))
                nc.scalar.activation(sil, psum[2 * (b % 2)][:, 0:HF], ACT.Silu).then_inc(moe_sil, 1)

            def h_side(j, i=None):
                act.wait_ge(moe_down, at_round(i, BODIES, E * l + j + 1))
                if j >= 2:
                    act.wait_ge(moe_ys[j % 2], at_round(i, 32 * BODIES // 2, 32 * (E // 2 * l + j // 2)))
                nc.scalar.activation(yb[:, j % 2, :], psum[4][:, :], ACT.Copy).then_inc(moe_ya, 1)
                act.wait_ge(moe_ya, at_round(i, BODIES, E * l + j + 1))
                store(rows_of(BR, at_round(i, BODIES, j)), j % 2, moe_ys[j % 2])

            def body(j, i):
                x_side(j + 1, i)
                h_side(j, i)

            act.nop().then_inc(ov_step[l], 1)
            x_side(0)
            rounds(act, body)
            h_side(E - 1)
            act.nop().then_inc(ov_step[l], 1)
            n_ov = ov_count(act, l)
            with act.If(n_ov > 0):
                act.wait_ge(ys_zero, N_ZERO)
                for i in range(2):
                    act.wait_ge(moe_ys[i], 16 * E * (l + 1))
                with act.Fori(0, n_ov) as i:
                    act.wait_ge(ov_step[l], i * OVN + 4)
                    turned(0, 0)
                    turned(0, 1).then_inc(ov_step[l], 1)
                    act.wait_ge(ov_step[l], i * OVN + 6)
                    nc.scalar.activation(sil, psum[0][:, 0:HF], ACT.Silu).then_inc(ov_step[l], 1)
                    act.wait_ge(ov_step[l], i * OVN + 11)
                    nc.scalar.activation(yb[:, 0, :], psum[4][:, :], ACT.Copy).then_inc(ov_step[l], 1)
                    act.wait_ge(ov_step[l], i * OVN + 12)
                    store(rows_of(P, i + E // 2), 0, ov_st[l])
                    act.wait_ge(ov_st[l], (i + 1) * 32)
                    act.nop().then_inc(ov_step[l], 1)
            act.nop().then_inc(moe_out, 1)
            for t in range(tiles[l]):
                b, q = t % 2, base_t[l] + t
                act.wait_ge(cb_in[b], 32 * (q // 2 + 1))
                nc.scalar.activation(cy[0][:, b], cy[0][:, b], ACT.Identity, scale=r_w[:, 0, t:t + 1]).then_inc(cb_s, 1)

        def moe_dve(dve, l):
            def x_side(b, i=None):
                if b % 2 == 0:
                    dve.wait_ge(moe_xT, at_round(i, BODIES, 2 * (E // 2 * l + b // 2) + 2))
                    nc.vector.tensor_copy(xgT[:, b // 2 % 2, 4:8].rearrange("p k n -> p (k n)"), psum[6][:, :]).then_inc(
                        moe_xd, 1)
                if b:
                    h_side(b - 1, i)
                dve.wait_ge(moe_sil, at_round(i, BODIES, E * l + b + 1))
                dve.wait_ge(moe_up, at_round(i, BODIES, E * l + b + 1))
                if b:
                    dve.wait_ge(moe_hT, at_round(i, BODIES, E * l + b))
                nc.vector.tensor_tensor(hid, sil, psum[2 * (b % 2) + 1][:, 0:HF], ALU.mult).then_inc(moe_h, 1)

            def h_side(j, i=None):
                dve.wait_ge(moe_hT, at_round(i, BODIES, E * l + j + 1))
                nc.vector.tensor_copy(hT[:, j % 2].rearrange("p c m -> p (c m)"), psum[7][:, 0:2 * P]).then_inc(moe_hc, 1)

            x_side(0)
            rounds(dve, lambda j, i: x_side(j + 1, i))
            h_side(E - 1)
            n_ov = ov_count(dve, l)
            with dve.If(n_ov > 0):
                with dve.Fori(0, n_ov) as i:
                    dve.wait_ge(ov_step[l], i * OVN + 2)
                    nc.vector.tensor_copy(r_ovidx, r_tok[:, bass.ds(i + E // 2, 1)]).then_inc(ov_step[l], 1)
                    dve.wait_ge(ov_step[l], i * OVN + 7)
                    nc.vector.tensor_tensor(hid, sil, psum[1][:, 0:HF], ALU.mult).then_inc(ov_step[l], 1)
                    dve.wait_ge(ov_step[l], i * OVN + 9)
                    nc.vector.tensor_copy(hT[:, 0].rearrange("p c m -> p (c m)"), psum[7][:, 0:2 * P]).then_inc(
                        ov_step[l], 1)
            nt, t0 = tiles[l], base_t[l]
            dve.wait_ge(n2_g2, (16 * 2, 16 * 3)[l])
            for t in range(nt):
                b = t % 2
                first, second = (v[:, b] for v in cy)
                dve.wait_ge(cb_s, t0 + t + 1)
                link(dve, nc.vector.scalar_tensor_tensor(first, second, r_w[:, 1, t:t + 1], first, ALU.mult, ALU.add))
                link(dve, nc.vector.tensor_tensor(first, first, gate2[:, t // 2], ALU.mult))
                nc.vector.tensor_tensor(xin[:, t], xin[:, t], first, ALU.add).then_inc(cb_x, 1)

        A1 = M0
        gate1a = region(A1, D)
        at_small = [A1 + D]

        def attn_tile(size, pattern=None, **dims):
            v = region(at_small[0], size, pattern, **dims)
            at_small[0] += size
            assert at_small[0] <= A1 + 2 * D
            return v

        rope = attn_tile(2 * NTL * 32, "p (w t n) -> p w t n", w=2, t=NTL)
        qgain = attn_tile(HD)
        kgain = attn_tile(HD)
        NQ, NK = NTL * QH, NT * KVH
        qk_ss = attn_tile(NQ + NK)
        qk_ms = attn_tile(NQ + NK)
        qk_rs = attn_tile(NQ + NK)
        qk_half = attn_tile(NQ + NK)
        amax = attn_tile(32)
        abias = attn_tile(32)
        asum = attn_tile(32)
        ainv = attn_tile(32)
        rtmp = [region(A1 + 2048 + 1024 * i, 1024) for i in range(4)]
        qrow = region(A_WORK, 2048, "p (t n) -> p t n", t=NTL)
        kv = region(A_WORK + 2048, 2048, "p (t n) -> p t n", t=NT)
        kdup = region(A_WORK + 4096, 2048, "p (t j c n) -> p t j c n", t=NT, j=KVH, c=2)
        prob = region(A_WORK + 6144, 1024, "p (b n) -> p b n", b=2)
        probT = region(A_WORK + 7168, 1024, "p (b k n) -> p b k n", b=2, k=NT)
        orow = region(A1 + 6144, 2048, "p (t n) -> p t n", t=NTL)
        oT = region(A1 + 8192, 2048, "p (k n) -> p k n", k=KD)
        qT = region(A1 + 10240, 2048, "p (r n) -> p r n", r=QH // 2)
        kT = region(A1 + 12288, 2048, "p (j n) -> p j n", j=KVH)
        SCALE = HD ** -0.5
        SB = [0, 1, 6, 7]
        at_in = sem("at_in")
        at_qe = sem("at_qe")
        at_ke = sem("at_ke")
        at_ms = sem("at_ms")
        at_rs = sem("at_rs")
        at_q = sem("at_q")
        at_k = sem("at_k")
        at_kd = sem("at_kd")
        at_tp = sem("at_tp")
        at_te = sem("at_te")
        at_s = sem("at_s")
        at_m = sem("at_m")
        at_p = sem("at_p")
        at_pt = sem("at_pt")
        at_pe = sem("at_pe")
        at_pv = sem("at_pv")
        at_o = sem("at_o")
        at_otp = sem("at_otp")
        at_oe = sem("at_oe")
        a1_x = sem("a1_x")
        AI = [(t, h) for t in range(NTL) for h in range(QH)]

        def attn_pool(pool):
            pool.wait_ge(cb_x, NT)
            pool.dma_start(gate1a, mod_dram[1, 0:1, 2 * D:3 * D].to_broadcast([P, D])).then_inc(at_in, 16)
            pool.dma_start(rope, a["rope"]).then_inc(at_in, 16)
            pool.dma_start(qgain, a["att_q_gain"][0:1, :].to_broadcast([P, HD])).then_inc(at_in, 16)
            pool.dma_start(kgain, a["att_k_gain"][0:1, :].to_broadcast([P, HD])).then_inc(at_in, 16)
            pool.wait_ge(at_ms, 1)
            nc.gpsimd.tensor_tensor(qk_rs, qk_ms, qk_half, ALU.pow).then_inc(at_rs, 1)

        def attn_pe(pe):
            pe.wait_ge(n1_ea, 8)
            pe.wait_ge(n1_ed, 8)
            for u in range(3):
                unit_wait(pe, U_QKV + u)
                w = unit(U_QKV + u)
                for t in range(NTL if u < 2 else NT):
                    for k in range(KD):
                        mm = nc.tensor.matmul(psum[2 * u + t][:, :], lhsT=aT[1][:, k, t * P:(t + 1) * P], rhs=w[:, k, :],
                                              start=(k == 0), stop=(k == KD - 1))
                    mm.then_inc(qkv_mm, 1)
            pe.wait_ge(at_qe, 4)
            pe.wait_ge(at_kd, 2)
            for i in range(8):
                if i == 4:
                    pe.wait_ge(at_q, 1)
                if i >= 2:
                    pe.wait_ge(at_te, i - 1)
                for r in range(4):
                    if i < 4:
                        src = kdup[:, r, i].rearrange("p c n -> p (c n)")
                    else:
                        pair, t = 2 * (i - 4) + r // 2, r % 2
                        src = qrow[:, t, pair * P:(pair + 1) * P]
                    tp = nc.tensor.transpose(psum[6 + i % 2][:, r * P:(r + 1) * P], src, ident)
                tp.then_inc(at_tp, 1)
            pe.wait_ge(at_te, 8)

            def scores(i):
                t, h = AI[i]
                lo = HD * (h % 2)
                if i >= 4:
                    pe.wait_ge(at_p, i - 3)
                nc.tensor.matmul(psum[SB[i % 4]][:, :], lhsT=qT[lo:lo + HD, h // 2, t * P:(t + 1) * P],
                                 rhs=kT[lo:lo + HD, h // 4, :], start=True, stop=True).then_inc(at_s, 1)

            def turn(i):
                pe.wait_ge(at_p, i + 1)
                if i >= 2:
                    pe.wait_ge(at_pe, i - 1)
                for k in range(NT):
                    tp = nc.tensor.transpose(psum[2 + i % 2][:, k * P:(k + 1) * P], prob[:, i % 2, k * P:(k + 1) * P], ident)
                tp.then_inc(at_pt, 1)

            def values(i):
                t, h = AI[i]
                pe.wait_ge(at_pe, i + 1)
                if i >= 16 and i % 8 == 0:
                    pe.wait_ge(at_o, i // 8 - 1)
                c = HD * (h % 8)
                v = (KVH + h // 4) * HD
                for k in range(NT):
                    mm = nc.tensor.matmul(psum[4 + i // 8 % 2][:, c:c + HD], lhsT=probT[:, i % 2, k, :],
                                          rhs=kv[:, k, v:v + HD], start=(k == 0), stop=(k == NT - 1))
                mm.then_inc(at_pv, 1)

            scores(0)
            scores(1)
            for i in range(len(AI) + 1):
                if i % 2 == 0 and i + 2 < len(AI):
                    scores(i + 2)
                    scores(i + 3)
                if i < len(AI):
                    turn(i)
                if i >= 1:
                    values(i - 1)
            pe.wait_ge(at_o, 4)
            for i in range(4):
                if i >= 2:
                    pe.wait_ge(at_oe, i - 1)
                for r in range(4):
                    k, t = 2 * i + r // 2, r % 2
                    tp = nc.tensor.transpose(psum[6 + i % 2][:, r * P:(r + 1) * P], orow[:, t, k::KD], ident)
                tp.then_inc(at_otp, 1)
            pe.wait_ge(at_oe, 4)
            pe.wait_ge(at_p, len(AI))
            for u in range(2):
                unit_wait(pe, U_WO + u)
                w = unit(U_WO + u)
                for t in range(NTL):
                    for k in range(KD):
                        mm = nc.tensor.matmul(psum[2 * u + t][:, :], lhsT=oT[:, k, t * P:(t + 1) * P], rhs=w[:, k, :],
                                              start=(k == 0), stop=(k == KD - 1))
                    mm.then_inc(wo_mm, 1)

        def attn_act(act):
            for i in range(4):
                act.wait_ge(qkv_mm, i + 1)
                u, t = divmod(i, 2)
                nc.scalar.activation(qrow[:, t, u * COLS:(u + 1) * COLS], psum[i][:, :], ACT.Copy).then_inc(at_qe, 1)
            act.wait_ge(at_k, 1)
            for c in range(2):
                nc.scalar.activation(kdup[:, :, :, c, :],
                                     kv[:, :, 0:KVH * HD].rearrange("p t (j n) -> p t j n", j=KVH),
                                     ACT.Copy).then_inc(at_kd, 1)
            for i in range(8):
                act.wait_ge(at_tp, i + 1)
                to = kT[:, i, :] if i < 4 else qT[:, 2 * (i - 4):2 * (i - 4) + 2, :].rearrange("p r n -> p (r n)")
                nc.scalar.activation(to, psum[6 + i % 2][:, :], ACT.Copy).then_inc(at_te, 1)
            for i in range(len(AI)):
                act.wait_ge(at_m, i + 1)
                if i >= 2:
                    act.wait_ge(at_pt, i - 1)
                nc.scalar.activation(prob[:, i % 2, :], psum[SB[i % 4]][:, :], ACT.Exp, bias=abias[:, i:i + 1], scale=SCALE,
                                     accum_out=asum[:, i:i + 1]).then_inc(at_p, 1)
            for i in range(4):
                act.wait_ge(at_otp, i + 1)
                nc.scalar.activation(oT[:, 2 * i:2 * i + 2, :].rearrange("p k n -> p (k n)"), psum[6 + i % 2][:, :],
                                     ACT.Copy).then_inc(at_oe, 1)

        def attn_dve(dve):
            V = nc.vector
            for t in range(NT):
                dve.wait_ge(qkv_mm, 5 + t)
                V.tensor_copy(kv[:, t, :], psum[4 + t][:, :]).then_inc(at_ke, 1)
            dve.wait_ge(at_ke, NT)
            V.memset(qk_half, -0.5)
            k4 = kv[:, :, 0:KVH * HD].rearrange("p t (j n) -> p t j n", j=KVH)
            q3 = qrow.rearrange("p t (h n) -> p (t h) n", n=HD)
            ksq = rtmp[2].rearrange("p (t j n) -> p t j n", t=NT, j=KVH)
            qsq = region(A1 + 2048, 2048, "p (h n) -> p h n", n=HD)
            link(dve, V.tensor_tensor(ksq, k4, k4, ALU.mult))
            V.tensor_reduce(qk_ss[:, NQ:], ksq.rearrange("p t j n -> p (t j) n"), AX, ALU.add)
            dve.wait_ge(at_qe, 4)
            link(dve, V.tensor_tensor(qsq, q3, q3, ALU.mult))
            link(dve, V.tensor_reduce(qk_ss[:, 0:NQ], qsq, AX, ALU.add))
            V.tensor_scalar(qk_ms, qk_ss, 1.0 / HD, EPS, ALU.mult, ALU.add).then_inc(at_ms, 1)
            dve.wait_ge(at_in, 64)
            dve.wait_ge(at_rs, 1)
            cos, sin = rope[:, 0], rope[:, 1]

            def turn_pairs(x, heads, tmp):
                n = NTL * heads * HD // 2
                T = [v[:, 0:n].rearrange("p (t h n) -> p t h n", t=NTL, h=heads) for v in tmp]
                c, s = bc(cos, 2, heads), bc(sin, 2, heads)
                V.tensor_tensor(T[0], x[:, :, :, 0::2], c, ALU.mult)
                V.tensor_tensor(T[1], x[:, :, :, 1::2], s, ALU.mult)
                V.tensor_tensor(T[2], x[:, :, :, 0::2], s, ALU.mult)
                link(dve, V.tensor_tensor(T[3], x[:, :, :, 1::2], c, ALU.mult))
                V.tensor_tensor(x[:, :, :, 0::2], T[0], T[1], ALU.subtract)
                return V.tensor_tensor(x[:, :, :, 1::2], T[2], T[3], ALU.add)

            for t in range(NT):
                ins = V.tensor_tensor(k4[:, t], k4[:, t], bc(qk_rs[:, NQ + KVH * t:NQ + KVH * (t + 1)], 2, HD), ALU.mult)
            link(dve, ins)
            for t in range(NT):
                ins = V.tensor_tensor(k4[:, t], k4[:, t], bc(kgain, 1, KVH), ALU.mult)
            link(dve, ins)
            turn_pairs(k4[:, 0:NTL], KVH, rtmp).then_inc(at_k, 1)
            dve.wait_ge(at_k, 1)
            link(dve, V.tensor_tensor(q3, q3, bc(qk_rs[:, 0:NQ], 2, HD), ALU.mult))
            link(dve, V.tensor_tensor(q3, q3, bc(qgain, 1, NQ), ALU.mult))
            turn_pairs(qrow.rearrange("p t (h n) -> p t h n", n=HD), QH, rtmp).then_inc(at_q, 1)

            def evac(i):
                dve.wait_ge(at_pt, i + 1)
                if i >= 2:
                    dve.wait_ge(at_pv, i - 1)
                V.tensor_copy(probT[:, i % 2].rearrange("p k n -> p (k n)"), psum[2 + i % 2][:, :]).then_inc(at_pe, 1)

            def output(q):
                dve.wait_ge(at_pv, 8 * q + 8)
                dve.wait_ge(at_p, 8 * q + 8)
                link(dve, V.reciprocal(ainv[:, 8 * q:8 * q + 8], asum[:, 8 * q:8 * q + 8]))
                t, hh = divmod(q, 2)
                V.tensor_tensor(orow[:, t, hh * COLS:(hh + 1) * COLS].rearrange("p (h n) -> p h n", h=8),
                                psum[4 + q % 2][:, :].rearrange("p (h n) -> p h n", h=8),
                                bc(ainv[:, 8 * q:8 * q + 8], 2, HD), ALU.mult).then_inc(at_o, 1)

            for i in range(len(AI) + 1):
                if i < len(AI):
                    dve.wait_ge(at_s, i + 1)
                    link(dve, V.tensor_reduce(amax[:, i:i + 1], psum[SB[i % 4]][:, :], AX, ALU.max))
                    V.tensor_scalar(abias[:, i:i + 1], amax[:, i:i + 1], -SCALE, None, ALU.mult).then_inc(at_m, 1)
                if i >= 1:
                    evac(i - 1)
                if i >= 10 and i % 8 == 2:
                    output(i // 8 - 1)
            output(3)
            for i in range(2 * NTL):
                u, t = divmod(i, NTL)
                cs = slice(u * COLS, (u + 1) * COLS)
                dve.wait_ge(wo_mm, i + 1)
                tmp = region(A_WORK + i % 2 * COLS, COLS)
                link(dve, V.tensor_tensor(tmp, psum[2 * u + t][:, :], gate1a[:, cs], ALU.mult))
                V.tensor_tensor(xin[:, t, cs], xin[:, t, cs], tmp, ALU.add).then_inc(a1_x, 1)

        out_st = sem("out_st")
        block = ctx.enter_context(nc.Block())

        @block.vector
        def _(dve):
            nc.vector.memset(mhalf[:, :], -0.5).then_inc(s_init, 1)
            norm1_scale_dve(dve, 0)
            mod_clear_dve((0, 1))
            mod_dve(dve, range(MOD_FIRST))
            norm1_dve(dve, 0)
            dt_dve(dve)
            conv_dve(dve)
            mod_wait(dve, 1, MODU)
            scan_dve(dve)
            finish_dve(dve)
            norm2_dve(dve, 0)
            moe_dve(dve, 0)
            norm1_scale_dve(dve, 1)
            norm1_dve(dve, 1)
            attn_dve(dve)
            norm2_dve(dve, 1)
            moe_dve(dve, 1)

        @block.sync
        def _(sp):
            sp.dma_start(consts[:, :], a["consts"]).then_inc(s_const, 16)
            sp.dma_start(craw[:, 0, :], a["c"][0].rearrange("(p k) -> p k", k=KD)).then_inc(s_c, 16)
            sp.dma_start(craw[:, 1, :], a["c_ctx"].rearrange("(p k) -> p k", k=KD)).then_inc(s_c, 16)
            for n in range(U_MOE[0]):
                load_unit(sp, n)
                if n == U_Z + 2:
                    clear_overflow_sp(sp)
            moe_sp(sp, 0)
            for i in range(2):
                sp.wait_ge(cb_in[i], 16 * NT)
            for n in range(U_QKV, U_MOE[1]):
                load_unit(sp, n)
            moe_sp(sp, 1)
            for t in range(NTL):
                sp.wait_ge(cb_x, NT + t + 1)
                sp.dma_start(out[0, t * P:(t + 1) * P, :], xin[:, t, :]).then_inc(out_st, 16)
            sp.wait_ge(out_st, 16 * NTL)

        @block.gpsimd
        def _(pool):
            pool.dma_start(xin[:, 0:2, :], a["x"][0].rearrange("(t p) d -> p t d", p=P)).then_inc(x_in, 16)
            pool.dma_start(xin[:, 2:4, :], a["ctx"][0].rearrange("(t p) d -> p t d", p=P)).then_inc(x_in, 16)
            pool.dma_start(wdt, a["ssd_w_in"][0, :, DI + XBC:].rearrange("(p k) n -> p k n", k=KD)).then_inc(sw_in, 16)
            pool.dma_start(convw, a["conv_w"]).then_inc(sw_in, 16)
            pool.dma_start(convb, a["conv_b"]).then_inc(sw_in, 16)
            for v, name in ((dtb, "ssd_dt_bias"), (alog, "ssd_a_log")):
                pool.dma_start(v, a[name].rearrange("a d h -> a (d h)").to_broadcast([P, 64])).then_inc(sw_in, 16)
            norm1_rstd_pool(pool, 0)
            norm1_pool(pool, 0)
            scan_pool(pool)
            finish_pool(pool)
            norm2_pool(pool, 0)
            moe_pool(pool, 0)
            norm1_pool(pool, 1)
            norm1_rstd_pool(pool, 1)
            attn_pool(pool)
            norm2_pool(pool, 1)
            moe_pool(pool, 1)

        @block.scalar
        def _(act):
            act.wait_ge(s_c, 32)
            for r in range(2):
                nc.scalar.activation(silu_c[:, :, r], craw[:, r, :], ACT.Silu).then_inc(s_silu_c, 1)
            norm1_square_act(act, 0)
            mod_act(act, range(MOD_FIRST))
            norm1_act(act, 0)
            dt_act(act)
            conv_act(act)
            scan_act(act)
            finish_act(act)
            norm2_act(act, 0)
            moe_act(act, 0)
            norm1_square_act(act, 1)
            norm1_act(act, 1)
            attn_act(act)
            norm2_act(act, 1)
            moe_act(act, 1)

        @block.tensor
        def _(pe):
            pe.wait_ge(s_const, 16)
            pe.wait_ge(s_silu_c, 2)
            mod_pe(pe, range(MOD_FIRST))
            norm1_pe(pe, 0)
            conv_pe(pe)
            scan_pe(pe)
            finish_pe(pe)
            norm2_pe(pe, 0)
            moe_pe(pe, 0)
            norm1_pe(pe, 1)
            attn_pe(pe)
            norm2_pe(pe, 1)
            moe_pe(pe, 1)


def kernel(**inputs):
    import concourse.bacc as _bacc
    from concourse.bass_utils import run_bass_kernel_spmd as _run

    host = dict(inputs)
    conv_w, conv_b, norm_g = (host.pop(n) for n in ("ssd_conv_w", "ssd_conv_b", "ssd_norm_g"))
    host["conv_w"] = conv_w[0].T.reshape(NCH, P, TAPS).transpose(1, 0, 2)
    host["conv_b"] = conv_b[0].reshape(NCH, P).T
    host["norm_cols"] = norm_g[0].reshape(DI // P, P).T
    host["consts"] = consts_array()
    host["rope"] = rope_array()
    nc = _bacc.Bacc("TRN2", target_bir_lowering=False, num_devices=1)
    arrays, a = {}, {}
    for name, v in host.items():
        v = np.ascontiguousarray(v)
        arrays[f"in_{name}_dram"] = v
        a[name] = nc.dram_tensor(f"in_{name}_dram", v.shape, mybir.dt.from_np(v.dtype), kind="ExternalInput").ap()
    out = nc.dram_tensor("out_0_dram", (1, SEQ, D), F32, kind="ExternalOutput").ap()
    hybrid_block(nc, a, out)
    r = _run(nc, [arrays], core_ids=[0])
    return r.results[0]["out_0_dram"]
```
